# Optimizing a Trainium2 kernel written in Bass

```python
import math
import jax
import jax.numpy as jnp
from jax import lax
import numpy as np

D_MODEL = 1024
BATCH = 1
SEQ = 1024
DEPTH = 1
DEC_BATCH = 8
DEC_SEQ = 8
PAST_LEN = 8192
PAGE_SIZE = 128

EPS = 1e-6
CONV_W = 4

LRU_WIDTH = D_MODEL
LRU_BLOCKS = 16
LRU_BLOCK = LRU_WIDTH // LRU_BLOCKS
LRU_C = 8.0

GLA_HEADS = 4
GLA_DK = D_MODEL // (2 * GLA_HEADS)
GLA_DV = D_MODEL // GLA_HEADS
GLA_RANK = 16
GLA_TAU = 16.0
GLA_CHUNK = 64

SSD_HEADS = 16
SSD_HEADDIM = D_MODEL // SSD_HEADS
SSD_WIDTH = SSD_HEADS * SSD_HEADDIM
SSD_GROUPS = 2
SSD_STATE = 64
SSD_CHUNK = 64
SSD_CONV_CH = SSD_WIDTH + 2 * SSD_GROUPS * SSD_STATE

MEM_TOKENS = 256
XA_HEADS = 4
XA_HD = D_MODEL // XA_HEADS

D_FF = 256 * (-(-(8 * D_MODEL) // (3 * 256)))

N_BRANCH = 3
IN_SIZES = (LRU_WIDTH, LRU_WIDTH,
            GLA_HEADS * GLA_DK, GLA_HEADS * GLA_DK, GLA_HEADS * GLA_DV, GLA_HEADS * GLA_DV, GLA_RANK,
            SSD_WIDTH, SSD_CONV_CH, SSD_HEADS,
            N_BRANCH * D_MODEL)
N_IN = sum(IN_SIZES)

kernel_name = 'hybrid_lru_gla_ssd_decoder_step'

def _split_points(sizes):
    pts, acc = [], 0
    for s in sizes[:-1]:
        acc += s
        pts.append(acc)
    return pts

def rmsnorm(x, g):
    xf = x.astype(jnp.float32)
    xf = xf * lax.rsqrt(jnp.mean(xf * xf, axis=-1, keepdims=True) + EPS)
    return (xf * g.astype(jnp.float32)).astype(x.dtype)

def grouped_rmsnorm(y, g, groups):
    b_, l_, w_ = y.shape
    yf = y.astype(jnp.float32).reshape(b_, l_, groups, w_ // groups)
    yf = yf * lax.rsqrt(jnp.mean(yf * yf, axis=-1, keepdims=True) + EPS)
    return (yf.reshape(b_, l_, w_) * g.astype(jnp.float32)).astype(y.dtype)

def causal_conv(x, buf, w, b):
    l_ = x.shape[1]
    xp = jnp.concatenate([buf.astype(x.dtype), x], axis=1)
    y = b
    for k in range(CONV_W):
        y = y + w[k] * xp[:, k:k + l_]
    return y, xp[:, xp.shape[1] - (CONV_W - 1):]

def _to_chunks(t, c):
    b_, l_ = t.shape[:2]
    return jnp.moveaxis(t.reshape((b_, l_ // c, c) + t.shape[2:]), 1, 0)

def _from_chunks(t):
    nc, b_, c = t.shape[:3]
    return jnp.moveaxis(t, 0, 1).reshape((b_, nc * c) + t.shape[3:])

def _lru_combine(left, right):
    a1, b1 = left
    a2, b2 = right
    return a1 * a2, a2 * b1 + b2

def rg_lru_branch(x_in, gate_in, h0, conv_buf, conv_w, conv_b, wa, ba, wx, bx, lam):
    b_, l_, _ = x_in.shape
    xc, new_buf = causal_conv(x_in, conv_buf, conv_w, conv_b)
    xb = xc.reshape(b_, l_, LRU_BLOCKS, LRU_BLOCK)
    r = jax.nn.sigmoid(jnp.einsum('blki,kij->blkj', xb, wa).reshape(b_, l_, LRU_WIDTH) + ba)
    i = jax.nn.sigmoid(jnp.einsum('blki,kij->blkj', xb, wx).reshape(b_, l_, LRU_WIDTH) + bx)
    log_a = -LRU_C * r.astype(jnp.float32) * jax.nn.softplus(-lam.astype(jnp.float32))
    a = jnp.exp(log_a)
    u = jnp.sqrt(-jnp.expm1(2.0 * log_a)) * (i * xc).astype(jnp.float32)
    a_cum, h_from_zero = lax.associative_scan(_lru_combine, (a, u), axis=1)
    h = a_cum * h0.astype(jnp.float32)[:, None] + h_from_zero
    y = h.astype(x_in.dtype) * jax.nn.gelu(gate_in)
    return y, h[:, -1], new_buf

def gla_chunked(q, k, v, g, s0):
    l_ = q.shape[1]
    c = math.gcd(l_, GLA_CHUNK)
    mask = jnp.tril(jnp.ones((c, c), dtype=bool))
    f32 = jnp.float32
    xs = tuple(_to_chunks(t.astype(f32), c) for t in (q * GLA_DK ** -0.5, k, v, g))

    def step(s, inp):
        qi, ki, vi, gi = inp
        b = jnp.cumsum(gi, axis=1)
        b_last = b[:, -1]
        qt = qi * jnp.exp(b)
        kt = ki * jnp.exp(-b)
        ke = ki * jnp.exp(b_last[:, None] - b)
        att = jnp.where(mask, jnp.einsum('bihd,bjhd->bhij', qt, kt), 0.0)
        o = jnp.einsum('bhij,bjhv->bihv', att, vi) + jnp.einsum('bihd,bhdv->bihv', qt, s)
        s = jnp.exp(b_last)[..., None] * s + jnp.einsum('bjhd,bjhv->bhdv', ke, vi)
        return s, o

    s, o = lax.scan(step, s0.astype(f32), xs)
    return _from_chunks(o), s

def ssd_chunked(x, dt, a, bm, cm, h0):
    b_, l_ = x.shape[:2]
    hpg = SSD_HEADS // SSD_GROUPS
    c = math.gcd(l_, SSD_CHUNK)
    f32 = jnp.float32
    mask = jnp.tril(jnp.ones((c, c), dtype=bool))[None, :, :, None, None]
    xg = x.astype(f32).reshape(b_, l_, SSD_GROUPS, hpg, SSD_HEADDIM)
    dtg = dt.astype(f32).reshape(b_, l_, SSD_GROUPS, hpg)
    dag = dtg * a.astype(f32).reshape(SSD_GROUPS, hpg)
    xs = tuple(_to_chunks(t, c) for t in (xg, dtg, dag, bm.astype(f32), cm.astype(f32)))
    hg0 = h0.astype(f32).reshape(b_, SSD_GROUPS, hpg, SSD_HEADDIM, SSD_STATE)

    def step(h, inp):
        xi, dti, dai, bi, ci = inp
        cum = jnp.cumsum(dai, axis=1)
        seg = cum[:, :, None] - cum[:, None, :]
        decay = jnp.exp(jnp.where(mask, seg, -jnp.inf))
        cb = jnp.einsum('bign,bjgn->bijg', ci, bi)
        m = cb[..., None] * decay * dti[:, None]
        y = jnp.einsum('bijgh,bjghp->bighp', m, xi)
        y = y + jnp.einsum('bign,bghpn->bighp', ci, h) * jnp.exp(cum)[..., None]
        last = cum[:, -1]
        w = jnp.exp(last[:, None] - cum) * dti
        h = jnp.exp(last)[..., None, None] * h + jnp.einsum('bjgh,bjghp,bjgn->bghpn', w, xi, bi)
        return h, y

    h, y = lax.scan(step, hg0, xs)
    y = _from_chunks(y).reshape(b_, l_, SSD_HEADS, SSD_HEADDIM)
    return y, h.reshape(b_, SSD_HEADS, SSD_HEADDIM, SSD_STATE)

def memory_kv(mem, g, wk, wv):
    b_, m_, _ = mem.shape
    mn = rmsnorm(mem, g)
    return ((mn @ wk).reshape(b_, m_, XA_HEADS, XA_HD), (mn @ wv).reshape(b_, m_, XA_HEADS, XA_HD))

def cross_attention(h, k, v, wq, wo):
    b_, l_, _ = h.shape
    q = (h @ wq).reshape(b_, l_, XA_HEADS, XA_HD)
    s = jnp.einsum('blhd,bmhd->bhlm', q, k.astype(q.dtype)).astype(jnp.float32) * XA_HD ** -0.5
    p = jax.nn.softmax(s, axis=-1).astype(h.dtype)
    o = jnp.einsum('bhlm,bmhd->blhd', p, v.astype(h.dtype)).reshape(b_, l_, D_MODEL)
    return o @ wo

def hybrid_layer(x, mem_k, mem_v, lru_h, lru_conv, gla_s, ssd_h, ssd_conv, W):
    b_, l_, _ = x.shape
    h = rmsnorm(x, W['norm_mix'])
    u = h @ W['w_in']
    (lru_x, lru_gate, gq, gk, gv, gr, g_low, sz, sxbc, sdt, gate_logits) = jnp.split(
        u, _split_points(IN_SIZES), axis=-1)

    y_lru, lru_h_new, lru_conv_new = rg_lru_branch(
        lru_x, lru_gate, lru_h, lru_conv, W['lru_conv_w'], W['lru_conv_b'],
        W['lru_wa'], W['lru_ba'], W['lru_wx'], W['lru_bx'], W['lru_lambda'])
    b_lru = y_lru @ W['w_lru_out']

    g_log = jax.nn.log_sigmoid((g_low @ W['gla_w_alpha'] + W['gla_b_alpha']).astype(jnp.float32)) / GLA_TAU
    o, gla_s_new = gla_chunked(
        gq.reshape(b_, l_, GLA_HEADS, GLA_DK), gk.reshape(b_, l_, GLA_HEADS, GLA_DK),
        gv.reshape(b_, l_, GLA_HEADS, GLA_DV), g_log.reshape(b_, l_, GLA_HEADS, GLA_DK), gla_s)
    o = rmsnorm(o, W['gla_norm']).reshape(b_, l_, GLA_HEADS * GLA_DV).astype(x.dtype)
    b_gla = (o * jax.nn.silu(gr)) @ W['w_gla_out']

    xbc, ssd_conv_new = causal_conv(sxbc, ssd_conv, W['ssd_conv_w'], W['ssd_conv_b'])
    xbc = jax.nn.silu(xbc)
    sx, sb, sc = jnp.split(xbc, [SSD_WIDTH, SSD_WIDTH + SSD_GROUPS * SSD_STATE], axis=-1)
    sx = sx.reshape(b_, l_, SSD_HEADS, SSD_HEADDIM)
    dt = jax.nn.softplus((sdt + W['ssd_dt_bias']).astype(jnp.float32))
    a = -jnp.exp(W['ssd_a_log'].astype(jnp.float32))
    y, ssd_h_new = ssd_chunked(sx, dt, a, sb.reshape(b_, l_, SSD_GROUPS, SSD_STATE),
                               sc.reshape(b_, l_, SSD_GROUPS, SSD_STATE), ssd_h)
    y = (y + W['ssd_d'].astype(jnp.float32)[:, None] * sx.astype(jnp.float32)).astype(x.dtype)
    y = grouped_rmsnorm(y.reshape(b_, l_, SSD_WIDTH) * jax.nn.silu(sz), W['ssd_norm'], SSD_GROUPS)
    b_ssd = y @ W['w_ssd_out']

    gates = jax.nn.sigmoid(gate_logits).reshape(b_, l_, N_BRANCH, D_MODEL)
    merged = gates[:, :, 0] * b_lru + gates[:, :, 1] * b_gla + gates[:, :, 2] * b_ssd
    x = x + merged @ W['w_mix_out']

    x = x + cross_attention(rmsnorm(x, W['norm_xattn']), mem_k, mem_v, W['w_xq'], W['w_xo'])

    h = rmsnorm(x, W['norm_ffn'])
    x = x + (jax.nn.silu(h @ W['w_ffn_gate']) * (h @ W['w_ffn_up'])) @ W['w_ffn_down']
    return x, (lru_h_new, lru_conv_new, gla_s_new, ssd_h_new, ssd_conv_new)

def setup_inputs(seed: int = 0) -> dict:
    key = jax.random.key(seed)
    keys = jax.random.split(key, 64)
    counter = [0]
    f32 = jnp.float32

    def nk():
        k = keys[counter[0]]
        counter[0] += 1
        return k

    def nrm(shape, scale=1.0):
        return scale * jax.random.normal(nk(), shape, f32)

    def gain(shape):
        return 1.0 + nrm(shape, 0.01)

    lam_u = jax.random.uniform(nk(), (DEPTH, LRU_WIDTH), f32, minval=0.9, maxval=0.999)
    dt0 = jnp.exp(jax.random.uniform(nk(), (DEPTH, SSD_HEADS), f32,
                                     minval=math.log(1e-3), maxval=math.log(1e-1)))
    a0 = jax.random.uniform(nk(), (DEPTH, SSD_HEADS), f32, minval=1.0, maxval=16.0)
    return {
        'x_prompt': nrm((BATCH, SEQ, D_MODEL)),
        'x_sample': nrm((DEC_BATCH, DEC_SEQ, D_MODEL)),
        'mem_prompt': nrm((BATCH, MEM_TOKENS, D_MODEL)),
        'state_lru_h': nrm((DEPTH, DEC_BATCH, LRU_WIDTH), 0.5),
        'state_lru_conv': nrm((DEPTH, DEC_BATCH, CONV_W - 1, LRU_WIDTH)),
        'state_gla_S': nrm((DEPTH, DEC_BATCH, GLA_HEADS, GLA_DK, GLA_DV), 0.3),
        'state_ssd_h': nrm((DEPTH, DEC_BATCH, SSD_HEADS, SSD_HEADDIM, SSD_STATE), 0.1),
        'state_ssd_conv': nrm((DEPTH, DEC_BATCH, CONV_W - 1, SSD_CONV_CH)),
        'cache_mem_k': nrm((DEPTH, DEC_BATCH, MEM_TOKENS, XA_HEADS, XA_HD)),
        'cache_mem_v': nrm((DEPTH, DEC_BATCH, MEM_TOKENS, XA_HEADS, XA_HD)),
        'norm_mix': gain((DEPTH, D_MODEL)),
        'w_in': nrm((DEPTH, D_MODEL, N_IN), D_MODEL ** -0.5),
        'lru_conv_w': nrm((DEPTH, CONV_W, LRU_WIDTH), CONV_W ** -0.5),
        'lru_conv_b': nrm((DEPTH, LRU_WIDTH), 0.01),
        'lru_wa': nrm((DEPTH, LRU_BLOCKS, LRU_BLOCK, LRU_BLOCK), LRU_BLOCK ** -0.5),
        'lru_ba': nrm((DEPTH, LRU_WIDTH), 0.01),
        'lru_wx': nrm((DEPTH, LRU_BLOCKS, LRU_BLOCK, LRU_BLOCK), LRU_BLOCK ** -0.5),
        'lru_bx': nrm((DEPTH, LRU_WIDTH), 0.01),
        'lru_lambda': jnp.log(lam_u) - jnp.log1p(-lam_u),
        'w_lru_out': nrm((DEPTH, LRU_WIDTH, D_MODEL), LRU_WIDTH ** -0.5),
        'gla_w_alpha': nrm((DEPTH, GLA_RANK, GLA_HEADS * GLA_DK), GLA_RANK ** -0.5),
        'gla_b_alpha': nrm((DEPTH, GLA_HEADS * GLA_DK), 0.1),
        'gla_norm': gain((DEPTH, GLA_DV)),
        'w_gla_out': nrm((DEPTH, GLA_HEADS * GLA_DV, D_MODEL), (GLA_HEADS * GLA_DV) ** -0.5),
        'ssd_conv_w': nrm((DEPTH, CONV_W, SSD_CONV_CH), CONV_W ** -0.5),
        'ssd_conv_b': nrm((DEPTH, SSD_CONV_CH), 0.01),
        'ssd_dt_bias': dt0 + jnp.log(-jnp.expm1(-dt0)),
        'ssd_a_log': jnp.log(a0),
        'ssd_d': 1.0 + nrm((DEPTH, SSD_HEADS), 0.1),
        'ssd_norm': gain((DEPTH, SSD_WIDTH)),
        'w_ssd_out': nrm((DEPTH, SSD_WIDTH, D_MODEL), SSD_WIDTH ** -0.5),
        'w_mix_out': nrm((DEPTH, D_MODEL, D_MODEL), D_MODEL ** -0.5),
        'norm_xattn': gain((DEPTH, D_MODEL)),
        'norm_mem': gain((DEPTH, D_MODEL)),
        'w_xq': nrm((DEPTH, D_MODEL, D_MODEL), D_MODEL ** -0.5),
        'w_xk': nrm((DEPTH, D_MODEL, D_MODEL), D_MODEL ** -0.5),
        'w_xv': nrm((DEPTH, D_MODEL, D_MODEL), D_MODEL ** -0.5),
        'w_xo': nrm((DEPTH, D_MODEL, D_MODEL), D_MODEL ** -0.5),
        'norm_ffn': gain((DEPTH, D_MODEL)),
        'w_ffn_gate': nrm((DEPTH, D_MODEL, D_FF), D_MODEL ** -0.5),
        'w_ffn_up': nrm((DEPTH, D_MODEL, D_FF), D_MODEL ** -0.5),
        'w_ffn_down': nrm((DEPTH, D_FF, D_MODEL), D_FF ** -0.5),
        'norm_final': gain((D_MODEL,)),
    }

def reference(x_prompt, x_sample, mem_prompt, state_lru_h, state_lru_conv, state_gla_S, state_ssd_h,
              state_ssd_conv, cache_mem_k, cache_mem_v, norm_mix, w_in, lru_conv_w, lru_conv_b, lru_wa,
              lru_ba, lru_wx, lru_bx, lru_lambda, w_lru_out, gla_w_alpha, gla_b_alpha, gla_norm, w_gla_out,
              ssd_conv_w, ssd_conv_b, ssd_dt_bias, ssd_a_log, ssd_d, ssd_norm, w_ssd_out, w_mix_out,
              norm_xattn, norm_mem, w_xq, w_xk, w_xv, w_xo, norm_ffn, w_ffn_gate, w_ffn_up, w_ffn_down,
              norm_final):
    stacked = {
        'norm_mix': norm_mix, 'w_in': w_in,
        'lru_conv_w': lru_conv_w, 'lru_conv_b': lru_conv_b, 'lru_wa': lru_wa, 'lru_ba': lru_ba,
        'lru_wx': lru_wx, 'lru_bx': lru_bx, 'lru_lambda': lru_lambda, 'w_lru_out': w_lru_out,
        'gla_w_alpha': gla_w_alpha, 'gla_b_alpha': gla_b_alpha, 'gla_norm': gla_norm, 'w_gla_out': w_gla_out,
        'ssd_conv_w': ssd_conv_w, 'ssd_conv_b': ssd_conv_b, 'ssd_dt_bias': ssd_dt_bias,
        'ssd_a_log': ssd_a_log, 'ssd_d': ssd_d, 'ssd_norm': ssd_norm, 'w_ssd_out': w_ssd_out,
        'w_mix_out': w_mix_out, 'norm_xattn': norm_xattn, 'norm_mem': norm_mem,
        'w_xq': w_xq, 'w_xk': w_xk, 'w_xv': w_xv, 'w_xo': w_xo,
        'norm_ffn': norm_ffn, 'w_ffn_gate': w_ffn_gate, 'w_ffn_up': w_ffn_up, 'w_ffn_down': w_ffn_down,
    }
    f32 = jnp.float32
    bp = x_prompt.shape[0]
    xp, xs = x_prompt, x_sample
    p_out = [[] for _ in range(7)]
    s_out = [[] for _ in range(5)]
    for l in range(DEPTH):
        W = {name: arr[l] for name, arr in stacked.items()}
        mk, mv = memory_kv(mem_prompt, W['norm_mem'], W['w_xk'], W['w_xv'])
        xp, p_st = hybrid_layer(
            xp, mk, mv,
            jnp.zeros((bp, LRU_WIDTH), f32),
            jnp.zeros((bp, CONV_W - 1, LRU_WIDTH), xp.dtype),
            jnp.zeros((bp, GLA_HEADS, GLA_DK, GLA_DV), f32),
            jnp.zeros((bp, SSD_HEADS, SSD_HEADDIM, SSD_STATE), f32),
            jnp.zeros((bp, CONV_W - 1, SSD_CONV_CH), xp.dtype),
            W)
        xs, s_st = hybrid_layer(
            xs, cache_mem_k[l], cache_mem_v[l], state_lru_h[l], state_lru_conv[l],
            state_gla_S[l], state_ssd_h[l], state_ssd_conv[l], W)
        for lst, val in zip(p_out, p_st + (mk, mv)):
            lst.append(val)
        for lst, val in zip(s_out, s_st):
            lst.append(val)
    y_prompt = rmsnorm(xp, norm_final)
    y_sample = rmsnorm(xs, norm_final)
    p_lru_h, p_lru_conv, p_gla_S, p_ssd_h, p_ssd_conv, p_mem_k, p_mem_v = [jnp.stack(t, axis=0) for t in p_out]
    s_lru_h, s_lru_conv, s_gla_S, s_ssd_h, s_ssd_conv = [jnp.stack(t, axis=0) for t in s_out]
    return (y_prompt, y_sample, p_lru_h, p_lru_conv, p_gla_S, p_ssd_h, p_ssd_conv, p_mem_k, p_mem_v,
            s_lru_h, s_lru_conv, s_gla_S, s_ssd_h, s_ssd_conv)


_drawn_inputs = setup_inputs


def setup_inputs(seed=0):
    import zlib

    import numpy as np

    out = dict(_drawn_inputs(seed))
    spreads = {}
    factors = {'norm_mix': 2.782,
     'lru_ba': 27.44,
     'lru_bx': 24.707,
     'gla_norm': 8.0,
     'ssd_conv_b': 4.075,
     'ssd_norm': 24.101,
     'norm_xattn': 8.0,
     'norm_mem': 5.681,
     'norm_ffn': 33.138,
     'norm_final': 30.462,
     'lru_conv_b': 4.526,
     'ssd_d': 4.23}
    for name, (base, spread) in spreads.items():
        noise = np.random.default_rng([zlib.crc32(name.encode()), seed]).standard_normal(out[name].shape)
        drawn = base * np.exp(spread * noise) if base else spread * noise
        out[name] = jnp.asarray(drawn.astype(out[name].dtype))
    for name, factor in factors.items():
        out[name] = (out[name] * factor).astype(out[name].dtype)
    return out
```

```python
from contextlib import ExitStack

import concourse.bass as bass
from concourse import mybir

F32 = mybir.dt.float32
F32R = mybir.dt.float32r
ALU = mybir.AluOpType
ACT = mybir.ActivationFunctionType
AX_X = mybir.AxisListType.X

P = 128
D = 1024
DT = D // P
LP = 1024
NB = 8
LS = 8
TS = NB * LS
T = LP + TS
TT = LP // P
GROUPS = [(0, 384), (384, 384), (768, 320)]
EPS = 1e-6
CW = 4
HIST = CW - 1
GH, DK, DV, GCH = 4, 128, 256, 64
SH, HD, NS = 16, 64, 64
SCC = D + 4 * NS
CT = SCC // P
M = 256
XH, XD = 4, 256
FF = 2816
FT = FF // P
FC = FT // 2
WT = 1152
GELU_C = 0.7978845608028654

C_LX, C_LG, C_Q, C_K, C_V, C_R, C_LOW = 0, 1024, 2048, 2560, 3072, 4096, 5120
C_Z, C_XBC, C_DT, C_GATE = 5136, 6160, 7440, 7456

R_CONV, R_H0, R_CW, R_CB, R_BA, R_BX, R_LAM = 0, 24, 32, 36, 37, 38, 39
R_NMIX, R_NX, R_NFFN, R_NFIN, R_NMEM, R_NSSD, R_GLA, NROW = 40, 41, 42, 43, 44, 45, 46, 47
Q_CONV, Q_CW, Q_CB, QROW = 0, 24, 28, 29


def plan():
    w, jobs = [], ["pk0", "pk1"] + [f"xt{c}" for c in range(TT + 1)]

    def use(tiles, *names):
        jobs.extend(names)
        w.extend((*tile, names[-1]) for tile in tiles)

    def out_jobs(b, name):
        for t in range(DT):
            use([("in", C_GATE + b * D + t * P)], f"og{b}_{t}")
            use([(name, t * P)], f"ob{b}_{t}")

    for t in range(DT):
        use([("in", C_LX + t * P)], f"lx{t}")
        use([("in", C_LG + t * P)], f"lg{t}")
        jobs.extend([f"lr{t}", f"li{t}"])
    jobs.append("lt")
    out_jobs(0, "lru_out")
    use([("in", C_LOW)], "low")
    use([("in", C_DT)], "dt")
    for h in range(GH):
        jobs.append(f"ga{h}")
        use([("in", C_Q + h * P)], f"gq{h}")
        use([("in", C_K + h * P)], f"gk{h}")
        use([("in", C_V + h * DV), ("in", C_V + h * DV + P)], f"gva{h}", f"gvb{h}")
        jobs.append(f"gt{h}")
        for v in range(2):
            use([("in", C_R + h * DV + v * P)], f"gr{h}_{v}")
        jobs.extend(f"go{h}_{c}" for c in range(TT + 1))
    out_jobs(1, "gla_out")
    jobs.append("dtt")
    for t in range(CT):
        use([("in", C_XBC + t * P)], f"sx{t}")
        if t < CT - 1:
            jobs.append(f"st{t}")
    jobs.append("qt")
    for z in range(4):
        use([("in", C_Z + 2 * z * P), ("in", C_Z + (2 * z + 1) * P)], f"sza{z}", f"szb{z}")
    for c in range(TT + 1):
        jobs.append(f"sc{c}")
        if c == TT:
            jobs.append("po")
            jobs.extend(f"si{b}" for b in range(NB))
        for g in range(2):
            jobs.extend([f"ss{c}_{g}", f"sy{c}_{g}", f"sn{c}_{g}"])
    for b in range(NB):
        jobs.extend([f"ua{b}", f"ub{b}", f"uc{b}"])
    out_jobs(2, "ssd_out")
    for t in range(DT):
        use([("mix", t * P)], f"mx{t}")
    jobs.extend(["xn", "mt0", "mt1"])
    for i in range(4):
        use([("xk", 2 * i * P), ("xk", (2 * i + 1) * P)], f"mk{i}")
    jobs.extend(["kt0", "kt1"])
    for i in range(4):
        use([("xv", 2 * i * P), ("xv", (2 * i + 1) * P)], f"mv{i}")
    for t in range(DT):
        use([("xq", t * P)], f"xq{t}")
    jobs.append("xs0")
    for c in range(TT + 1):
        if c + 1 < TT:
            jobs.append(f"xs{c + 1}")
        if c == TT:
            jobs.append(f"xs{c}")
        jobs.extend([f"xp{c}", f"xv{c}"])
    for t in range(DT):
        use([("xo", t * P)], f"xo{t}")
    jobs.append("fn")
    for c in range(FC + 1):
        for i in range(2 if c < FC else 0):
            use([("fg", (2 * c + i) * P)], f"fg{c}_{i}")
            use([("fu", (2 * c + i) * P)], f"fu{c}_{i}")
        for i in range(2 if c else 0):
            use([("fd", (c - 1, i))], *(f"fd{c - 1}_{t}" for t in range(4 * i, 4 * i + 4)))
    jobs.append("yn")
    jobs.extend(f"yt{c}" for c in range(TT + 1))
    return w, jobs


WLIST, JOBS = plan()
JOB = {name: n for n, name in enumerate(JOBS)}
FIRST_W = {}
for _n, _tile in enumerate(WLIST):
    FIRST_W.setdefault(_tile[:2], _n)


NW_AT = {0: 0, 1: 32, 2: 74, 3: 108, 4: 148}


def build(nc, ins, outs, stop=99):
    I, O = ins, outs
    ctx = ExitStack()
    with ctx:
        def sb(name, shape, dt=F32):
            return ctx.enter_context(nc.sbuf_tensor(name, shape, dt))

        def sem(name):
            return ctx.enter_context(nc.semaphore(name))

        base = -(-nc.sbuf_base // 32) * 32
        arena = sb("arena", [P, 4 * DT * T + 8])

        def at(name, shape, dt, offset):
            return nc.alloc_sbuf_tensor_at(name, shape, dt, offset=base + offset)

        HALF = 4 * DT * T
        Hh = at("Hh", [P, DT, T], F32R, 0)
        Hl = at("Hl", [P, DT, T], F32R, HALF)
        Yh = at("Yh", [P, DT, T], F32R, 2 * HALF)
        Yl = at("Yl", [P, DT, T], F32R, 3 * HALF)
        YA = at("YA", [P, 2 * DT, T], F32, 2 * HALF)
        X = at("X", [P, DT, T], F32, 2 * HALF)
        XT = at("XT", [P, 2, TT + 1, P], F32, 3 * HALF)
        MNh = at("MNh", [P, DT, M], F32R, 3 * HALF)
        MNl = at("MNl", [P, DT, M], F32R, 3 * HALF + 4 * DT * M)
        KM = at("KM", [P, 2, D], F32, 3 * HALF + 8 * DT * M)
        Q = at("Q", [P, DT, T], F32, 3 * HALF)
        Fh = at("Fh", [P, 2, 2, T], F32R, 3 * HALF)
        Fl = at("Fl", [P, 2, 2, T], F32R, 3 * HALF + 16 * T)
        Wr = sb("Wr", [P, 2, DT, P])
        Wh = sb("Wh", [P, 2, DT, P], F32R)
        Wl = sb("Wl", [P, 2, DT, P], F32R)
        WK = sb("WK", [P, 8 * WT])
        ident = sb("ident", [P, P])
        ones = sb("ones", [P, P])
        m_le = sb("m_le", [P, P])
        m_gt = sb("m_gt", [P, P])
        m_ch = sb("m_ch", [P, P])
        s_le = sb("s_le", [TS, TS])
        s_gt = sb("s_gt", [TS, TS])
        seqcol = sb("seqcol", [TS, NB])
        seqm = sb("seqm", [P, NB, TS], mybir.dt.bfloat16)
        rmask = sb("rmask", [P, T], mybir.dt.bfloat16)
        PV = sb("PV", [P, DT, NROW])
        PQ = sb("PQ", [P, CT, QROW])
        SC = sb("SC", [P, DT, 3])
        CB = sb("CB", [P, DT, 36])
        CQ = sb("CQ", [P, CT, 27])
        NSC = sb("NSC", [P, DT])
        LAM = sb("LAM", [P, 4, DT])
        EPSC = sb("EPSC", [P, 1])
        ST = sb("ST", [P, 48])

        def wk(i, n=WT, off=0):
            return WK[:, i * WT + off:i * WT + off + n]

        PS = ctx.enter_context(nc.psum_tensor("PS", [P, 2, 3, 512], F32))
        PM = ctx.enter_context(nc.psum_tensor("PM", [P, 2, 512], F32))

        DTK = wk(7, 288).rearrange("p (s c h) -> p s c h", s=2, c=TT + 1)
        H_ssd = wk(7, 512, 288)
        CBM = wk(7, 256, 800)
        DBC = wk(7, SH, 1056)
        EL = wk(3, 128, D)
        EC = wk(4, 32, D)
        WJ = wk(4, 16, D + 32)
        DAB = wk(6, 128, D)
        CZ = wk(6, 512).rearrange("p (b t) -> p b t", b=NB)
        YI = [wk(7, 512, 288), wk(2, 512, 512)]

        MV = WK[:, 2 * WT:2 * WT + 2 * D].rearrange("p (m f) -> p m f", m=2)
        KT_m = WK[:, 0:DT * M].rearrange("p (k m) -> p k m", k=DT)
        KVb = [WK[:, i * 2 * WT:i * 2 * WT + 2 * D].rearrange("p (m f) -> p m f", m=2) for i in range(2)]
        KTb = WK[:, 4 * WT:4 * WT + DT * M].rearrange("p (k m) -> p k m", k=DT)
        QZb = WK[:, 6 * WT:6 * WT + 2 * DT * 120].rearrange("p (a k t) -> p a k t", a=2, k=DT)

        def Pr(c):
            return wk(4 + c % 2 if c < TT else 6, D)

        def PrT(c):
            return wk(6 + c % 2 if c < TT else 7, D).rearrange("p (k t) -> p k t", k=DT)

        merged = nc.dram_tensor("merged", (3, DT, P, T), F32, kind="Internal").ap()
        dt_scr = nc.dram_tensor("dt_scr", (SH, T), F32, kind="Internal").ap()
        x_scr = nc.dram_tensor("x_scr", ((TT + 1) * P, D), F32, kind="Internal").ap()
        z_scr = nc.dram_tensor("z_scr", ((TT + 1) * P, D), F32, kind="Internal").ap()

        ps_ready = [sem("ps_ready0"), sem("ps_ready1")]
        ps_free = [sem("ps_free0"), sem("ps_free1")]
        w_loaded = [sem("w_loaded0"), sem("w_loaded1")]
        w_split = sem("w_split")
        w_hi = sem("w_hi")
        masks = sem("masks")
        act_chain = sem("act_chain")
        dve_chain = sem("dve_chain")
        packs = sem("packs")
        packs_zero = sem("packs_zero")
        stored = sem("stored")
        pack_cols = sem("pack_cols")
        NMASK = 25
        NPACK = 18
        NW = NW_AT[stop] if stop in NW_AT else len(WLIST)

        def ready(eng, name):
            n = JOB[name]
            eng.wait_ge(ps_ready[n % 2], n // 2 + 1)

        def read(eng, name):
            n = JOB[name]
            eng.wait_ge(ps_free[n % 2], n // 2 + 1)

        def free_set(eng, name):
            n = JOB[name]
            if n >= 2:
                eng.wait_ge(ps_free[n % 2], n // 2)

        def branch_done(eng, b):
            if b == 0:
                eng.wait_ge(S("y_lo"), DT)
            elif b == 1:
                eng.wait_ge(S("gy_lo"), GH)
            else:
                eng.wait_ge(S("sy_lo"), 2 * (TT + 1))
                read(eng, f"ub{NB - 1}")
                ready(eng, f"uc{NB - 1}")

        def sum_stored(eng, b, t):
            eng.wait_ge(S(f"m_put{t % 2}"), 16 * (b * DT // 2 + t // 2 + 1))

        def pset(name):
            return PS[:, JOB[name] % 2]

        def done(ins, name):
            ins.then_inc(ps_ready[JOB[name] % 2], 1)

        def freed(ins, name):
            ins.then_inc(ps_free[JOB[name] % 2], 1)

        n_stores = [0]
        sems = {}

        def S(name):
            if name not in sems:
                sems[name] = sem(name)
            return sems[name]

        def seqs(ap):
            return ap[:, LP:T].rearrange("p (b l) -> p b l", b=NB)

        def bc(ap, n):
            return ap.unsqueeze(2).broadcast_to([ap.shape[0], ap.shape[1], n])

        def mid(ap, n):
            return ap.unsqueeze(1).broadcast_to([ap.shape[0], n, ap.shape[1]])

        block = ctx.enter_context(nc.Block())

        @block.sync
        def _(sp):
            src = {"in": "w_in", "lru_out": "w_lru_out", "gla_out": "w_gla_out", "ssd_out": "w_ssd_out",
                   "mix": "w_mix_out", "xk": "w_xk", "xv": "w_xv", "xq": "w_xq", "xo": "w_xo",
                   "fg": "w_ffn_gate", "fu": "w_ffn_up"}
            for n, (kind, col, _) in enumerate(WLIST[:NW]):
                if n >= 2:
                    sp.wait_ge(w_split, n - 1)
                if kind == "fd":
                    c, half = col
                    tile = I["w_ffn_down"][0, 2 * c * P:(2 * c + 2) * P, half * 512:half * 512 + 512]
                    dst = Wr[:, n % 2].rearrange("p (k a) m -> p k (a m)", k=2)
                    sp.dma_start(dst, tile.rearrange("(k p) m -> p k m", p=P)).then_inc(w_loaded[n % 2], 16)
                else:
                    tile = I[src[kind]][0, :, col:col + P]
                    sp.dma_start(Wr[:, n % 2], tile.rearrange("(k p) m -> p k m", p=P)).then_inc(w_loaded[n % 2], 16)

        @block.gpsimd
        def _(pool):
            chain = [0]

            def link(ins):
                chain[0] += 1
                ins.then_inc(masks, 1)
                pool.wait_ge(masks, chain[0])

            def select(tile, compare, pattern, base, cm, fill=0.0):
                link(pool.affine_select(out=tile, in_=tile, pattern=pattern, compare_op=compare, fill=fill,
                                        base=base, channel_multiplier=cm))

            GE = ALU.is_ge
            link(pool.memset(ident[:], 0.0))
            select(ident[:], ALU.not_equal, [[-1, P]], 0, 1, 1.0)
            for tile in (ones, m_le, m_gt, m_ch, s_le, s_gt, seqcol, seqm, rmask):
                link(pool.memset(tile[:], 1.0))
            select(m_le[:], GE, [[1, P]], 0, -1)
            select(m_gt[:], GE, [[-1, P]], -1, 1)
            select(m_ch[:], GE, [[1, P]], 0, -1)
            ch = m_ch[:].rearrange("p (a c) -> p a c", a=2)
            select(ch, GE, [[-GCH, 2], [0, GCH]], 0, 1)
            sl = s_le[:].rearrange("p (b c) -> p b c", b=NB)
            select(sl, GE, [[LS, NB], [1, LS]], 0, -1)
            select(sl, GE, [[-LS, NB], [0, LS]], 0, 1)
            sg = s_gt[:].rearrange("p (b c) -> p b c", b=NB)
            select(sg, GE, [[-LS, NB], [-1, LS]], -1, 1)
            select(sg, GE, [[LS, NB], [0, LS]], LS - 1, -1)
            select(seqcol[:], GE, [[-LS, NB]], 0, 1)
            select(seqcol[:], GE, [[LS, NB]], LS - 1, -1)
            select(seqm[:], GE, [[-LS, NB], [1, TS]], 0, 0)
            select(seqm[:], GE, [[LS, NB], [-1, TS]], LS - 1, 0)
            link(pool.memset(rmask[:, 0:LP].rearrange("p (a c) -> p a c", c=GCH)[:, :, 0:1], 0.0))
            link(pool.memset(seqs(rmask[:])[:, :, 0:1], 0.0))
            assert chain[0] == NMASK, chain[0]
            for n in range(NW):
                pool.wait_ge(w_loaded[n % 2], 16 * (n // 2 + 1))
                if n >= 2:
                    ready(pool, WLIST[n - 2][2])
                pool.tensor_copy(Wh[:, n % 2], Wr[:, n % 2]).then_inc(w_hi, 1)
                pool.wait_ge(w_hi, n + 1)
                pool.tensor_tensor(Wl[:, n % 2], Wr[:, n % 2], Wh[:, n % 2].bitcast(F32),
                                   ALU.subtract).then_inc(w_split, 1)

        @block.tensor
        def _(pe):
            def project(name, w, Rh, Rl, by_tile=None, last=True):
                pe.wait_ge(w_split, w + 1)
                free_set(pe, name)
                for k in range(DT):
                    if by_tile:
                        pe.wait_ge(S(by_tile), k + 1)
                    for i, (L, R) in enumerate(((Wh, Rh), (Wh, Rl), (Wl, Rh))):
                        for g, (t0, n) in enumerate(GROUPS):
                            mm = pe.matmul(pset(name)[:, g, 0:n], L[:, w % 2, k, :], R[:, k, t0:t0 + n],
                                           start=(k == 0 and i == 0), stop=(last and k == DT - 1 and i == 2),
                                           skip_group_check=not last)
                return mm

            def project_tokens(name, w, tiles, Ah=Hh, Al=Hl):
                pe.wait_ge(w_split, w + 2)
                free_set(pe, name)
                for j, c in enumerate(tiles):
                    n = P if c < TT else TS
                    for k in range(DT):
                        for i, (A, W) in enumerate(((Ah, Wh), (Al, Wh), (Ah, Wl))):
                            mm = pe.matmul(pset(name)[0:n, j // 2, (j % 2) * 256:(j % 2) * 256 + 256]
                                           .rearrange("p (a m) -> p a m", a=2),
                                           A[:, k, c * P:c * P + n], W[:, :, k, :],
                                           start=(k == 0 and i == 0), stop=(k == DT - 1 and i == 2))
                return mm

            def turn(out, in_, n):
                return pe.transpose(out, in_, ident[0:n, 0:n])

            def fp32_all(name, lhsT, rhs):
                for g, (t0, n) in enumerate(GROUPS):
                    mm = pe.matmul(pset(name)[:, g, 0:n], lhsT, rhs[:, t0:t0 + n], start=True, stop=True)
                return mm

            def out_jobs(b, kind):
                for t in range(DT):
                    done(project(f"og{b}_{t}", FIRST_W["in", C_GATE + b * D + t * P], Hh, Hl), f"og{b}_{t}")
                    if t == 0:
                        branch_done(pe, b)
                    done(project(f"ob{b}_{t}", FIRST_W[kind, t * P], Yh, Yl), f"ob{b}_{t}")

            pe.wait_ge(masks, NMASK)
            pe.wait_ge(packs, 16 * NPACK)
            for k in range(DT):
                mm = turn(pset("pk0")[:, 0, k * NROW:(k + 1) * NROW], wk(0)[0:NROW, k * P:(k + 1) * P], NROW)
            done(mm, "pk0")
            for k in range(CT):
                mm = turn(pset("pk1")[:, 0, k * QROW:(k + 1) * QROW], WK[0:QROW, WT + k * P:WT + (k + 1) * P], QROW)
            done(mm, "pk1")
            for c in range(TT + 1):
                n = P if c < TT else TS
                pe.wait_ge(S("x_scaled"), c + 1)
                free_set(pe, f"xt{c}")
                for k in range(DT):
                    mm = turn(pset(f"xt{c}")[:, k // 4, (k % 4) * P:(k % 4) * P + n],
                              wk(5 + c % 2)[0:n, k * P:(k + 1) * P], n)
                done(mm, f"xt{c}")
            if stop < 1:
                return
            pe.wait_ge(S("h_lo"), TT + 1)
            for t in range(DT):
                done(project(f"lx{t}", FIRST_W["in", C_LX + t * P], Hh, Hl), f"lx{t}")
                done(project(f"lg{t}", FIRST_W["in", C_LG + t * P], Hh, Hl), f"lg{t}")
                if t == 0:
                    pe.wait_ge(S("wax"), 64)
                pe.wait_ge(S("conv"), t + 1)
                for name, off in ((f"lr{t}", 0), (f"li{t}", P)):
                    free_set(pe, name)
                    done(fp32_all(name, YA[:, DT + t, off:off + P], wk(1)), name)
            pe.wait_ge(S("cb"), DT)
            free_set(pe, "lt")
            for k in range(DT):
                mm = turn(pset("lt")[0:36, k // 4, (k % 4) * P:(k % 4 + 1) * P], CB[:, k, :], P)
            done(mm, "lt")
            out_jobs(0, "lru_out")
            if stop < 2:
                return
            V = WK[:, 6 * WT:8 * WT].rearrange("p (c v) -> p c v", c=TT + 1)
            KEt = wk(1).rearrange("p (c d) -> p c d", c=TT + 1)
            QT, KT = wk(3)[:, 0:T], wk(4)[:, 0:T]
            done(project("low", FIRST_W["in", C_LOW], Hh, Hl), "low")
            done(project("dt", FIRST_W["in", C_DT], Hh, Hl), "dt")
            for h in range(GH):
                A = [YA[:, i] for i in (2 * h, 2 * h + 1, DT + 2 * h, DT + 2 * h + 1)]
                name = f"ga{h}"
                read(pe, "low")
                pe.wait_ge(S(f"wal{h % 2}"), 16 * (h // 2 + 1))
                free_set(pe, name)
                done(fp32_all(name, CB[0:16].rearrange("p k c -> p (k c)")[:, h % 2 * P:h % 2 * P + P],
                              wk(0)[0:16]), name)
                done(project(f"gq{h}", FIRST_W["in", C_Q + h * P], Hh, Hl), f"gq{h}")
                done(project(f"gk{h}", FIRST_W["in", C_K + h * P], Hh, Hl), f"gk{h}")
                wv = FIRST_W["in", C_V + h * DV]
                done(project_tokens(f"gva{h}", wv, range(0, 5)), f"gva{h}")
                done(project_tokens(f"gvb{h}", wv, range(5, TT + 1)), f"gvb{h}")
                name = f"gt{h}"
                pe.wait_ge(S("ke"), h + 1)
                free_set(pe, name)
                for c in range(TT + 1):
                    n = P if c < TT else TS
                    mm = turn(pset(name)[0:n, c // 4, (c % 4) * P:(c % 4 + 1) * P], A[0][:, c * P:c * P + n], P)
                done(mm, name)
                for v in range(2):
                    done(project(f"gr{h}_{v}", FIRST_W["in", C_R + h * DV + v * P], Hh, Hl), f"gr{h}_{v}")
                att = lambda c: A[1][:, c % 2 * P:c % 2 * P + P]
                on = lambda c: A[1][:, 256 + c % 2 * DV:256 + (c % 2 + 1) * DV]
                St = lambda c: A[2][:, c % 2 * DV:(c % 2 + 1) * DV]
                QZ = A[2][:, 512:1024].rearrange("p (b t) -> p b t", b=NB)
                KEm = A[0][0:TS, 0:D].rearrange("p (b d) -> p b d", b=NB)
                Sb = lambda b: A[3][:, b % 2 * DV:(b % 2 + 1) * DV]

                def turn_o(c):
                    n = P if c < TT else TS
                    q = h * (TT + 1) + c
                    read(pe, f"go{h}_{c}")
                    if q:
                        pe.wait_ge(S("ymul"), q)
                    for v in range(2):
                        mm = turn(PM[:, 1, v * P:v * P + n],
                                  on(c)[0:n, v * P:(v + 1) * P], n)
                    mm.then_inc(S("ot"), 1)
                read(pe, f"gt{h}")
                read(pe, f"gvb{h}")
                for c in range(TT + 1):
                    n = P if c < TT else TS
                    name = f"go{h}_{c}"
                    q = h * (TT + 1) + c
                    free_set(pe, name)
                    cols = slice(c * P, c * P + n)
                    pe.matmul(pset(name)[0:n, 1, 0:n], KT[:, cols], QT[:, cols], start=True, stop=True)\
                        .then_inc(S("att"), 1)
                    if c < TT:
                        for i in range(2):
                            e = h * 24 + 2 * c + i
                            if i == 0 and e >= 2:
                                pe.wait_ge(S("s_upd"), e - 1)
                            pe.matmul(PM[:, 0, 0:256] if i == 0 else pset(name)[:, 2, 0:256],
                                      KEt[64 * i:64 * i + 64, c, :], V[64 * i:64 * i + 64, c, :],
                                      start=True, stop=True).then_inc(S("ds"), 1)
                        pe.wait_ge(S("att_m"), q + 1)
                        pe.matmul(pset(name)[:, 0, 0:DV], att(c), V[:, c, :], start=True, stop=False,
                                  skip_group_check=True)
                        for i in range(2):
                            e = h * 24 + 2 * c + i
                            if c == 0 and i == 0:
                                pe.wait_ge(S("s_zero"), h + 1)
                            else:
                                pe.wait_ge(S("s_upd"), e)
                            mm = pe.matmul(pset(name)[64 * i:64 * i + 64, 0, 0:DV],
                                           QT[:, c * P + 64 * i:c * P + 64 * i + 64], St(e),
                                           start=False, stop=True, skip_group_check=True)
                            if i == 0:
                                mm.then_inc(S("inter"), 1)
                    else:
                        pe.wait_ge(S("att_m"), q + 1)
                        pe.matmul(pset(name)[0:n, 0, 0:DV], att(c)[0:n, 0:n], V[0:n, c, :], start=True, stop=False,
                                  skip_group_check=True)
                        pe.wait_ge(S("kem"), h + 1)
                        for b in range(NB):
                            e = h * 24 + 16 + b
                            pe.wait_ge(S("s_upd"), e - 1)
                            pe.matmul(PM[:, 0, 0:256] if b % 2 == 0 else pset(name)[:, 2, 0:256], KEm[:, b, :], V[0:TS, c, :],
                                      start=True, stop=True).then_inc(S("ds"), 1)
                            pe.wait_ge(S(f"sb_in{b % 2}"), 16 * (h * 4 + b // 2 + 1))
                            mm = pe.matmul(pset(name)[0:n, 0, 0:DV], QZ[:, b, :], Sb(b), start=False,
                                           stop=(b == NB - 1), skip_group_check=True)
                            if b < NB - 1:
                                mm.then_inc(S("sb_int"), 1)
                    done(mm, name)
                    if c:
                        turn_o(c - 1)
                turn_o(TT)
            out_jobs(1, "gla_out")
            if stop < 3:
                return
            bT, cT = wk(0), wk(1)
            b_tok = wk(2).rearrange("p (c n) -> p c n", c=TT + 1)
            pe.wait_ge(S("dt_done"), 1)
            free_set(pe, "dtt")
            for s, src in enumerate((5, 6)):
                for c in range(TT + 1):
                    n = P if c < TT else TS
                    o = (s * (TT + 1) + c) * SH
                    mm = turn(pset("dtt")[0:n, 0, o:o + SH], wk(src)[0:SH, c * P:c * P + n], SH)
            done(mm, "dtt")

            def turn_channels(t):
                name = f"st{t}"
                pe.wait_ge(S("s_act"), t + 1)
                free_set(pe, name)
                src = wk(4) if t < DT else bT
                for c in range(TT + 1):
                    n = P if c < TT else TS
                    mm = turn(pset(name)[0:n, c // 4, (c % 4) * P:(c % 4 + 1) * P], src[:, c * P:c * P + n], P)
                done(mm, name)
            for t in range(CT):
                done(project(f"sx{t}", FIRST_W["in", C_XBC + t * P], Hh, Hl), f"sx{t}")
                if t < CT - 1:
                    turn_channels(t)
            free_set(pe, "qt")
            pe.wait_ge(S("sconv"), CT)
            for k in range(CT):
                mm = turn(pset("qt")[0:27, k // 4, (k % 4) * P:(k % 4 + 1) * P], CQ[:, k, :], P)
            done(mm, "qt")
            for z in range(4):
                wz = FIRST_W["in", C_Z + 2 * z * P]
                done(project_tokens(f"sza{z}", wz, range(0, 5)), f"sza{z}")
                done(project_tokens(f"szb{z}", wz, range(5, TT + 1)), f"szb{z}")
            for c in range(TT + 1):
                n = P if c < TT else TS
                cols = slice(c * P, c * P + n)
                le, gt = (m_le, m_gt) if c < TT else (s_le, s_gt)
                da = DTK[0:n, 1, c, :]
                name = f"sc{c}"
                free_set(pe, name)
                if c == 0:
                    pe.wait_ge(S("s_act"), CT)
                    read(pe, "dtt")
                    read(pe, f"st{CT - 2}")
                ps = pset(name)
                pe.matmul(ps[0:n, 0, 0:16], le[:], da, start=True, stop=True)
                pe.matmul(ps[0:n, 0, 16:32], gt[:], da, start=True, stop=True)
                if c < TT:
                    pe.matmul(ps[:, 0, 32:48], ones[:], da, start=True, stop=True)
                else:
                    pe.wait_ge(S("dab"), 1)
                    pe.matmul(ps[:, 0, 32:160], ones[0:n], DAB[0:n], start=True, stop=True)
                for g in range(2):
                    mm = pe.matmul(ps[0:n, 1 + g, 0:n], bT[64 * g:64 * g + 64, cols], cT[64 * g:64 * g + 64, cols],
                                   start=True, stop=True)
                done(mm, name)
                if c == TT:
                    free_set(pe, "po")
                    for k in range(4):
                        mm = turn(pset("po")[:, 0, k * P:(k + 1) * P], H_ssd[:, k * P:(k + 1) * P], P)
                    done(mm, "po")
                    pe.wait_ge(S("cz"), 1)
                    for b in range(NB):
                        name = f"si{b}"
                        pe.wait_ge(S(f"h_in{b % 2}"), 16 * 2 * (b // 2 + 1))
                        free_set(pe, name)
                        for k in range(4):
                            mm = turn(pset(name)[:, 0, k * P:(k + 1) * P],
                                      wk(0, P, b % 2 * 512 + k * P), P)
                        done(mm, name)
                        read(pe, name)
                        for g in range(2):
                            mm = pe.matmul(PM[0:TS, g, :], CZ[64 * g:64 * g + 64, b, :],
                                           wk(1, 512, b % 2 * 512)[64 * g:64 * g + 64], start=(b == 0),
                                           stop=(b == NB - 1))
                        mm.then_inc(S("si_mm"), 1)
                for g in range(2):
                    q = 2 * c + g
                    name = f"ss{c}_{g}"
                    pe.wait_ge(S("r"), q + 1)
                    free_set(pe, name)
                    for i in range(8 * n // 512):
                        mm = pe.matmul(pset(name)[0:n, i, :], gt[:], wk(6)[0:n, i * 512:(i + 1) * 512],
                                       start=True, stop=True)
                    done(mm, name)
                    name = f"sy{c}_{g}"
                    pe.wait_ge(S("m"), q + 1)
                    free_set(pe, name)
                    ps = pset(name)
                    for h in range(8):
                        mm = pe.matmul(ps[0:n, 0, h * HD:(h + 1) * HD], wk(6)[0:n, h * n:(h + 1) * n],
                                       wk(5)[0:n, h * HD:(h + 1) * HD], start=True, stop=True)
                    if c < TT:
                        pe.matmul(ps[0:n, 1, :], cT[64 * g:64 * g + 64, cols], H_ssd[64 * g:64 * g + 64],
                                  start=True, stop=True)
                        mm = pe.matmul(ps[64 * g:64 * g + 64, 2, :], b_tok[0:n, c, 64 * g:64 * g + 64],
                                       wk(5)[0:n, 512:1024], start=True, stop=True)
                    done(mm, name)
                    name = f"sn{c}_{g}"
                    pe.wait_ge(S("y_norm"), q + 1)
                    free_set(pe, name)
                    for k in range(4):
                        mm = turn(pset(name)[:, 0, k * P:k * P + n], wk(4)[0:n, 512 + k * P:512 + (k + 1) * P], n)
                    done(mm, name)
            for b in range(NB):
                name = f"ua{b}"
                pe.wait_ge(S(f"h_in{b % 2}"), 16 * 2 * (4 + b // 2 + 1))
                free_set(pe, name)
                for k in range(4):
                    mm = turn(pset(name)[:, 0, k * P:(k + 1) * P], wk(0, P, b % 2 * 512 + k * P), P)
                done(mm, name)
                name = f"ub{b}"
                pe.wait_ge(S("bm"), b + 1)
                free_set(pe, name)
                for g in range(2):
                    mm = pe.matmul(pset(name)[64 * g:64 * g + 64, 0, :], wk(5 + b % 2, P, D)[0:TS, 64 * g:64 * g + 64],
                                   wk(5)[0:TS, g * 512:(g + 1) * 512], start=True, stop=True)
                done(mm, name)
                name = f"uc{b}"
                read(pe, f"ub{b}")
                free_set(pe, name)
                for k in range(4):
                    mm = turn(pset(name)[:, 0, k * P:(k + 1) * P], wk(2, P, k * P), P)
                done(mm, name)
            out_jobs(2, "ssd_out")
            if stop < 4:
                return
            for t in range(DT):
                name = f"mx{t}"
                project(name, FIRST_W["mix", t * P], Hh, Hl, by_tile="mi_lo" if t == 0 else None, last=False)
                pe.wait_ge(S(f"xt_in{t % 2}"), 32 * (t // 2 + 1))
                for c in range(TT + 1):
                    n = P if c < TT else TS
                    mm = pe.matmul(pset(name)[:, c // 3, c % 3 * P:c % 3 * P + n], XT[0:n, t % 2, c, :],
                                   ident[0:n, 0:n], start=False, stop=True, skip_group_check=True)
                done(mm, name)

            def sum_squares(i, name):
                free_set(pe, name)
                for k in range(DT):
                    pe.wait_ge(S("nrm_sq"), i * DT + k + 1)
                    for g, (t0, n) in enumerate(GROUPS):
                        mm = pe.matmul(pset(name)[:, g, 0:n], ones[:], wk(4 + k % 2)[:, t0:t0 + n],
                                       start=(k == 0), stop=(k == DT - 1))
                    if k < DT - 1:
                        mm.then_inc(S("nrm_mm"), 1)
                done(mm, name)
            sum_squares(0, "xn")
            for i in range(2):
                name = f"mt{i}"
                pe.wait_ge(S("mem_scaled"), 2)
                free_set(pe, name)
                for k in range(DT):
                    mm = turn(pset(name)[:, k // 4, k % 4 * P:(k % 4 + 1) * P], MV[:, i, k * P:(k + 1) * P], P)
                done(mm, name)
            pe.wait_ge(S("mem_lo"), 2)
            for i in range(4):
                done(project_tokens(f"mk{i}", FIRST_W["xk", 2 * i * P], range(2), MNh, MNl), f"mk{i}")
            for i in range(2):
                name = f"kt{i}"
                for j in range(4):
                    read(pe, f"mk{j}")
                free_set(pe, name)
                for k in range(DT):
                    mm = turn(pset(name)[:, k // 4, k % 4 * P:(k % 4 + 1) * P], KM[:, i, k * P:(k + 1) * P], P)
                done(mm, name)
            for i in range(4):
                done(project_tokens(f"mv{i}", FIRST_W["xv", 2 * i * P], range(2), MNh, MNl), f"mv{i}")
            pe.wait_ge(S("nrm_lo"), DT)
            for t in range(DT):
                done(project(f"xq{t}", FIRST_W["xq", t * P], Hh, Hl), f"xq{t}")

            def scores(c):
                name = f"xs{c}"
                free_set(pe, name)
                if c == 0:
                    read(pe, f"xq{DT - 2}")
                    read(pe, f"xq{DT - 1}")
                for h in range(XH):
                    for k in range(2):
                        mm = pe.matmul(pset(name)[:, h // 2, h % 2 * M:(h % 2 + 1) * M],
                                       Q[:, 2 * h + k, c * P:(c + 1) * P], KT_m[:, 2 * h + k, :],
                                       start=(k == 0), stop=(k == 1))
                done(mm, name)

            def turn_probs(c):
                n = P if c < TT else TS
                name = f"xp{c}"
                pe.wait_ge(S("x_p"), c + 1)
                free_set(pe, name)
                for k in range(DT):
                    mm = turn(pset(name)[:, k // 4, k % 4 * P:k % 4 * P + n], Pr(c)[0:n, k * P:(k + 1) * P], n)
                done(mm, name)

            def attend(c):
                name = f"xv{c}"
                read(pe, f"xp{c}")
                free_set(pe, name)
                for k in range(DT):
                    for m in range(2):
                        mm = pe.matmul(pset(name)[:, k // 4, k % 4 * P:(k % 4 + 1) * P], MV[:, m, k * P:(k + 1) * P],
                                       PrT(c)[:, k // 2 * 2 + m, :], start=(m == 0), stop=(m == 1))
                done(mm, name)
            scores(0)
            for c in range(TT):
                if c + 1 < TT:
                    scores(c + 1)
                turn_probs(c)
                attend(c)
            name = f"xs{TT}"
            free_set(pe, name)
            for s in range(4 * NB + 2):
                if s < 4 * NB:
                    b, h = divmod(s, 4)
                    if h == 0:
                        pe.wait_ge(S(f"kv_in{b % 2}"), 16 * (b // 2 + 1))
                    if s >= 2:
                        pe.wait_ge(S("kb_e"), s - 1)
                    for k in range(2):
                        for m in range(2):
                            mm = turn(PM[:, s % 2, (2 * k + m) * P:(2 * k + m + 1) * P],
                                      KVb[b % 2][:, m, (2 * h + k) * P:(2 * h + k + 1) * P], P)
                    mm.then_inc(S("kb_t"), 1)
                if s >= 2:
                    b, h = divmod(s - 2, 4)
                    pe.wait_ge(S("kb_e"), s - 1)
                    pe.wait_ge(S("qz"), b + 1)
                    for k in range(2):
                        mm = pe.matmul(pset(name)[0:TS, h // 2, h % 2 * M:(h % 2 + 1) * M],
                                       QZb[:, b % 2, 2 * h + k, 56 - LS * b:120 - LS * b], KTb[:, 2 * h + k, :],
                                       start=(b == 0 and k == 0 and h % 2 == 0), stop=(b == NB - 1 and k == 1),
                                       skip_group_check=True)
                    if s < 4 * NB + 1:
                        mm.then_inc(S("kb_s"), 1)
            done(mm, name)
            turn_probs(TT)
            name = f"xv{TT}"
            read(pe, f"xp{TT}")
            free_set(pe, name)
            for b in range(NB):
                pe.wait_ge(S(f"kv_in{b % 2}"), 16 * (4 + b // 2 + 1))
                for k in range(DT):
                    for m in range(2):
                        o = k % 4 * P + LS * b
                        mm = pe.matmul(pset(name)[:, k // 4, o:o + LS], KVb[b % 2][:, m, k * P:(k + 1) * P],
                                       PrT(TT)[:, k // 2 * 2 + m, LS * b:LS * b + LS], start=(m == 0), stop=(m == 1))
                if b < NB - 1:
                    mm.then_inc(S("vb"), 1)
            done(mm, name)
            read(pe, name)
            for t in range(DT):
                done(project(f"xo{t}", FIRST_W["xo", t * P], Hh, Hl), f"xo{t}")
            sum_squares(1, "fn")
            pe.wait_ge(S("nrm_lo"), 2 * DT)
            for c in range(FC + 1):
                if c < FC:
                    for i in range(2):
                        for kind in ("fg", "fu"):
                            name = f"{kind}{c}_{i}"
                            done(project(name, FIRST_W[kind, (2 * c + i) * P], Hh, Hl), name)
                if c:
                    e = c - 1
                    pe.wait_ge(S("f_lo"), 2 * c)
                    for t in range(DT):
                        name = f"fd{e}_{t}"
                        w = FIRST_W["fd", (e, t // 4)]
                        pe.wait_ge(w_split, w + 1)
                        free_set(pe, name)
                        for k in range(2):
                            for i, (L, R) in enumerate(((Wh, Fh), (Wh, Fl), (Wl, Fh))):
                                lhsT = L[:, w % 2].rearrange("p (k a) m -> p k (a m)", k=2)[:, k, t % 4 * P:(t % 4 + 1) * P]
                                for g, (t0, n) in enumerate(GROUPS):
                                    mm = pe.matmul(pset(name)[:, g, 0:n], lhsT, R[:, e % 2, k, t0:t0 + n],
                                                   start=(k == 0 and i == 0), stop=(k == 1 and i == 2))
                        done(mm, name)
            sum_squares(2, "yn")
            for c in range(TT + 1):
                n = P if c < TT else TS
                name = f"yt{c}"
                if c == 0:
                    pe.wait_ge(S("nrm_t"), 3 * DT)
                free_set(pe, name)
                for k in range(DT):
                    mm = turn(pset(name)[0:n, k // 4, k % 4 * P:(k % 4 + 1) * P], X[:, k, c * P:c * P + n], P)
                done(mm, name)

        @block.scalar
        def _(act):
            chain = [0]

            def link(ins):
                chain[0] += 1
                ins.then_inc(act_chain, 1)
                act.wait_ge(act_chain, chain[0])

            def sync_chain():
                act.wait_ge(act_chain, chain[0])

            def all_groups(name, dst, func, bias=0.0, scale=1.0):
                ready(act, name)
                for g, (t0, n) in enumerate(GROUPS):
                    ins = act.activation(dst[:, t0:t0 + n], pset(name)[:, g, 0:n], func, bias=bias, scale=scale)
                freed(ins, name)
                read(act, name)

            def store(dst, src):
                n_stores[0] += 1
                act.dma_start(dst, src).then_inc(stored, 16)

            def out_jobs(b):
                def put(t):
                    act.wait_ge(S(f"m_new{b}"), t + 1)
                    act.dma_start(merged[b, t], wk(4 + t % 2)[:, 0:T]).then_inc(S(f"m_put{t % 2}"), 16)
                for t in range(DT):
                    if b > 0:
                        if t >= 2:
                            act.wait_ge(S(f"m_new{b}"), t - 1)
                        else:
                            branch_done(act, b)
                        sum_stored(act, b - 1, t)
                        act.dma_start(wk(2 + t % 2)[:, 0:T], merged[b - 1, t]).then_inc(S(f"m_get{t % 2}"), 16)
                    if t >= 2:
                        read(act, f"ob{b}_{t - 2}")
                    else:
                        branch_done(act, b)
                    all_groups(f"og{b}_{t}", wk(t % 2), ACT.Tanh, scale=0.5)
                    if t:
                        put(t - 1)
                put(DT - 1)

            act.wait_ge(packs_zero, 2)
            for row, name, n in ((R_CW, "lru_conv_w", CW), (R_CB, "lru_conv_b", 1), (R_BA, "lru_ba", 1),
                                 (R_BX, "lru_bx", 1), (R_LAM, "lru_lambda", 1), (R_NMIX, "norm_mix", 1),
                                 (R_NX, "norm_xattn", 1), (R_NFFN, "norm_ffn", 1), (R_NMEM, "norm_mem", 1),
                                 (R_NSSD, "ssd_norm", 1)):
                src = I[name][0] if n > 1 else I[name]
                act.dma_start(wk(0)[row:row + n, 0:D], src).then_inc(packs, 16)
            act.dma_start(wk(0)[R_NFIN:R_NFIN + 1, 0:D], I["norm_final"].unsqueeze(0)).then_inc(packs, 16)
            act.dma_start(wk(0)[R_CONV:R_CONV + NB * HIST, 0:D],
                          I["state_lru_conv"][0].rearrange("b k f -> (b k) f")).then_inc(packs, 16)
            act.dma_start(wk(0)[R_H0:R_H0 + NB, 0:D], I["state_lru_h"][0]).then_inc(packs, 16)
            act.dma_start(wk(0)[R_GLA:R_GLA + 1, 0:GH * DK], I["gla_b_alpha"]).then_inc(packs, 16)
            act.dma_start(wk(0)[R_GLA:R_GLA + 1, GH * DK:GH * DK + DV], I["gla_norm"]).then_inc(packs, 16)
            pq = WK[:, WT:WT + SCC]
            act.dma_start(pq[Q_CONV:Q_CONV + NB * HIST],
                          I["state_ssd_conv"][0].rearrange("b k f -> (b k) f")).then_inc(packs, 16)
            act.dma_start(pq[Q_CW:Q_CW + CW], I["ssd_conv_w"][0]).then_inc(packs, 16)
            act.dma_start(pq[Q_CB:Q_CB + 1], I["ssd_conv_b"]).then_inc(packs, 16)
            for i, name in enumerate(("lru_wa", "lru_wx")):
                blocks = I[name][0].rearrange("(t two) i j -> two i t j", two=2)
                for h in range(2):
                    act.dma_start(YA[64 * h:64 * h + 64, DT:2 * DT, i * P + 64 * h:i * P + 64 * h + 64],
                                  blocks[h]).then_inc(S("wax"), 16)
            def load_x(c):
                n = P if c < TT else TS
                if c >= 2:
                    act.wait_ge(S("x_scaled"), c - 1)
                x = I["x_prompt"][0, c * P:c * P + n] if c < TT else I["x_sample"].rearrange("b l f -> (b l) f")
                act.dma_start(wk(3 + c % 2)[0:n, 0:D], x).then_inc(S(f"x_in{c % 2}"), 16)
            load_x(0)
            load_x(1)

            def split_x(c):
                n = P if c < TT else TS
                read(act, f"xt{c}")
                act.activation(Hh[:, :, c * P:c * P + n],
                               wk(7)[:, 0:DT * n].rearrange("p (k t) -> p k t", k=DT), ACT.Copy).then_inc(S("h_hi"), 1)
            for c in range(TT + 1):
                n = P if c < TT else TS
                act.wait_ge(S(f"x_in{c % 2}"), 16 * (c // 2 + 1))
                if c >= 2:
                    ready(act, f"xt{c - 2}")
                link(act.activation(wk(5 + c % 2)[0:n, 0:D], wk(3 + c % 2)[0:n, 0:D], ACT.Square,
                                    accum_out=ST[0:n, c:c + 1]))
                act.wait_ge(S("eps"), 1)
                act.activation(ST[0:n, c:c + 1], ST[0:n, c:c + 1], ACT.Sqrt, bias=EPSC[0:n],
                               scale=1.0 / D).then_inc(S("x_std"), 1)
                if c + 2 <= TT:
                    load_x(c + 2)
                if c:
                    split_x(c - 1)
            split_x(TT)
            if stop < 1:
                return
            read(act, "pk0")
            act.activation(LAM[:, 1], PV[:, :, R_LAM], ACT.Relu, scale=-1.0)
            link(act.activation(LAM[:, 0], PV[:, :, R_LAM], ACT.Abs))
            act.activation(LAM[:, 0], LAM[:, 0], ACT.Exp, scale=-1.0).then_inc(S("lam_exp"), 1)
            xin = WK[:, 0:HIST + LP + NB * (HIST + LS)]
            xin_p = xin[:, 0:HIST + LP]
            xin_s = xin[:, HIST + LP:].rearrange("p (b c) -> p b c", b=NB)
            for t in range(DT):
                name = f"lx{t}"
                ready(act, name)
                if t:
                    act.wait_ge(S("conv"), t)
                else:
                    act.wait_ge(S("h_lo"), TT + 1)
                for g, (t0, n) in enumerate(GROUPS):
                    np_ = min(n, LP - t0)
                    ins = act.activation(xin_p[:, HIST + t0:HIST + t0 + np_], pset(name)[:, g, 0:np_], ACT.Copy)
                ins = act.activation(xin_s[:, :, HIST:], pset(name)[:, 2, LP - 768:T - 768]
                                     .rearrange("p (b l) -> p b l", b=NB), ACT.Copy)
                freed(ins, name)
                if t:
                    act.wait_ge(S("y_lo"), t)
                all_groups(f"lg{t}", wk(5), ACT.Copy)
                act.activation(wk(6)[:, 0:T], wk(5)[:, 0:T], ACT.Square).then_inc(S("g_sq"), 1)
                if t == 0:
                    act.wait_ge(S("sc"), 1)
                all_groups(f"lr{t}", wk(2), ACT.Tanh, bias=SC[:, t, 1:2], scale=0.5)
                link(act.activation(wk(3)[:, 0:T], wk(2)[:, 0:T], ACT.Tanh, bias=SC[:, t, 0:1], scale=SC[:, t, 0:1]))
                act.activation(wk(2)[:, 0:T], wk(2)[:, 0:T], ACT.Exp, bias=NSC[:, t:t + 1],
                               scale=NSC[:, t:t + 1]).then_inc(S("a"), 1)
                all_groups(f"li{t}", wk(4), ACT.Tanh, bias=SC[:, t, 2:3], scale=0.5)
                act.wait_ge(S("g_inner"), t + 1)
                act.activation(wk(6)[:, 0:T], wk(6)[:, 0:T], ACT.Tanh, scale=GELU_C).then_inc(S("g_tanh"), 1)
                act.wait_ge(S("u_var"), t + 1)
                act.activation(wk(3)[:, 0:T], wk(3)[:, 0:T], ACT.Sqrt, scale=0.25).then_inc(S("u_mult"), 1)
                act.wait_ge(S("y"), t + 1)
                act.activation(Yh[:, t], wk(5)[:, 0:T], ACT.Copy).then_inc(S("y_hi"), 1)
            ready(act, "lt")
            branch_done(act, 0)
            freed(act.activation(wk(2)[0:36, 0:D], pset("lt")[0:36, 0:2].rearrange("p a c -> p (a c)"), ACT.Copy), "lt")
            read(act, "lt")
            store(O["p_lru_conv"][0, 0], wk(2)[0:3, 0:D])
            store(O["s_lru_conv"][0].rearrange("b k f -> (b k) f"), wk(2)[3:27, 0:D])
            store(O["p_lru_h"][0:1, 0, :], wk(2)[27:28, 0:D])
            store(O["s_lru_h"][0], wk(2)[28:36, 0:D])
            out_jobs(0)
            if stop < 2:
                return
            for t in range(DT - 2, DT):
                sum_stored(act, 0, t)
            act.wait_ge(S("m_new0"), DT)
            V = WK[:, 6 * WT:8 * WT].rearrange("p (c v) -> p c v", c=TT + 1)
            KEt = wk(1).rearrange("p (c d) -> p c d", c=TT + 1)
            RS = [wk(2)[:, 0:T], wk(5)[:, 0:T]]

            def load_alpha(h):
                if h >= 2:
                    ready(act, f"ga{h - 2}")
                act.dma_start(CB[0:16].rearrange("p k c -> p (k c)")[:, h % 2 * P:h % 2 * P + P],
                              I["gla_w_alpha"][0, :, h * P:(h + 1) * P]).then_inc(S(f"wal{h % 2}"), 16)
            load_alpha(0)
            load_alpha(1)
            ready(act, "low")
            for g, (t0, n) in enumerate(GROUPS):
                ins = act.activation(wk(0)[0:16, t0:t0 + n], pset("low")[0:16, g, 0:n], ACT.Copy)
            freed(ins, "low")
            ready(act, "dt")
            for g, (t0, n) in enumerate(GROUPS):
                ins = act.activation(wk(1)[0:16, t0:t0 + n], pset("dt")[0:16, g, 0:n], ACT.Copy)
            freed(ins, "dt")
            read(act, "dt")
            act.dma_start(dt_scr, wk(1)[0:16, 0:T]).then_inc(S("dt_put"), 16)
            act.wait_ge(S("dt_put"), 16)
            for h in range(GH):
                A = [YA[:, i] for i in (2 * h, 2 * h + 1, DT + 2 * h, DT + 2 * h + 1)]
                on = lambda c: A[1][:, 256 + c % 2 * DV:256 + (c % 2 + 1) * DV]
                St = lambda c: A[2][:, c % 2 * DV:(c % 2 + 1) * DV]
                Sb = lambda b: A[3][:, b % 2 * DV:(b % 2 + 1) * DV]
                So = lambda b: A[3][:, 512 + b % 2 * DV:512 + (b % 2 + 1) * DV]
                name = f"ga{h}"
                ready(act, name)
                act.wait_ge(S("nb"), 1)
                for g, (t0, n) in enumerate(GROUPS):
                    act.activation(A[0][:, t0:t0 + n], pset(name)[:, g, 0:n], ACT.Abs, bias=PV[:, h, R_GLA:R_GLA + 1])
                    ins = act.activation(A[1][:, t0:t0 + n], pset(name)[:, g, 0:n], ACT.Relu,
                                         bias=LAM[:, 3, h:h + 1], scale=-1.0)
                freed(ins, name)
                read(act, name)
                link(act.activation(A[0], A[0], ACT.Exp, scale=-1.0))
                act.activation(A[0], A[0], ACT.Ln, bias=1.0).then_inc(S("gl_ln"), 1)
                act.wait_ge(S("gl_cum"), h + 1)
                act.activation(A[2], A[1], ACT.Exp, scale=-1.0 / 16)
                act.activation(A[3], A[1], ACT.Exp, scale=1.0 / 16).then_inc(S("gl_exp"), 1)
                act.wait_ge(S("gl_d"), h + 1)
                act.activation(A[0], A[0], ACT.Exp, scale=-1.0 / 16).then_inc(S("gl_ed"), 1)
                read(act, f"gk{h}")
                for b in range(2):
                    act.dma_start(Sb(b), I["state_gla_S"][0, b, h]).then_inc(S(f"sb_in{b}"), 16)
                name = f"gva{h}"
                ready(act, name)
                act.activation(V[:, 0:4].rearrange("p (a c) v -> p a (c v)", a=2), pset(name)[:, 0:2, :], ACT.Copy)
                freed(act.activation(V[:, 4], pset(name)[:, 2, 0:DV], ACT.Copy), name)
                name = f"gvb{h}"
                ready(act, name)
                act.activation(V[:, 5:7].rearrange("p c v -> p (c v)"), pset(name)[:, 0, :], ACT.Copy)
                act.activation(V[:, 7], pset(name)[:, 1, 0:DV], ACT.Copy)
                freed(act.activation(V[0:TS, 8], pset(name)[0:TS, 1, DV:2 * DV], ACT.Copy), name)
                name = f"gt{h}"
                ready(act, name)
                act.activation(KEt[:, 0:8].rearrange("p (a c) d -> p a (c d)", a=2), pset(name)[:, 0:2, :], ACT.Copy)
                freed(act.activation(KEt[0:TS, 8], pset(name)[0:TS, 2, 0:P], ACT.Copy), name)
                if h:
                    act.wait_ge(S("gy_lo"), h)
                for v in range(2):
                    ready(act, f"gr{h}_{v}")
                    for g, (t0, n) in enumerate(GROUPS):
                        ins = act.activation(RS[v][:, t0:t0 + n], pset(f"gr{h}_{v}")[:, g, 0:n], ACT.Tanh, scale=0.5)
                    ins.then_inc(S("gr_th"), 1)
                if h + 2 < GH:
                    load_alpha(h + 2)
                for c in range(TT + 1):
                    n = P if c < TT else TS
                    q = h * (TT + 1) + c
                    name = f"go{h}_{c}"
                    if c == TT:
                        act.wait_ge(S("s_upd"), h * 24 + 16)
                        act.dma_start(O["p_gla_S"][0, 0, h], St(0)).then_inc(S("gs_put"), 16)
                        for b in range(NB):
                            act.wait_ge(S("s_upd"), h * 24 + 17 + b)
                            act.dma_start(O["s_gla_S"][0, b, h], So(b)).then_inc(S(f"sb_put{b % 2}"), 16)
                            if b + 2 < NB:
                                act.wait_ge(S("sb_int"), h * 7 + b + 1)
                                act.dma_start(Sb(b), I["state_gla_S"][0, b + 2, h]).then_inc(S(f"sb_in{b % 2}"), 16)
                    ready(act, name)
                    if q >= 2:
                        act.wait_ge(S("ot"), q - 1)
                    st = ST[0:n, 24 + q % 2:25 + q % 2]
                    link(act.activation(on(c)[0:n], pset(name)[0:n, 0, 0:DV], ACT.Square, accum_out=st))
                    act.activation(st, st, ACT.Sqrt, bias=EPSC[0:n], scale=1.0 / DV).then_inc(S("g_std"), 1)
                act.wait_ge(S("ymul"), (h + 1) * (TT + 1))
                act.wait_ge(S("gs_put"), 16 * (h + 1))
                for i in range(2):
                    act.wait_ge(S(f"sb_put{i}"), 16 * 4 * (h + 1))
                for v in range(2):
                    act.activation(Yh[:, 2 * h + v], RS[v], ACT.Copy).then_inc(S("gy_hi"), 1)
            out_jobs(1)
            if stop < 3:
                return
            for t in range(DT - 2, DT):
                sum_stored(act, 1, t)
            act.wait_ge(S("m_new1"), DT)
            act.dma_start(wk(6)[0:SH, 0:T], dt_scr).then_inc(S("dt_in"), 16)
            act.dma_start(ST[0:SH, 26:27], I["ssd_dt_bias"].rearrange("o h -> h o")).then_inc(S("dt_in"), 16)
            act.dma_start(ST[0:SH, 27:28], I["ssd_a_log"].rearrange("o h -> h o")).then_inc(S("dt_in"), 16)
            act.dma_start(DBC, I["ssd_d"].broadcast_to([P, SH])).then_inc(S("d_in"), 16)
            act.wait_ge(S("dt_in"), 48)
            act.activation(wk(1)[0:SH, 0:T], wk(6)[0:SH, 0:T], ACT.Relu, bias=ST[0:SH, 26:27])
            act.activation(ST[0:SH, 27:28], ST[0:SH, 27:28], ACT.Exp)
            link(act.activation(wk(0)[0:SH, 0:T], wk(6)[0:SH, 0:T], ACT.Abs, bias=ST[0:SH, 26:27]))
            act.activation(wk(0)[0:SH, 0:T], wk(0)[0:SH, 0:T], ACT.Exp, scale=-1.0).then_inc(S("dt_exp"), 1)
            xin = wk(3)
            xin_p = xin[:, 0:HIST + LP]
            xin_s = xin[:, HIST + LP:HIST + LP + NB * (HIST + LS)].rearrange("p (b c) -> p b c", b=NB)
            b_tok = wk(2).rearrange("p (c n) -> p c n", c=TT + 1)
            read(act, "dtt")
            for t in range(CT):
                name = f"sx{t}"
                ready(act, name)
                if t:
                    act.wait_ge(S("sconv"), t)
                for g, (t0, n) in enumerate(GROUPS):
                    np_ = min(n, LP - t0)
                    act.activation(xin_p[:, HIST + t0:HIST + t0 + np_], pset(name)[:, g, 0:np_], ACT.Copy)
                freed(act.activation(xin_s[:, :, HIST:], pset(name)[:, 2, LP - 768:T - 768]
                                     .rearrange("p (b l) -> p b l", b=NB), ACT.Copy), name)
                act.wait_ge(S("sconv"), t + 1)
                act.activation(wk(5)[:, 0:T], wk(4)[:, 0:T], ACT.Tanh, scale=0.5).then_inc(S("s_th"), 1)
                if t < CT - 1:
                    name = f"st{t}"
                    ready(act, name)
                    if t < DT:
                        if t:
                            act.wait_ge(S("x_put"), 32 * t)
                        dst, scale = wk(6).rearrange("p (c n) -> p c n", c=TT + 1), 0.5
                    else:
                        dst, scale = b_tok, 1.0
                    act.activation(dst[:, 0:8].rearrange("p (a c) n -> p a (c n)", a=2), pset(name)[:, 0:2, :],
                                   ACT.Copy, scale=scale)
                    freed(act.activation(dst[0:TS, 8], pset(name)[0:TS, 2, 0:P], ACT.Copy, scale=scale), name)
                    if t < DT:
                        read(act, name)
                        act.dma_start(x_scr[0:LP, t * P:(t + 1) * P].rearrange("(c p) n -> p c n", p=P),
                                      dst[:, 0:8]).then_inc(S("x_put"), 16)
                        act.dma_start(x_scr[LP:T, t * P:(t + 1) * P], dst[0:TS, 8]).then_inc(S("x_put"), 16)
            act.wait_ge(S("x_put"), 32 * DT)
            act.wait_ge(S("s_act"), CT)
            ready(act, "qt")
            tails = WK[0:27, 5 * WT:5 * WT + SCC]
            act.activation(tails[:, 0:D], pset("qt")[0:27, 0:2].rearrange("p a c -> p (a c)"), ACT.Copy)
            freed(act.activation(tails[:, D:SCC], pset("qt")[0:27, 2, 0:SCC - D], ACT.Copy), "qt")
            read(act, "qt")
            store(O["p_ssd_conv"][0, 0], tails[0:3])
            store(O["s_ssd_conv"][0].rearrange("b k f -> (b k) f"), tails[3:27])
            act.wait_ge(stored, 16 * n_stores[0])
            za = WK[:, 3 * WT:3 * WT + 5 * 256].rearrange("p (c n) -> p c n", n=256)
            zb = wk(5, D).rearrange("p (c n) -> p c n", n=256)
            for z in range(4):
                cols = slice(z * 256, (z + 1) * 256)
                name = f"sza{z}"
                ready(act, name)
                if z:
                    act.wait_ge(S("za_put"), 16 * z)
                act.activation(za[:, 0:4].rearrange("p (a c) n -> p a (c n)", a=2), pset(name)[:, 0:2, :], ACT.Tanh,
                               scale=0.5)
                act.activation(za[:, 4], pset(name)[:, 2, 0:256], ACT.Tanh, scale=0.5).then_inc(S("z_th"), 1)
                name = f"szb{z}"
                ready(act, name)
                if z:
                    act.wait_ge(S("zb_put"), 32 * z)
                act.activation(zb[:, 0:2].rearrange("p c n -> p (c n)"), pset(name)[:, 0, :], ACT.Tanh, scale=0.5)
                act.activation(zb[:, 2], pset(name)[:, 1, 0:256], ACT.Tanh, scale=0.5)
                act.activation(zb[0:TS, 3], pset(name)[0:TS, 1, 256:512], ACT.Tanh, scale=0.5).then_inc(S("z_th"), 1)
                read(act, f"sza{z}")
                act.dma_start(z_scr[0:5 * P, cols].rearrange("(c p) n -> p c n", p=P), za).then_inc(S("za_put"), 16)
                read(act, name)
                act.dma_start(z_scr[5 * P:8 * P, cols].rearrange("(c p) n -> p c n", p=P), zb[:, 0:3])\
                    .then_inc(S("zb_put"), 16)
                act.dma_start(z_scr[LP:T, cols], zb[0:TS, 3]).then_inc(S("zb_put"), 16)
            act.wait_ge(S("za_put"), 64)
            act.wait_ge(S("zb_put"), 128)

            def load_z(q):
                c, g = divmod(q, 2)
                n = P if c < TT else TS
                act.dma_start(wk(4)[0:n, 0:512], z_scr[c * P:c * P + n, g * 512:(g + 1) * 512]).then_inc(S("z_in"), 16)

            def load_xs(c):
                n = P if c < TT else TS
                act.dma_start(wk(3)[0:n, 0:D], x_scr[c * P:c * P + n]).then_inc(S("xs_in"), 16)

            def state_in(b, slot):
                src = I["state_ssd_h"][0, b].rearrange("(g k h) p n -> g (h p) k n", g=2, k=4)
                dst = wk(0, 512, slot * 512).rearrange("p (k g n) -> p k g n", k=4, g=2)
                for g in range(2):
                    act.dma_start(dst[:, :, g], src[g]).then_inc(S(f"h_in{slot}"), 16)

            def state_out(dst, src, signal):
                d = dst.rearrange("(g k h) p n -> g (h p) k n", g=2, k=4)
                s = src.rearrange("p (k g n) -> p k g n", k=4, g=2)
                for g in range(2):
                    act.dma_start(d[g], s[:, :, g]).then_inc(signal, 16)
            load_z(0)
            load_xs(0)
            for c in range(TT + 1):
                n = P if c < TT else TS
                name = f"sc{c}"
                ready(act, name)
                act.activation(EC[0:n], pset(name)[0:n, 0, 0:32], ACT.Exp)
                m = 16 if c < TT else 128
                act.activation(EL[:, 0:m], pset(name)[:, 0, 32:32 + m], ACT.Exp).then_inc(S("sc_exp"), 1)
                if c == TT:
                    for b in range(2):
                        state_in(b, b)
                    ready(act, "po")
                    freed(act.activation(wk(2, 512), pset("po")[:, 0, :], ACT.Copy), "po")
                    read(act, "po")
                    n_stores[0] += 2
                    state_out(O["p_ssd_h"][0, 0], wk(2, 512), stored)
                    for b in range(NB):
                        name = f"si{b}"
                        ready(act, name)
                        if b + 2 < NB:
                            state_in(b + 2, b % 2)
                        if b >= 2:
                            act.wait_ge(S("si_mm"), b - 1)
                        freed(act.activation(wk(1, 512, b % 2 * 512), pset(name)[:, 0, :], ACT.Copy), name)
                    act.wait_ge(S("si_mm"), NB)
                    act.activation(YI[0][0:TS], PM[0:TS, 0, :], ACT.Copy)
                    act.activation(YI[1][0:TS], PM[0:TS, 1, :], ACT.Copy).then_inc(S("yi"), 1)
                    for b in range(2):
                        state_in(b, b)
                for g in range(2):
                    q = 2 * c + g
                    name = f"ss{c}_{g}"
                    ready(act, name)
                    for i in range(8 * n // 512):
                        ins = act.activation(wk(6)[0:n, i * 512:(i + 1) * 512], pset(name)[0:n, i, :], ACT.Exp)
                    freed(ins, name)
                    act.wait_ge(S("y_gated"), q + 1)
                    st = ST[0:n, 28 + q % 2:29 + q % 2]
                    link(act.activation(wk(4)[0:n, 0:512], wk(4)[0:n, 512:1024], ACT.Square, scale=0.5, accum_out=st))
                    act.activation(st, st, ACT.Sqrt, bias=EPSC[0:n], scale=1.0 / 512).then_inc(S("y_std"), 1)
                    if q + 1 < 2 * (TT + 1):
                        load_z(q + 1)
                    if g == 1 and c < TT:
                        act.wait_ge(S("x_used"), c + 1)
                        load_xs(c + 1)
                    read(act, f"sn{c}_{g}")
                    act.activation(Yh[:, 4 * g:4 * g + 4, c * P:c * P + n],
                                   wk(5, 4 * n).rearrange("p (k t) -> p k t", k=4), ACT.Copy).then_inc(S("sy_hi"), 1)
            for b in range(NB):
                name = f"ua{b}"
                ready(act, name)
                if b + 2 < NB:
                    state_in(b + 2, b % 2)
                if b >= 2:
                    read(act, f"ub{b - 2}")
                freed(act.activation(wk(1, 512, b % 2 * 512), pset(name)[:, 0, :], ACT.Copy), name)
                name = f"uc{b}"
                ready(act, name)
                if b >= 2:
                    act.wait_ge(S(f"h_put{b % 2}"), 32 * (b // 2))
                if b == 0:
                    act.wait_ge(S("sy_lo"), 2 * (TT + 1))
                    act.wait_ge(S("wx2"), 1)
                freed(act.activation(wk(4, 512, b % 2 * 512), pset(name)[:, 0, :], ACT.Copy), name)
                read(act, name)
                state_out(O["s_ssd_h"][0, b], wk(4, 512, b % 2 * 512), S(f"h_put{b % 2}"))
            for i in range(2):
                act.wait_ge(S(f"h_put{i}"), 32 * 4)
            act.wait_ge(stored, 16 * n_stores[0])
            out_jobs(2)
            if stop < 4:
                return
            for t in range(DT - 2, DT):
                sum_stored(act, 2, t)
            act.wait_ge(S("m_new2"), DT)
            for i in range(2):
                act.dma_start(WK[:, 4 * i * WT:4 * (i + 1) * WT].rearrange("p (k w) -> p k w", k=4)[:, :, 0:T],
                              merged[2, 4 * i:4 * i + 4].rearrange("k p t -> p k t")).then_inc(S(f"mi_in{i}"), 16)

            def load_xt(t):
                cols = slice(t * P, (t + 1) * P)
                act.dma_start(XT[:, t % 2, 0:TT], I["x_prompt"][0, :, cols].rearrange("(c p) f -> p c f", p=P))\
                    .then_inc(S(f"xt_in{t % 2}"), 16)
                act.dma_start(XT[0:TS, t % 2, TT], I["x_sample"].rearrange("b l f -> (b l) f")[:, cols])\
                    .then_inc(S(f"xt_in{t % 2}"), 16)
            load_xt(0)
            load_xt(1)
            for k in range(DT):
                act.wait_ge(S(f"mi_in{k // 4}"), 16)
                act.activation(Hh[:, k], wk(k)[:, 0:T], ACT.Copy).then_inc(S("mi_hi"), 1)
            for t in range(DT):
                all_groups(f"mx{t}", X[:, t], ACT.Copy)
                if t + 2 < DT:
                    load_xt(t + 2)
            act.wait_ge(S("mi_lo"), DT)

            def norm(i, name, split):
                for k in range(DT):
                    if i == 1:
                        read(act, f"xo{k}")
                    if k >= 2:
                        act.wait_ge(S("nrm_mm"), i * (DT - 1) + k - 1)
                    act.activation(wk(4 + k % 2)[:, 0:T], X[:, k], ACT.Square).then_inc(S("nrm_sq"), 1)
                ready(act, name)
                for g, (t0, n) in enumerate(GROUPS):
                    ins = act.activation(wk(6)[:, t0:t0 + n], pset(name)[:, g, 0:n], ACT.Sqrt, bias=EPSC[:],
                                         scale=1.0 / D)
                freed(ins, name)
                if split:
                    for k in range(DT):
                        act.wait_ge(S("nrm_t"), i * DT + k + 1)
                        act.activation(Hh[:, k], wk(4 + k % 2)[:, 0:T], ACT.Copy).then_inc(S("nrm_hi"), 1)
            act.dma_start(MV, I["mem_prompt"][0].rearrange("(m p) f -> p m f", p=P)).then_inc(S("mem_in"), 16)
            norm(0, "xn", True)
            act.wait_ge(S("mem_in"), 16)
            for i in range(2):
                link(act.activation(wk(0)[:, 0:D], MV[:, i], ACT.Square, accum_out=ST[:, 30 + i:31 + i]))
            act.activation(ST[:, 30:32], ST[:, 30:32], ACT.Sqrt, bias=EPSC[:], scale=1.0 / D).then_inc(S("mem_std"), 1)
            for i in range(2):
                read(act, f"mt{i}")
                act.activation(MNh[:, :, i * P:(i + 1) * P], wk(7, D).rearrange("p (k m) -> p k m", k=DT), ACT.Copy)\
                    .then_inc(S("mem_hi"), 1)
            for i in range(4):
                name = f"mk{i}"
                ready(act, name)
                freed(act.activation(KM[:, :, i * 256:(i + 1) * 256],
                                     pset(name)[:, 0, :].rearrange("p (m f) -> p m f", m=2), ACT.Copy), name)
            for i in range(4):
                read(act, f"mk{i}")
            store(O["p_mem_k"][0, 0].rearrange("(m p) h d -> p m (h d)", p=P), KM[:])
            for i in range(2):
                name = f"kt{i}"
                ready(act, name)
                freed(act.activation(KT_m[:, :, i * P:(i + 1) * P],
                                     pset(name)[:, 0:2, :].rearrange("p a (k m) -> p (a k) m", k=4), ACT.Copy), name)
            for i in range(4):
                name = f"mv{i}"
                ready(act, name)
                freed(act.activation(MV[:, :, i * 256:(i + 1) * 256],
                                     pset(name)[:, 0, :].rearrange("p (m f) -> p m f", m=2), ACT.Copy), name)
            for i in range(4):
                read(act, f"mv{i}")
            store(O["p_mem_v"][0, 0].rearrange("(m p) h d -> p m (h d)", p=P), MV)
            act.wait_ge(stored, 16 * n_stores[0])
            for t in range(DT):
                all_groups(f"xq{t}", Q[:, t], ACT.Copy)

            def probs(c):
                n = P if c < TT else TS
                name = f"xs{c}"
                act.wait_ge(S("x_max"), c + 1)
                if 2 <= c < TT:
                    ready(act, f"xp{c - 2}")
                for h in range(XH):
                    ins = act.activation(Pr(c)[0:n, h * M:(h + 1) * M], pset(name)[0:n, h // 2, h % 2 * M:(h % 2 + 1) * M],
                                         ACT.Exp, bias=ST[0:n, 32 + 4 * (c % 2) + h:33 + 4 * (c % 2) + h],
                                         scale=XD ** -0.5,
                                         accum_out=ST[0:n, 40 + 4 * (c % 2) + h:41 + 4 * (c % 2) + h])
                freed(ins, name)

            def outputs(c):
                n = P if c < TT else TS
                name = f"xp{c}"
                ready(act, name)
                if 2 <= c < TT:
                    ready(act, f"xv{c - 2}")
                for a in range(2):
                    ins = act.activation(PrT(c)[:, 4 * a:4 * a + 4, 0:n],
                                         pset(name)[:, a, :].rearrange("p (k t) -> p k t", k=4)[:, :, 0:n], ACT.Copy)
                freed(ins, name)
                if c == TT:
                    for b in range(NB):
                        if b >= 2:
                            act.wait_ge(S("vb"), b - 1)
                            load_kv(b, "v")
                name = f"xv{c}"
                ready(act, name)
                for a in range(2):
                    ins = act.activation(Hh[:, 4 * a:4 * a + 4, c * P:c * P + n],
                                         pset(name)[:, a, :].rearrange("p (k t) -> p k t", k=4)[:, :, 0:n], ACT.Copy)
                ins.then_inc(S("xo_hi"), 1)

            def load_kv(b, which):
                act.dma_start(KVb[b % 2], I[f"cache_mem_{which}"][0, b].rearrange("(m p) h d -> p m (h d)", p=P))\
                    .then_inc(S(f"kv_in{b % 2}"), 16)
            probs(0)
            for c in range(TT):
                if c + 1 < TT:
                    probs(c + 1)
                outputs(c)
            load_kv(0, "k")
            load_kv(1, "k")
            for s in range(4 * NB):
                act.wait_ge(S("kb_t"), s + 1)
                if s >= 4:
                    act.wait_ge(S("kb_s"), s - 3)
                act.activation(KTb[:, s % 4 * 2:s % 4 * 2 + 2].rearrange("p k m -> p (k m)"), PM[:, s % 2, :], ACT.Copy)\
                    .then_inc(S("kb_e"), 1)
                if s % 4 == 3:
                    b = s // 4
                    load_kv(b % 2 if b + 2 >= NB else b + 2, "v" if b + 2 >= NB else "k")
            probs(TT)
            outputs(TT)
            norm(1, "fn", True)
            for c in range(FC):
                for i in range(2):
                    q = 2 * c + i
                    name = f"fg{c}_{i}"
                    ready(act, name)
                    if q >= 4:
                        act.wait_ge(S("f_lo"), q - 3)
                    for g, (t0, n) in enumerate(GROUPS):
                        ins = act.activation(wk(q % 4)[:, t0:t0 + n], pset(name)[:, g, 0:n], ACT.Tanh, scale=0.5)
                    ins.then_inc(S("f_th"), 1)
                    read(act, f"fu{c}_{i}")
                    if q >= 4:
                        ready(act, f"fd{c - 2}_{DT - 1}")
                    act.activation(Fh[:, c % 2, i], wk(q % 4)[:, 0:T], ACT.Copy).then_inc(S("f_hi"), 1)
            for i in range(2):
                read(act, f"fd{FC - 1}_{DT - 1 - i}")
            norm(2, "yn", False)
            for c in range(TT + 1):
                n = P if c < TT else TS
                name = f"yt{c}"
                ready(act, name)
                if c >= 2:
                    act.wait_ge(S(f"out{c % 2}"), 16 * (c // 2))
                freed(act.activation(wk(c % 2)[0:n, 0:D], pset(name)[0:n, 0:2].rearrange("p a c -> p (a c)"), ACT.Copy), name)
                read(act, name)
                y = O["y_prompt"][0, c * P:c * P + n] if c < TT else O["y_sample"].rearrange("b l f -> (b l) f")
                act.dma_start(y, wk(c % 2)[0:n, 0:D]).then_inc(S(f"out{c % 2}"), 16)
            act.wait_ge(S("out0"), 16 * 5)
            act.wait_ge(S("out1"), 16 * 4)
            act.wait_ge(stored, 16 * n_stores[0])

        @block.vector
        def _(dve):
            chain = [0]

            def link(ins):
                chain[0] += 1
                ins.then_inc(dve_chain, 1)
                dve.wait_ge(dve_chain, chain[0])

            def stt(out, in0, scalar, in1, op0, op1):
                return dve.scalar_tensor_tensor(out=out, in0=in0, scalar=scalar, in1=in1, op0=op0, op1=op1)

            MUL, ADD, SUB = ALU.mult, ALU.add, ALU.subtract

            def out_jobs(b):
                for t in range(DT):
                    th = wk(t % 2)
                    read(dve, f"og{b}_{t}")
                    ready(dve, f"ob{b}_{t}")
                    for g, (t0, n) in enumerate(GROUPS):
                        ins = stt(th[:, t0:t0 + n], th[:, t0:t0 + n], 1.0, pset(f"ob{b}_{t}")[:, g, 0:n], ADD, MUL)
                    freed(ins, f"ob{b}_{t}")
                    read(dve, f"ob{b}_{t}")
                    if t >= 2:
                        sum_stored(dve, b, t - 2)
                    if b == 0:
                        dve.tensor_scalar(wk(4 + t % 2)[:, 0:T], th[:, 0:T], 0.5, None, MUL).then_inc(S(f"m_new{b}"), 1)
                    else:
                        dve.wait_ge(S(f"m_get{t % 2}"), 16 * ((b - 1) * DT // 2 + t // 2 + 1))
                        stt(wk(4 + t % 2)[:, 0:T], th[:, 0:T], 0.5, wk(2 + t % 2)[:, 0:T], MUL, ADD)\
                            .then_inc(S(f"m_new{b}"), 1)

            def conv(xin_p, xin_s, dst, taps, bias, hist, tail):
                link(dve.tensor_copy(xin_s[:, :, 0:HIST], hist))
                for out, src in ((dst[:, 0:LP], lambda k: xin_p[:, k:k + LP]),
                                 (seqs(dst), lambda k: xin_s[:, :, k:k + LS])):
                    link(dve.tensor_scalar(out, src(0), taps[0], bias, MUL, ADD))
                    for k in range(1, CW):
                        link(stt(out, src(k), taps[k], out, MUL, ADD))
                link(dve.tensor_copy(tail[:, 0:HIST], xin_p[:, LP:LP + HIST]))
                return dve.tensor_copy(tail[:, HIST:HIST + NB * HIST].rearrange("p (b k) -> p b k", b=NB),
                                       xin_s[:, :, LS:LS + HIST])

            dve.memset(EPSC[:], EPS).then_inc(S("eps"), 1)
            dve.memset(wk(0)[0:NROW, 0:D], 0.0).then_inc(packs_zero, 1)
            dve.memset(YA[:, DT:2 * DT, 0:2 * P], 0.0).then_inc(packs_zero, 1)
            ready(dve, "pk0")
            freed(dve.tensor_copy(PV[:], pset("pk0")[:, 0, 0:DT * NROW].rearrange("p (k r) -> p k r", k=DT)), "pk0")
            ready(dve, "pk1")
            freed(dve.tensor_copy(PQ[:], pset("pk1")[:, 0, 0:CT * QROW].rearrange("p (k r) -> p k r", k=CT)), "pk1")
            read(dve, "pk0")
            read(dve, "pk1")
            def lo_x(c):
                n = P if c < TT else TS
                dve.wait_ge(S("h_hi"), c + 1)
                dve.tensor_tensor(Hl[:, :, c * P:c * P + n], wk(7)[:, 0:DT * n].rearrange("p (k t) -> p k t", k=DT),
                                  Hh[:, :, c * P:c * P + n].bitcast(F32), SUB).then_inc(S("h_lo"), 1)
            for c in range(TT + 1):
                n = P if c < TT else TS
                dve.wait_ge(S("x_std"), c + 1)
                link(dve.reciprocal(ST[0:n, c:c + 1], ST[0:n, c:c + 1]))
                dve.tensor_scalar(wk(5 + c % 2)[0:n, 0:D], wk(3 + c % 2)[0:n, 0:D], ST[0:n, c:c + 1], None, MUL)\
                    .then_inc(S("x_scaled"), 1)
                if c:
                    lo_x(c - 1)
                    dve.wait_ge(S("h_lo"), c)
                ready(dve, f"xt{c}")
                for i in range(2):
                    ins = dve.tensor_tensor(
                        wk(7)[:, i * 4 * n:(i + 1) * 4 * n].rearrange("p (k t) -> p k t", k=4),
                        pset(f"xt{c}")[:, i].rearrange("p (k t) -> p k t", k=4)[:, :, 0:n],
                        PV[:, 4 * i:4 * i + 4, R_NMIX:R_NMIX + 1].broadcast_to([P, 4, n]), MUL)
                    if i == 0:
                        link(ins)
                freed(ins, f"xt{c}")
                read(dve, f"xt{c}")
            lo_x(TT)
            if stop < 1:
                return

            def atanh_of(e, s, s2, p):
                link(dve.tensor_scalar(s, e, 2.0, None, ADD))
                link(dve.reciprocal(s, s))
                link(dve.tensor_tensor(s, s, e, MUL))
                link(dve.tensor_tensor(s2, s, s, MUL))
                link(dve.tensor_scalar(p, s2, 1.0 / 15, None, MUL))
                for m in (13, 11, 9, 7, 5, 3):
                    link(stt(p, p, 1.0 / m, s2, ADD, MUL))
                link(stt(s, p, 1.0, s, ADD, MUL))

            dve.wait_ge(S("lam_exp"), 1)
            atanh_of(LAM[:, 0], LAM[:, 2], LAM[:, 3], NSC[:])
            link(stt(NSC[:], LAM[:, 2], 2.0, LAM[:, 1], MUL, ADD))
            link(dve.tensor_scalar(SC[:, :, 0], NSC[:], 4.0, None, MUL))
            link(dve.tensor_scalar(NSC[:], NSC[:], -4.0, None, MUL))
            dve.tensor_scalar(SC[:, :, 1:3], PV[:, :, R_BA:R_BX + 1], 0.5, None, MUL).then_inc(S("sc"), 1)
            xin = WK[:, 0:HIST + LP + NB * (HIST + LS)]
            xin_p = xin[:, 0:HIST + LP]
            xin_s = xin[:, HIST + LP:].rearrange("p (b c) -> p b c", b=NB)
            link(dve.memset(xin_p[:, 0:HIST], 0.0))
            xc, A, TZ, TI, G, GP, U = (wk(i)[:, 0:T] for i in range(1, 8))
            for t in range(DT):
                read(dve, f"lx{t}")
                conv(xin_p, xin_s, xc, [PV[:, t, R_CW + k:R_CW + k + 1] for k in range(CW)],
                     PV[:, t, R_CB:R_CB + 1], PV[:, t, R_CONV:R_CONV + NB * HIST].rearrange("p (b k) -> p b k", b=NB),
                     CB[:, t]).then_inc(S("conv"), 1)
                dve.wait_ge(S("g_sq"), t + 1)
                link(dve.tensor_scalar(GP, GP, 0.044715, 1.0, MUL, ADD))
                dve.tensor_tensor(GP, GP, G, MUL).then_inc(S("g_inner"), 1)
                dve.wait_ge(S("a"), t + 1)
                link(dve.tensor_tensor(U, A, A, MUL))
                stt(TZ, U, 1.0, TZ, ADD, MUL).then_inc(S("u_var"), 1)
                read(dve, f"li{t}")
                link(stt(TI, TI, 1.0, xc, ADD, MUL))
                dve.wait_ge(S("u_mult"), t + 1)
                link(dve.tensor_tensor(TI, TI, TZ, MUL))
                h0 = PV[:, t, R_H0:R_H0 + NB]
                link(dve.tensor_tensor(LAM[:, 0], seqs(A)[:, :, 0], h0, MUL))
                link(dve.tensor_tensor(seqs(TI)[:, :, 0], seqs(TI)[:, :, 0], LAM[:, 0], ADD))
                link(dve.memset(seqs(A)[:, :, 0:1], 0.0))
                link(dve.tensor_tensor_scan(U, A, TI, 0.0, MUL, ADD))
                dve.tensor_copy(CB[:, t, 27:28], U[:, LP - 1:LP])
                dve.tensor_copy(CB[:, t, 28:36], seqs(U)[:, :, LS - 1]).then_inc(S("cb"), 1)
                dve.wait_ge(S("g_tanh"), t + 1)
                link(stt(GP, GP, 1.0, G, ADD, MUL))
                stt(G, GP, 0.5, U, MUL, MUL).then_inc(S("y"), 1)
                dve.wait_ge(S("y"), t + 1)
                dve.wait_ge(S("y_hi"), t + 1)
                ins = dve.tensor_tensor(Yl[:, t], G, Yh[:, t].bitcast(F32), SUB)
                ins.then_inc(S("y_lo"), 1)
            out_jobs(0)
            if stop < 2:
                return
            V = WK[:, 6 * WT:8 * WT].rearrange("p (c v) -> p c v", c=TT + 1)
            KEt = wk(1).rearrange("p (c d) -> p c d", c=TT + 1)
            QT, KT = wk(3)[:, 0:T], wk(4)[:, 0:T]
            RS = [wk(2)[:, 0:T], wk(5)[:, 0:T]]
            RS2 = WK[:, 2 * WT:8 * WT].rearrange("p (a w) -> p a w", a=2)
            dve.tensor_scalar(LAM[:, 3, 0:GH], PV[:, 0:GH, R_GLA], -1.0, None, MUL).then_inc(S("nb"), 1)

            def chunks(ap, size):
                return ap.rearrange("p (a c) -> p a c", c=size)
            for h in range(GH):
                A = [YA[:, i] for i in (2 * h, 2 * h + 1, DT + 2 * h, DT + 2 * h + 1)]
                att = lambda c: A[1][:, c % 2 * P:c % 2 * P + P]
                on = lambda c: A[1][:, 256 + c % 2 * DV:256 + (c % 2 + 1) * DV]
                St = lambda c: A[2][:, c % 2 * DV:(c % 2 + 1) * DV]
                QZ = A[2][:, 512:1024].rearrange("p (b t) -> p b t", b=NB)
                KEm = A[0][0:TS, 0:D].rearrange("p (b d) -> p b d", b=NB)
                Sb = lambda b: A[3][:, b % 2 * DV:(b % 2 + 1) * DV]
                So = lambda b: A[3][:, 512 + b % 2 * DV:512 + (b % 2 + 1) * DV]
                dve.wait_ge(S("gl_ln"), h + 1)
                link(dve.tensor_tensor(A[0], A[0], A[1], ADD))
                dve.tensor_tensor_scan(A[1], rmask[:], A[0], 0.0, MUL, ADD).then_inc(S("gl_cum"), 1)
                dve.wait_ge(S("gl_cum"), h + 1)
                for src, dst, size in ((A[1][:, 0:LP], A[0][:, 0:LP], GCH), (A[1][:, LP:T], A[0][:, LP:T], LS)):
                    s3 = chunks(src, size)
                    ins = dve.tensor_tensor(chunks(dst, size), s3[:, :, size - 1:size]
                                            .broadcast_to(list(s3.shape)), s3, SUB)
                ins.then_inc(S("gl_d"), 1)
                dve.wait_ge(S("gl_exp"), h + 1)
                dve.tensor_copy(ST[:, 0:16], chunks(A[2][:, 0:LP], GCH)[:, :, GCH - 1])
                link(dve.tensor_copy(ST[:, 16:24], seqs(A[2])[:, :, LS - 1]))
                ready(dve, f"gq{h}")
                for g, (t0, n) in enumerate(GROUPS):
                    ins = stt(QT[:, t0:t0 + n], pset(f"gq{h}")[:, g, 0:n], DK ** -0.5, A[2][:, t0:t0 + n], MUL, MUL)
                freed(ins, f"gq{h}")
                read(dve, f"gq{h}")
                ready(dve, f"gk{h}")
                for g, (t0, n) in enumerate(GROUPS):
                    link(dve.tensor_tensor(KT[:, t0:t0 + n], pset(f"gk{h}")[:, g, 0:n], A[3][:, t0:t0 + n], MUL))
                dve.wait_ge(S("gl_ed"), h + 1)
                for g, (t0, n) in enumerate(GROUPS):
                    ins = dve.tensor_tensor(A[0][:, t0:t0 + n], pset(f"gk{h}")[:, g, 0:n], A[0][:, t0:t0 + n], MUL)
                    if g < 2:
                        link(ins)
                freed(ins, f"gk{h}")
                read(dve, f"gk{h}")
                dve.memset(St(0), 0.0).then_inc(S("ke"), 1)
                dve.wait_ge(S("ke"), h + 1)
                dve.tensor_tensor(QZ, mid(QT[:, LP:T], NB), seqm[:], MUL).then_inc(S("s_zero"), 1)
                for v in range(2):
                    name = f"gr{h}_{v}"
                    dve.wait_ge(S("gr_th"), 2 * h + v + 1)
                    for g, (t0, n) in enumerate(GROUPS):
                        ins = stt(RS[v][:, t0:t0 + n], RS[v][:, t0:t0 + n], 1.0, pset(name)[:, g, 0:n], ADD, MUL)
                    freed(ins, name)
                    read(dve, name)
                    link(dve.tensor_scalar(RS[v], RS[v], PV[:, 4 + v, R_GLA:R_GLA + 1], 0.5, MUL, MUL))
                read(dve, f"gt{h}")
                dve.tensor_tensor(KEm, mid(KEt[0:TS, 8], NB), bc(seqcol[:], DK), MUL).then_inc(S("kem"), 1)

                def gate_o(c):
                    n = P if c < TT else TS
                    q = h * (TT + 1) + c
                    dve.wait_ge(S("ot"), q + 1)
                    r = RS2[:, :, c * P:c * P + n]
                    dve.tensor_tensor(r, PM[:, 1, 0:256].rearrange("p (v t) -> p v t", v=2)[:, :, 0:n],
                                      r, MUL).then_inc(S("ymul"), 1)

                def update(e, part, b=None):
                    i = e - 24 * h
                    dve.wait_ge(S("ds"), e + 1)
                    new, old = (St(e + 1), St(e)) if b is None else (So(b), Sb(b))
                    stt(new, old, ST[:, i:i + 1], part, MUL, ADD)\
                        .then_inc(S("s_upd"), 1)
                    dve.wait_ge(S("s_upd"), e + 1)
                for c in range(TT + 1):
                    n = P if c < TT else TS
                    q = h * (TT + 1) + c
                    name = f"go{h}_{c}"
                    dve.wait_ge(S("att"), q + 1)
                    mask = m_ch if c < TT else s_le
                    dve.tensor_tensor(att(c)[0:n, 0:n], pset(name)[0:n, 1, 0:n], mask[:], MUL).then_inc(S("att_m"), 1)
                    if c < TT:
                        if c:
                            ready(dve, f"go{h}_{c - 1}")
                        update(24 * h + 2 * c, PM[:, 0, 0:256])
                        dve.wait_ge(S("inter"), h * TT + c + 1)
                        update(24 * h + 2 * c + 1, pset(name)[:, 2, 0:256])
                    else:
                        for b in range(NB):
                            dve.wait_ge(S(f"sb_in{b % 2}"), 16 * (h * 4 + b // 2 + 1))
                            if h * NB + b >= 2:
                                dve.wait_ge(S(f"sb_put{b % 2}"), 16 * (h * 4 + b // 2))
                            update(24 * h + 16 + b, PM[:, 0, 0:256] if b % 2 == 0 else pset(name)[:, 2, 0:256], b)
                    dve.wait_ge(S("g_std"), q + 1)
                    st = ST[0:n, 24 + q % 2:25 + q % 2]
                    link(dve.reciprocal(st, st))
                    freed(dve.tensor_scalar(on(c)[0:n], pset(name)[0:n, 0, 0:DV], st, None, MUL), name)
                    if c:
                        gate_o(c - 1)
                gate_o(TT)
                for v in range(2):
                    dve.wait_ge(S("gy_hi"), 2 * h + v + 1)
                    ins = dve.tensor_tensor(Yl[:, 2 * h + v], RS[v], Yh[:, 2 * h + v].bitcast(F32), SUB)
                ins.then_inc(S("gy_lo"), 1)
                dve.wait_ge(S("gy_lo"), h + 1)
            out_jobs(1)
            if stop < 3:
                return
            dve.wait_ge(S("dt_exp"), 1)
            tl = [wk(i)[0:SH, 0:T] for i in range(7)]
            atanh_of(tl[0], tl[2], tl[3], tl[4])
            link(stt(tl[5], tl[2], 2.0, tl[1], MUL, ADD))
            dve.tensor_scalar(tl[6], tl[5], ST[0:SH, 27:28], -1.0, MUL, MUL).then_inc(S("dt_done"), 1)
            ready(dve, "dtt")
            turned = pset("dtt")[:, 0, 0:288].rearrange("p (s c h) -> p s c h", s=2, c=TT + 1)
            dve.wait_ge(S("d_in"), 16)
            dve.tensor_copy(DTK[:, :, 0:TT, :], turned[:, :, 0:TT, :])
            freed(dve.tensor_copy(DTK[0:TS, :, TT, :], turned[0:TS, :, TT, :]), "dtt")
            xin = wk(3)
            xin_p = xin[:, 0:HIST + LP]
            xin_s = xin[:, HIST + LP:HIST + LP + NB * (HIST + LS)].rearrange("p (b c) -> p b c", b=NB)
            b_tok = wk(2).rearrange("p (c n) -> p c n", c=TT + 1)
            dve.wait_ge(S("dt_done"), 1)
            link(dve.memset(xin_p[:, 0:HIST], 0.0))
            for t in range(CT):
                read(dve, f"sx{t}")
                if 1 <= t <= DT:
                    ready(dve, f"st{t - 1}")
                conv(xin_p, xin_s, wk(4)[:, 0:T], [PQ[:, t, Q_CW + k:Q_CW + k + 1] for k in range(CW)],
                     PQ[:, t, Q_CB:Q_CB + 1], PQ[:, t, Q_CONV:Q_CONV + NB * HIST].rearrange("p (b k) -> p b k", b=NB),
                     CQ[:, t]).then_inc(S("sconv"), 1)
                dve.wait_ge(S("s_th"), t + 1)
                dve.wait_ge(S("sconv"), t + 1)
                ins = stt(wk(4)[:, 0:T], wk(5)[:, 0:T], 1.0, wk(4)[:, 0:T], ADD, MUL)
                if t >= DT:
                    link(ins)
                    ins = dve.tensor_scalar(wk(t - DT)[:, 0:T], wk(4)[:, 0:T], 0.5, None, MUL)
                ins.then_inc(S("s_act"), 1)
            za = WK[:, 3 * WT:3 * WT + 5 * 256].rearrange("p (c n) -> p c n", n=256)
            zb = wk(5, D).rearrange("p (c n) -> p c n", n=256)

            def gate(zt, src):
                return stt(zt, zt, 1.0, src, ADD, MUL)
            for z in range(4):
                name = f"sza{z}"
                dve.wait_ge(S("z_th"), 2 * z + 1)
                gate(za[:, 0:4].rearrange("p (a c) n -> p a (c n)", a=2), pset(name)[:, 0:2, :])
                freed(gate(za[:, 4], pset(name)[:, 2, 0:256]), name)
                name = f"szb{z}"
                dve.wait_ge(S("z_th"), 2 * z + 2)
                gate(zb[:, 0:2].rearrange("p c n -> p (c n)"), pset(name)[:, 0, :])
                gate(zb[:, 2], pset(name)[:, 1, 0:256])
                freed(gate(zb[0:TS, 3], pset(name)[0:TS, 1, 256:512]), name)
            link(dve.memset(H_ssd, 0.0))

            def heads(ap):
                return ap.rearrange("p (h d) -> p h d", d=HD)
            for c in range(TT + 1):
                n = P if c < TT else TS
                le = m_le if c < TT else s_le
                dt, da = DTK[0:n, 0, c, :], DTK[0:n, 1, c, :]
                if c == TT:
                    for b in range(NB):
                        ins = dve.tensor_scalar(DAB[0:n, b * SH:(b + 1) * SH], da, seqcol[:, b:b + 1], None, MUL)
                    ins.then_inc(S("dab"), 1)
                dve.wait_ge(S("sc_exp"), c + 1)
                dve.tensor_tensor(WJ[0:n], EC[0:n, 16:32], dt, MUL)
                for g in range(2):
                    ins = dve.tensor_tensor(CBM[0:n, g * P:g * P + n], pset(f"sc{c}")[0:n, 1 + g, 0:n], le[:], MUL)
                freed(ins, f"sc{c}")
                read(dve, f"sc{c}")
                dve.wait_ge(S("xs_in"), 16 * (c + 1))
                if c == TT:
                    dve.tensor_tensor(CZ, mid(wk(1)[:, LP:T], NB), seqm[:], MUL).then_inc(S("cz"), 1)
                    dve.wait_ge(S("yi"), 1)
                for g in range(2):
                    q = 2 * c + g
                    xg = heads(wk(3)[0:n, g * 512:(g + 1) * 512])
                    hs = slice(8 * g, 8 * g + 8)
                    R = wk(6)[0:n, 0:8 * n].rearrange("p (h i) -> p h i", h=8)
                    dve.tensor_tensor(R, bc(da[:, hs], n), mid(le[:], 8), MUL).then_inc(S("r"), 1)
                    dve.tensor_tensor(heads(wk(5)[0:n, 0:512]), xg, bc(dt[:, hs], HD), MUL)
                    dve.tensor_tensor(heads(wk(5)[0:n, 512:1024]), xg, bc(WJ[0:n, hs], HD), MUL)
                    read(dve, f"ss{c}_{g}")
                    dve.tensor_tensor(R, R, mid(CBM[0:n, g * P:g * P + n], 8), MUL).then_inc(S("m"), 1)
                    name = f"sy{c}_{g}"
                    ready(dve, name)
                    ps = pset(name)
                    y = wk(4)[0:n, 512:1024]
                    src = ps[0:n, 1, :] if c < TT else YI[g][0:n]
                    link(dve.tensor_tensor(heads(y), heads(src), bc(EC[0:n, hs], HD), MUL))
                    ins = dve.tensor_tensor(y, y, ps[0:n, 0, :], ADD)
                    if c < TT:
                        link(ins)
                    else:
                        freed(ins, name)
                        read(dve, name)
                    ins = dve.tensor_tensor(heads(wk(5)[0:n, 0:512]), xg, bc(DBC[0:n, hs], HD), MUL)
                    if g == 0:
                        link(ins)
                    else:
                        ins.then_inc(S("x_used"), 1)
                        dve.wait_ge(S("x_used"), c + 1)
                    link(dve.tensor_tensor(y, y, wk(5)[0:n, 0:512], ADD))
                    st = H_ssd[64 * g:64 * g + 64]
                    if c < TT:
                        link(dve.tensor_tensor(heads(st), heads(st), bc(EL[64 * g:64 * g + 64, hs], HD), MUL))
                        freed(dve.tensor_tensor(st, st, ps[64 * g:64 * g + 64, 2, :], ADD), name)
                    dve.wait_ge(S("z_in"), 16 * (q + 1))
                    dve.tensor_tensor(y, y, wk(4)[0:n, 0:512], MUL).then_inc(S("y_gated"), 1)
                    dve.wait_ge(S("y_std"), q + 1)
                    sc = ST[0:n, 28 + q % 2:29 + q % 2]
                    link(dve.reciprocal(sc, sc))
                    dve.tensor_scalar(y, y, sc, 0.5, MUL, MUL).then_inc(S("y_norm"), 1)
                    name = f"sn{c}_{g}"
                    ready(dve, name)
                    yt = wk(5, 4 * n).rearrange("p (k t) -> p k t", k=4)
                    freed(dve.tensor_tensor(yt, pset(name)[:, 0, :].rearrange("p (k t) -> p k t", k=4)[:, :, 0:n],
                                            PV[:, 4 * g:4 * g + 4, R_NSSD:R_NSSD + 1].broadcast_to([P, 4, n]), MUL),
                          name)
                    dve.wait_ge(S("sy_hi"), q + 1)
                    cols = slice(c * P, c * P + n)
                    dve.tensor_tensor(Yl[:, 4 * g:4 * g + 4, cols], yt, Yh[:, 4 * g:4 * g + 4, cols].bitcast(F32),
                                      SUB).then_inc(S("sy_lo"), 1)
                    dve.wait_ge(S("sy_lo"), q + 1)
            for g in range(2):
                ins = dve.tensor_tensor(heads(wk(5)[0:TS, g * 512:(g + 1) * 512]),
                                        heads(wk(3)[0:TS, g * 512:(g + 1) * 512]),
                                        bc(WJ[0:TS, 8 * g:8 * g + 8], HD), MUL)
            ins.then_inc(S("wx2"), 1)
            for b in range(NB):
                if b >= 2:
                    ready(dve, f"ub{b - 2}")
                dve.tensor_scalar(wk(5 + b % 2, P, D)[0:TS], b_tok[0:TS, TT, :], seqcol[:, b:b + 1], None, MUL)\
                    .then_inc(S("bm"), 1)
                read(dve, f"ua{b}")
                if b:
                    ready(dve, f"uc{b - 1}")
                for g in range(2):
                    r = slice(64 * g, 64 * g + 64)
                    link(dve.tensor_tensor(heads(wk(2, 512)[r]), heads(wk(1, 512, b % 2 * 512)[r]),
                                           bc(EL[r, b * SH + 8 * g:b * SH + 8 * g + 8], HD), MUL))
                ready(dve, f"ub{b}")
                freed(dve.tensor_tensor(wk(2, 512), wk(2, 512), pset(f"ub{b}")[:, 0, :], ADD), f"ub{b}")
            out_jobs(2)
            if stop < 4:
                return
            for k in range(DT):
                dve.wait_ge(S("mi_hi"), k + 1)
                dve.tensor_tensor(Hl[:, k], wk(k)[:, 0:T], Hh[:, k].bitcast(F32), SUB).then_inc(S("mi_lo"), 1)

            def norm(i, name, row, split):
                read(dve, name)
                link(dve.reciprocal(wk(6)[:, 0:T], wk(6)[:, 0:T]))
                for k in range(DT + 1):
                    if k < DT:
                        if split and k >= 2:
                            dve.wait_ge(S("nrm_lo"), i * DT + k - 1)
                        dst = wk(4 + k % 2)[:, 0:T] if split else X[:, k]
                        stt(dst, X[:, k], PV[:, k, row:row + 1], wk(6)[:, 0:T], MUL, MUL).then_inc(S("nrm_t"), 1)
                    if split and k:
                        dve.wait_ge(S("nrm_hi"), i * DT + k)
                        dve.tensor_tensor(Hl[:, k - 1], wk(4 + (k - 1) % 2)[:, 0:T], Hh[:, k - 1].bitcast(F32), SUB)\
                            .then_inc(S("nrm_lo"), 1)
            norm(0, "xn", R_NX, True)
            dve.wait_ge(S("mem_std"), 1)
            link(dve.reciprocal(ST[:, 30:32], ST[:, 30:32]))
            for i in range(2):
                dve.tensor_scalar(MV[:, i], MV[:, i], ST[:, 30 + i:31 + i], None, MUL).then_inc(S("mem_scaled"), 1)
            for i in range(2):
                name = f"mt{i}"
                ready(dve, name)
                if i:
                    dve.wait_ge(S("mem_lo"), i)
                for a in range(2):
                    ins = dve.tensor_tensor(wk(7, 512, a * 512).rearrange("p (k m) -> p k m", k=4),
                                            pset(name)[:, a, :].rearrange("p (k m) -> p k m", k=4),
                                            PV[:, 4 * a:4 * a + 4, R_NMEM:R_NMEM + 1].broadcast_to([P, 4, P]), MUL)
                    if a == 0:
                        link(ins)
                freed(ins, name)
                read(dve, name)
                dve.wait_ge(S("mem_hi"), i + 1)
                dve.tensor_tensor(MNl[:, :, i * P:(i + 1) * P], wk(7, D).rearrange("p (k m) -> p k m", k=DT),
                                  MNh[:, :, i * P:(i + 1) * P].bitcast(F32), SUB).then_inc(S("mem_lo"), 1)

            def maxima(c):
                n = P if c < TT else TS
                name = f"xs{c}"
                ready(dve, name)
                if c >= 2:
                    read(dve, f"xs{c - 2}")
                mx = ST[0:n, 32 + 4 * (c % 2):36 + 4 * (c % 2)]
                link(dve.tensor_reduce(mx, pset(name)[0:n, 0:2, :].rearrange("p a (h m) -> p (a h) m", h=2),
                                       AX_X, ALU.max))
                dve.tensor_scalar(mx, mx, -(XD ** -0.5), None, MUL).then_inc(S("x_max"), 1)

            def probs(c):
                n = P if c < TT else TS
                read(dve, f"xs{c}")
                sums = ST[0:n, 40 + 4 * (c % 2):44 + 4 * (c % 2)]
                link(dve.reciprocal(sums, sums))
                p = Pr(c)[0:n].rearrange("p (h m) -> p h m", h=XH)
                dve.tensor_tensor(p, p, bc(sums, M), MUL).then_inc(S("x_p"), 1)

            def outputs(c):
                n = P if c < TT else TS
                name = f"xv{c}"
                dve.wait_ge(S("xo_hi"), c + 1)
                for a in range(2):
                    cols = slice(c * P, c * P + n)
                    ins = dve.tensor_tensor(Hl[:, 4 * a:4 * a + 4, cols],
                                            pset(name)[:, a, :].rearrange("p (k t) -> p k t", k=4)[:, :, 0:n],
                                            Hh[:, 4 * a:4 * a + 4, cols].bitcast(F32), SUB)
                freed(ins, name)
            maxima(0)
            for c in range(TT):
                if c + 1 < TT:
                    maxima(c + 1)
                probs(c)
                outputs(c)
            link(dve.memset(WK[:, 6 * WT:6 * WT + 2 * DT * 120], 0.0))
            for b in range(NB):
                if b >= 2:
                    dve.wait_ge(S("kb_s"), 4 * (b - 1))
                dve.tensor_copy(QZb[:, b % 2, :, 56:56 + LS], Q[:, :, LP + LS * b:LP + LS * (b + 1)])\
                    .then_inc(S("qz"), 1)
            maxima(TT)
            probs(TT)
            outputs(TT)

            def add_to_x(name, t):
                ready(dve, name)
                for g, (t0, n) in enumerate(GROUPS):
                    ins = dve.tensor_tensor(X[:, t, t0:t0 + n], X[:, t, t0:t0 + n], pset(name)[:, g, 0:n], ADD)
                freed(ins, name)
            for t in range(DT):
                add_to_x(f"xo{t}", t)
            norm(1, "fn", R_NFFN, True)
            for c in range(FC + 1):
                for i in range(2 if c < FC else 0):
                    q = 2 * c + i
                    h = wk(q % 4)[:, 0:T]
                    dve.wait_ge(S("f_th"), q + 1)
                    name = f"fg{c}_{i}"
                    for g, (t0, n) in enumerate(GROUPS):
                        ins = stt(h[:, t0:t0 + n], h[:, t0:t0 + n], 1.0, pset(name)[:, g, 0:n], ADD, MUL)
                    freed(ins, name)
                    read(dve, name)
                    name = f"fu{c}_{i}"
                    ready(dve, name)
                    for g, (t0, n) in enumerate(GROUPS):
                        ins = stt(h[:, t0:t0 + n], h[:, t0:t0 + n], 0.5, pset(name)[:, g, 0:n], MUL, MUL)
                        if g < 2:
                            link(ins)
                    freed(ins, name)
                    read(dve, name)
                    dve.wait_ge(S("f_hi"), q + 1)
                    dve.tensor_tensor(Fl[:, c % 2, i], h, Fh[:, c % 2, i].bitcast(F32), SUB).then_inc(S("f_lo"), 1)
                if c:
                    for t in range(DT):
                        add_to_x(f"fd{c - 1}_{t}", t)
            norm(2, "yn", R_NFIN, False)


_OUTS = [("y_prompt", (1, LP, D)), ("y_sample", (NB, LS, D)), ("p_lru_h", (1, 1, D)), ("p_lru_conv", (1, 1, HIST, D)),
         ("p_gla_S", (1, 1, GH, DK, DV)), ("p_ssd_h", (1, 1, SH, HD, NS)), ("p_ssd_conv", (1, 1, HIST, SCC)),
         ("p_mem_k", (1, 1, M, XH, XD)), ("p_mem_v", (1, 1, M, XH, XD)), ("s_lru_h", (1, NB, D)),
         ("s_lru_conv", (1, NB, HIST, D)), ("s_gla_S", (1, NB, GH, DK, DV)), ("s_ssd_h", (1, NB, SH, HD, NS)),
         ("s_ssd_conv", (1, NB, HIST, SCC))]
_INS = ["x_prompt", "x_sample", "mem_prompt", "state_lru_h", "state_lru_conv", "state_gla_S", "state_ssd_h",
        "state_ssd_conv", "cache_mem_k", "cache_mem_v", "norm_mix", "w_in", "lru_conv_w", "lru_conv_b", "lru_wa",
        "lru_ba", "lru_wx", "lru_bx", "lru_lambda", "w_lru_out", "gla_w_alpha", "gla_b_alpha", "gla_norm",
        "w_gla_out", "ssd_conv_w", "ssd_conv_b", "ssd_dt_bias", "ssd_a_log", "ssd_d", "ssd_norm", "w_ssd_out",
        "w_mix_out", "norm_xattn", "norm_mem", "w_xq", "w_xk", "w_xv", "w_xo", "norm_ffn", "w_ffn_gate",
        "w_ffn_up", "w_ffn_down", "norm_final"]


def kernel(**inputs):
    import numpy as np
    import concourse.bacc as bacc
    from concourse.bass_utils import run_bass_kernel_spmd as run

    nc = bacc.Bacc("TRN2", target_bir_lowering=False, num_devices=1)
    arrays = {f"in_{name}": np.ascontiguousarray(inputs[name]) for name in _INS}
    ins = {name: nc.dram_tensor(f"in_{name}", arrays[f"in_{name}"].shape, F32, kind="ExternalInput").ap()
           for name in _INS}
    outs = {name: nc.dram_tensor(f"out_{name}", shape, F32, kind="ExternalOutput").ap() for name, shape in _OUTS}
    build(nc, ins, outs)
    r = run(nc, [arrays], core_ids=[0])
    return tuple(r.results[0][f"out_{name}"] for name, _ in _OUTS)
```

```python
from contextlib import ExitStack

import concourse.bass as bass
from concourse import mybir

F32 = mybir.dt.float32
F32R = mybir.dt.float32r
ALU = mybir.AluOpType
ACT = mybir.ActivationFunctionType
AX_X = mybir.AxisListType.X

P = 128
D = 1024
DT = D // P
LP = 1024
NB = 8
LS = 8
TS = NB * LS
T = LP + TS
TT = LP // P
GROUPS = [(0, 384), (384, 384), (768, 320)]
EPS = 1e-6
CW = 4
HIST = CW - 1
GH, DK, DV, GCH = 4, 128, 256, 64
SH, HD, NS = 16, 64, 64
SCC = D + 4 * NS
CT = SCC // P
M = 256
XH, XD = 4, 256
FF = 2816
FT = FF // P
FC = FT // 2
WT = 1152
GELU_C = 0.7978845608028654

C_LX, C_LG, C_Q, C_K, C_V, C_R, C_LOW = 0, 1024, 2048, 2560, 3072, 4096, 5120
C_Z, C_XBC, C_DT, C_GATE = 5136, 6160, 7440, 7456

R_CONV, R_H0, R_CW, R_CB, R_BA, R_BX, R_LAM = 0, 24, 32, 36, 37, 38, 39
R_NMIX, R_NX, R_NFFN, R_NFIN, R_NMEM, R_NSSD, R_GLA, NROW = 40, 41, 42, 43, 44, 45, 46, 47
Q_CONV, Q_CW, Q_CB, QROW = 0, 24, 28, 29


def plan():
    w, jobs = [], ["pk0", "pk1"] + [f"xt{c}" for c in range(TT + 1)]

    def use(tiles, *names):
        jobs.extend(names)
        w.extend((*tile, names[-1]) for tile in tiles)

    def out_jobs(b, name):
        for t in range(DT):
            use([("in", C_GATE + b * D + t * P)], f"og{b}_{t}")
            use([(name, t * P)], f"ob{b}_{t}")

    for t in range(DT):
        use([("in", C_LX + t * P)], f"lx{t}")
        use([("in", C_LG + t * P)], f"lg{t}")
        jobs.extend([f"lr{t}", f"li{t}"])
    jobs.append("lt")
    out_jobs(0, "lru_out")
    use([("in", C_LOW)], "low")
    use([("in", C_DT)], "dt")
    for h in range(GH):
        jobs.append(f"ga{h}")
        use([("in", C_Q + h * P)], f"gq{h}")
        use([("in", C_K + h * P)], f"gk{h}")
        use([("in", C_V + h * DV), ("in", C_V + h * DV + P)], f"gva{h}", f"gvb{h}")
        jobs.append(f"gt{h}")
        for v in range(2):
            use([("in", C_R + h * DV + v * P)], f"gr{h}_{v}")
        jobs.extend(f"go{h}_{c}" for c in range(TT + 1))
    out_jobs(1, "gla_out")
    jobs.append("dtt")
    for t in range(CT):
        use([("in", C_XBC + t * P)], f"sx{t}")
        if t < CT - 1:
            jobs.append(f"st{t}")
    jobs.append("qt")
    for z in range(4):
        use([("in", C_Z + 2 * z * P), ("in", C_Z + (2 * z + 1) * P)], f"sza{z}", f"szb{z}")
    jobs.append("ss0")
    for q in range(2 * TT):
        jobs.extend([f"sy{q}"] + ([f"ss{q + 1}"] if q + 1 < 2 * TT else []) + [f"sn{q}"])
    jobs.extend(["po", "si0"])
    for b in range(NB):
        jobs.extend([f"ub{b}"] + ([f"si{b + 1}"] if b + 1 < NB else []) + [f"uc{b}"])
    q = 2 * TT
    jobs.extend([f"ss{q}", f"sy{q}", f"ss{q + 1}", f"sn{q}", f"sy{q + 1}", f"sn{q + 1}"])
    out_jobs(2, "ssd_out")
    for t in range(DT):
        use([("mix", t * P)], f"mx{t}")
    jobs.extend(["xn", "mt0", "mt1"])
    for i in range(4):
        use([("xk", 2 * i * P), ("xk", (2 * i + 1) * P)], f"mk{i}")
    jobs.extend(["kt0", "kt1"])
    for i in range(4):
        use([("xv", 2 * i * P), ("xv", (2 * i + 1) * P)], f"mv{i}")
    for t in range(DT):
        use([("xq", t * P)], f"xq{t}")
    jobs.append("xs0")
    for c in range(TT + 1):
        if c + 1 < TT:
            jobs.append(f"xs{c + 1}")
        if c == TT:
            jobs.append(f"xs{c}")
        jobs.extend([f"xp{c}", f"xv{c}"])
    for t in range(DT):
        use([("xo", t * P)], f"xo{t}")
    jobs.append("fn")
    for c in range(FC + 1):
        for i in range(2 if c < FC else 0):
            use([("fg", (2 * c + i) * P)], f"fg{c}_{i}")
            use([("fu", (2 * c + i) * P)], f"fu{c}_{i}")
        for i in range(2 if c else 0):
            use([("fd", (c - 1, i))], *(f"fd{c - 1}_{t}" for t in range(4 * i, 4 * i + 4)))
    jobs.append("yn")
    jobs.extend(f"yt{c}" for c in range(TT + 1))
    return w, jobs


WLIST, JOBS = plan()
JOB = {name: n for n, name in enumerate(JOBS)}
FIRST_W = {}
for _n, _tile in enumerate(WLIST):
    FIRST_W.setdefault(_tile[:2], _n)


NW_AT = {0: 0, 1: 32, 2: 74, 3: 108, 4: 148}


def build(nc, ins, outs, stop=99):
    I, O = ins, outs
    ctx = ExitStack()
    with ctx:
        def sb(name, shape, dt=F32):
            return ctx.enter_context(nc.sbuf_tensor(name, shape, dt))

        def sem(name):
            return ctx.enter_context(nc.semaphore(name))

        base = -(-nc.sbuf_base // 32) * 32
        arena = sb("arena", [P, 4 * DT * T + 8])

        def at(name, shape, dt, offset):
            return nc.alloc_sbuf_tensor_at(name, shape, dt, offset=base + offset)

        HALF = 4 * DT * T
        Hh = at("Hh", [P, DT, T], F32R, 0)
        Hl = at("Hl", [P, DT, T], F32R, HALF)
        Yh = at("Yh", [P, DT, T], F32R, 2 * HALF)
        Yl = at("Yl", [P, DT, T], F32R, 3 * HALF)
        YA = at("YA", [P, 2 * DT, T], F32, 2 * HALF)
        X = at("X", [P, DT, T], F32, 2 * HALF)
        XT = at("XT", [P, 2, TT + 1, P], F32, 3 * HALF)
        MNh = at("MNh", [P, DT, M], F32R, 3 * HALF)
        MNl = at("MNl", [P, DT, M], F32R, 3 * HALF + 4 * DT * M)
        KM = at("KM", [P, 2, D], F32, 3 * HALF + 8 * DT * M)
        Q = at("Q", [P, DT, T], F32, 3 * HALF)
        Fh = at("Fh", [P, 2, 2, T], F32R, 3 * HALF)
        Fl = at("Fl", [P, 2, 2, T], F32R, 3 * HALF + 16 * T)
        Wr = sb("Wr", [P, 2, DT, P])
        Wh = sb("Wh", [P, 2, DT, P], F32R)
        Wl = sb("Wl", [P, 2, DT, P], F32R)
        WK = sb("WK", [P, 8 * WT])
        ident = sb("ident", [P, P])
        ones = sb("ones", [P, P])
        m_le = sb("m_le", [P, P])
        m_gt = sb("m_gt", [P, P])
        m_ch = sb("m_ch", [P, P])
        s_le = sb("s_le", [TS, TS])
        s_gt = sb("s_gt", [TS, TS])
        seqcol = sb("seqcol", [TS, NB])
        seqm = sb("seqm", [P, NB, TS], mybir.dt.bfloat16)
        YT = sb("YT", [P, T // 2])
        rmask = YT[:].bitcast(mybir.dt.bfloat16)
        PV = sb("PV", [P, DT, NROW])
        PQ = sb("PQ", [P, CT, QROW])
        SC = sb("SC", [P, DT, 3])
        CB = sb("CB", [P, DT, 36])
        CQ = sb("CQ", [P, CT, 27])
        NSC = sb("NSC", [P, DT])
        LAM = sb("LAM", [P, 4, DT])
        EPSC = sb("EPSC", [P, 1])
        ST = sb("ST", [P, 48])

        def wk(i, n=WT, off=0):
            return WK[:, i * WT + off:i * WT + off + n]

        PS = ctx.enter_context(nc.psum_tensor("PS", [P, 2, 3, 512], F32))
        PM = ctx.enter_context(nc.psum_tensor("PM", [P, 2, 512], F32))

        DTK = wk(7, 288).rearrange("p (s c h) -> p s c h", s=2, c=TT + 1)
        H_ssd = wk(7, 512, 288)
        CBM = wk(7, 256, 800)
        DBC = wk(7, SH, 1056)
        DAB = wk(6, 128, D)
        CZ = wk(6, 512).rearrange("p (b t) -> p b t", b=NB)
        YI = [wk(7, 512, 288), wk(0, 512)]
        Yhf = at("Yhf", [P, DT, T], F32, 2 * HALF)
        Ylf = at("Ylf", [P, DT, T], F32, 3 * HALF)

        def EC(c):
            return wk(4, 32, D + 48 * (c % 2))

        def WJ(c):
            return wk(4, 16, D + 48 * (c % 2) + 32)

        def EL(c):
            return wk(4, 16, D + 96 + 16 * (c % 2)) if c < TT else wk(3, 128, D)

        def RM(q):
            c, g = divmod(q, 2)
            n = P if c < TT else TS
            if g == 0:
                return Ylf[0:n, :, c * P:c * P + n]
            return wk(6)[0:n, 0:8 * n].rearrange("p (h i) -> p h i", h=8)

        def pairs(ap):
            return ap.rearrange("p (k a d) -> p k a d", k=4, a=2)

        def XDT(q):
            c, g = divmod(q, 2)
            if g == 0 and c < TT:
                return Yhf[:, 0:4, c * P:(c + 1) * P].rearrange("p k (a d) -> p k a d", a=2)
            if g == 0:
                return Yhf[0:TS, :, LP:T].rearrange("p (k a) d -> p k a d", a=2)
            return pairs(wk(5, 512)) if c < TT else pairs(wk(1, 512)[0:TS])

        def XW(q):
            c, g = divmod(q, 2)
            if g == 0:
                return Yhf[:, 4:8, c * P:(c + 1) * P]
            return wk(5, 512, 512).rearrange("p (k w) -> p k w", k=4)

        MV = WK[:, 2 * WT:2 * WT + 2 * D].rearrange("p (m f) -> p m f", m=2)
        KT_m = WK[:, 0:DT * M].rearrange("p (k m) -> p k m", k=DT)
        KVb = [WK[:, i * 2 * WT:i * 2 * WT + 2 * D].rearrange("p (m f) -> p m f", m=2) for i in range(2)]
        KTb = WK[:, 4 * WT:4 * WT + DT * M].rearrange("p (k m) -> p k m", k=DT)
        QZb = WK[:, 6 * WT:6 * WT + 2 * DT * 120].rearrange("p (a k t) -> p a k t", a=2, k=DT)

        def Pr(c):
            return wk(4 + c % 2 if c < TT else 6, D)

        def PrT(c):
            return wk(6 + c % 2 if c < TT else 7, D).rearrange("p (k t) -> p k t", k=DT)

        merged = nc.dram_tensor("merged", (3, DT, P, T), F32, kind="Internal").ap()
        dt_scr = nc.dram_tensor("dt_scr", (SH, T), F32, kind="Internal").ap()
        x_scr = nc.dram_tensor("x_scr", ((TT + 1) * P, D), F32, kind="Internal").ap()
        z_scr = nc.dram_tensor("z_scr", ((TT + 1) * P, D), F32, kind="Internal").ap()

        ps_ready = [sem("ps_ready0"), sem("ps_ready1")]
        ps_free = [sem("ps_free0"), sem("ps_free1")]
        w_loaded = [sem("w_loaded0"), sem("w_loaded1")]
        w_split = sem("w_split")
        w_hi = sem("w_hi")
        masks = sem("masks")
        act_chain = sem("act_chain")
        dve_chain = sem("dve_chain")
        packs = sem("packs")
        packs_zero = sem("packs_zero")
        stored = sem("stored")
        pack_cols = sem("pack_cols")
        NMASK = 25
        NPACK = 18
        NW = NW_AT[stop] if stop in NW_AT else len(WLIST)

        def ready(eng, name):
            n = JOB[name]
            eng.wait_ge(ps_ready[n % 2], n // 2 + 1)

        def read(eng, name):
            n = JOB[name]
            eng.wait_ge(ps_free[n % 2], n // 2 + 1)

        def free_set(eng, name):
            n = JOB[name]
            if n >= 2:
                eng.wait_ge(ps_free[n % 2], n // 2)

        def branch_done(eng, b):
            if b == 0:
                eng.wait_ge(S("y_lo"), DT)
            elif b == 1:
                eng.wait_ge(S("gy_lo"), GH)
            else:
                eng.wait_ge(S("sy_lo"), 2 * (TT + 1))

        def sum_stored(eng, b, t):
            eng.wait_ge(S(f"m_put{t % 2}"), 16 * (b * DT // 2 + t // 2 + 1))

        def pset(name):
            return PS[:, JOB[name] % 2]

        def done(ins, name):
            ins.then_inc(ps_ready[JOB[name] % 2], 1)

        def freed(ins, name):
            ins.then_inc(ps_free[JOB[name] % 2], 1)

        n_stores = [0]
        sems = {}

        def S(name):
            if name not in sems:
                sems[name] = sem(name)
            return sems[name]

        def seqs(ap):
            return ap[:, LP:T].rearrange("p (b l) -> p b l", b=NB)

        def bc(ap, n):
            return ap.unsqueeze(2).broadcast_to([ap.shape[0], ap.shape[1], n])

        def mid(ap, n):
            return ap.unsqueeze(1).broadcast_to([ap.shape[0], n, ap.shape[1]])

        block = ctx.enter_context(nc.Block())

        @block.sync
        def _(sp):
            src = {"in": "w_in", "lru_out": "w_lru_out", "gla_out": "w_gla_out", "ssd_out": "w_ssd_out",
                   "mix": "w_mix_out", "xk": "w_xk", "xv": "w_xv", "xq": "w_xq", "xo": "w_xo",
                   "fg": "w_ffn_gate", "fu": "w_ffn_up"}
            for n, (kind, col, _) in enumerate(WLIST[:NW]):
                if n >= 2:
                    sp.wait_ge(w_split, n - 1)
                if kind == "fd":
                    c, half = col
                    tile = I["w_ffn_down"][0, 2 * c * P:(2 * c + 2) * P, half * 512:half * 512 + 512]
                    dst = Wr[:, n % 2].rearrange("p (k a) m -> p k (a m)", k=2)
                    sp.dma_start(dst, tile.rearrange("(k p) m -> p k m", p=P)).then_inc(w_loaded[n % 2], 16)
                else:
                    tile = I[src[kind]][0, :, col:col + P]
                    sp.dma_start(Wr[:, n % 2], tile.rearrange("(k p) m -> p k m", p=P)).then_inc(w_loaded[n % 2], 16)

        @block.gpsimd
        def _(pool):
            chain = [0]

            def link(ins):
                chain[0] += 1
                ins.then_inc(masks, 1)
                pool.wait_ge(masks, chain[0])

            def select(tile, compare, pattern, base, cm, fill=0.0):
                link(pool.affine_select(out=tile, in_=tile, pattern=pattern, compare_op=compare, fill=fill,
                                        base=base, channel_multiplier=cm))

            GE = ALU.is_ge
            link(pool.memset(ident[:], 0.0))
            select(ident[:], ALU.not_equal, [[-1, P]], 0, 1, 1.0)
            for tile in (ones, m_le, m_gt, m_ch, s_le, s_gt, seqcol, seqm):
                link(pool.memset(tile[:], 1.0))
            link(pool.memset(rmask, 1.0))
            select(m_le[:], GE, [[1, P]], 0, -1)
            select(m_gt[:], GE, [[-1, P]], -1, 1)
            select(m_ch[:], GE, [[1, P]], 0, -1)
            ch = m_ch[:].rearrange("p (a c) -> p a c", a=2)
            select(ch, GE, [[-GCH, 2], [0, GCH]], 0, 1)
            sl = s_le[:].rearrange("p (b c) -> p b c", b=NB)
            select(sl, GE, [[LS, NB], [1, LS]], 0, -1)
            select(sl, GE, [[-LS, NB], [0, LS]], 0, 1)
            sg = s_gt[:].rearrange("p (b c) -> p b c", b=NB)
            select(sg, GE, [[-LS, NB], [-1, LS]], -1, 1)
            select(sg, GE, [[LS, NB], [0, LS]], LS - 1, -1)
            select(seqcol[:], GE, [[-LS, NB]], 0, 1)
            select(seqcol[:], GE, [[LS, NB]], LS - 1, -1)
            select(seqm[:], GE, [[-LS, NB], [1, TS]], 0, 0)
            select(seqm[:], GE, [[LS, NB], [-1, TS]], LS - 1, 0)
            link(pool.memset(rmask[:, 0:LP].rearrange("p (a c) -> p a c", c=GCH)[:, :, 0:1], 0.0))
            link(pool.memset(seqs(rmask)[:, :, 0:1], 0.0))
            assert chain[0] == NMASK, chain[0]
            splits = [0]

            def split_to(end):
                for n in range(splits[0], min(end, NW)):
                    pool.wait_ge(w_loaded[n % 2], 16 * (n // 2 + 1))
                    if n >= 2:
                        ready(pool, WLIST[n - 2][2])
                    pool.tensor_copy(Wh[:, n % 2], Wr[:, n % 2]).then_inc(w_hi, 1)
                    pool.wait_ge(w_hi, n + 1)
                    pool.tensor_tensor(Wl[:, n % 2], Wr[:, n % 2], Wh[:, n % 2].bitcast(F32),
                                       ALU.subtract).then_inc(w_split, 1)
                splits[0] = max(splits[0], end)

            split_to(FIRST_W["in", C_Z + 7 * P] + 3)

            def weight_x(q, part=None):
                c, g = divmod(q, 2)
                n = P if c < TT else TS
                dt = DTK[0:n, 0, c, :]
                x = pairs(wk(3)[0:n, g * 512:(g + 1) * 512])

                def per_head(ap):
                    ap = ap[0:n, 8 * g:8 * g + 8].rearrange("p (k a) -> p k a", a=2)
                    return ap.unsqueeze(3).broadcast_to([n, 4, 2, HD])
                if part != "skip":
                    pool.wait_ge(S(f"xs_in{g}"), 16 * (c + 1))
                    pool.wait_ge(S("wj"), c + 1)
                if part != "skip" and c < TT:
                    if q >= 2:
                        ready(pool, f"sy{q - 2}")
                    pool.tensor_tensor(XW(q).rearrange("p k (a d) -> p k a d", a=2), x, per_head(WJ(c)), ALU.mult)
                elif part != "skip":
                    dst = pairs(wk(5)[0:TS, g * 512:(g + 1) * 512])
                    pool.tensor_tensor(dst, x, per_head(WJ(c)), ALU.mult).then_inc(S("wx2"), 1)
                if part != "state":
                    pool.tensor_tensor(XDT(q), x, per_head(dt), ALU.mult).then_inc(S("xdt"), 1)
                    pool.wait_ge(S("xdt"), q + 1)
                    pool.tensor_tensor(x, x, per_head(DBC), ALU.mult).then_inc(S("xd"), 1)

            weight_x(0)
            weight_x(1)
            for q in range(2, 2 * TT):
                weight_x(q)
            q = 2 * TT
            ready(pool, f"sy{q - 1}")
            weight_x(q, "state")
            weight_x(q + 1, "state")
            pool.wait_ge(S("wx2"), 2)
            weight_x(q, "skip")
            pool.wait_ge(S("si_mm"), NB)
            read(pool, f"ub{NB - 1}")
            weight_x(q + 1, "skip")
            split_to(NW)

        @block.tensor
        def _(pe):
            def project(name, w, Rh, Rl, by_tile=None, last=True):
                pe.wait_ge(w_split, w + 1)
                free_set(pe, name)
                for k in range(DT):
                    if by_tile:
                        pe.wait_ge(S(by_tile), k + 1)
                    for i, (L, R) in enumerate(((Wh, Rh), (Wh, Rl), (Wl, Rh))):
                        for g, (t0, n) in enumerate(GROUPS):
                            mm = pe.matmul(pset(name)[:, g, 0:n], L[:, w % 2, k, :], R[:, k, t0:t0 + n],
                                           start=(k == 0 and i == 0), stop=(last and k == DT - 1 and i == 2),
                                           skip_group_check=not last)
                return mm

            def project_tokens(name, w, tiles, Ah=Hh, Al=Hl):
                pe.wait_ge(w_split, w + 2)
                free_set(pe, name)
                for j, c in enumerate(tiles):
                    n = P if c < TT else TS
                    for k in range(DT):
                        for i, (A, W) in enumerate(((Ah, Wh), (Al, Wh), (Ah, Wl))):
                            mm = pe.matmul(pset(name)[0:n, j // 2, (j % 2) * 256:(j % 2) * 256 + 256]
                                           .rearrange("p (a m) -> p a m", a=2),
                                           A[:, k, c * P:c * P + n], W[:, :, k, :],
                                           start=(k == 0 and i == 0), stop=(k == DT - 1 and i == 2))
                return mm

            def turn(out, in_, n):
                return pe.transpose(out, in_, ident[0:n, 0:n])

            def fp32_all(name, lhsT, rhs):
                for g, (t0, n) in enumerate(GROUPS):
                    mm = pe.matmul(pset(name)[:, g, 0:n], lhsT, rhs[:, t0:t0 + n], start=True, stop=True)
                return mm

            def out_jobs(b, kind):
                for t in range(DT):
                    done(project(f"og{b}_{t}", FIRST_W["in", C_GATE + b * D + t * P], Hh, Hl), f"og{b}_{t}")
                    if t == 0:
                        branch_done(pe, b)
                    done(project(f"ob{b}_{t}", FIRST_W[kind, t * P], Yh, Yl), f"ob{b}_{t}")

            pe.wait_ge(masks, NMASK)
            pe.wait_ge(packs, 16 * NPACK)
            for k in range(DT):
                mm = turn(pset("pk0")[:, 0, k * NROW:(k + 1) * NROW], wk(0)[0:NROW, k * P:(k + 1) * P], NROW)
            done(mm, "pk0")
            for k in range(CT):
                mm = turn(pset("pk1")[:, 0, k * QROW:(k + 1) * QROW], WK[0:QROW, WT + k * P:WT + (k + 1) * P], QROW)
            done(mm, "pk1")
            for c in range(TT + 1):
                n = P if c < TT else TS
                pe.wait_ge(S("x_scaled"), c + 1)
                free_set(pe, f"xt{c}")
                for k in range(DT):
                    mm = turn(pset(f"xt{c}")[:, k // 4, (k % 4) * P:(k % 4) * P + n],
                              wk(5 + c % 2)[0:n, k * P:(k + 1) * P], n)
                done(mm, f"xt{c}")
            if stop < 1:
                return
            pe.wait_ge(S("h_lo"), TT + 1)
            for t in range(DT):
                done(project(f"lx{t}", FIRST_W["in", C_LX + t * P], Hh, Hl), f"lx{t}")
                done(project(f"lg{t}", FIRST_W["in", C_LG + t * P], Hh, Hl), f"lg{t}")
                if t == 0:
                    pe.wait_ge(S("wax"), 64)
                pe.wait_ge(S("conv"), t + 1)
                for name, off in ((f"lr{t}", 0), (f"li{t}", P)):
                    free_set(pe, name)
                    done(fp32_all(name, YA[:, DT + t, off:off + P], wk(1)), name)
            pe.wait_ge(S("cb"), DT)
            free_set(pe, "lt")
            for k in range(DT):
                mm = turn(pset("lt")[0:36, k // 4, (k % 4) * P:(k % 4 + 1) * P], CB[:, k, :], P)
            done(mm, "lt")
            out_jobs(0, "lru_out")
            if stop < 2:
                return
            V = WK[:, 6 * WT:8 * WT].rearrange("p (c v) -> p c v", c=TT + 1)
            KEt = wk(1).rearrange("p (c d) -> p c d", c=TT + 1)
            QT, KT = wk(3)[:, 0:T], wk(4)[:, 0:T]
            done(project("low", FIRST_W["in", C_LOW], Hh, Hl), "low")
            done(project("dt", FIRST_W["in", C_DT], Hh, Hl), "dt")
            for h in range(GH):
                A = [YA[:, i] for i in (2 * h, 2 * h + 1, DT + 2 * h, DT + 2 * h + 1)]
                name = f"ga{h}"
                read(pe, "low")
                pe.wait_ge(S(f"wal{h % 2}"), 16 * (h // 2 + 1))
                free_set(pe, name)
                done(fp32_all(name, CB[0:16].rearrange("p k c -> p (k c)")[:, h % 2 * P:h % 2 * P + P],
                              wk(0)[0:16]), name)
                done(project(f"gq{h}", FIRST_W["in", C_Q + h * P], Hh, Hl), f"gq{h}")
                done(project(f"gk{h}", FIRST_W["in", C_K + h * P], Hh, Hl), f"gk{h}")
                wv = FIRST_W["in", C_V + h * DV]
                done(project_tokens(f"gva{h}", wv, range(0, 5)), f"gva{h}")
                done(project_tokens(f"gvb{h}", wv, range(5, TT + 1)), f"gvb{h}")
                name = f"gt{h}"
                pe.wait_ge(S("ke"), h + 1)
                free_set(pe, name)
                for c in range(TT + 1):
                    n = P if c < TT else TS
                    mm = turn(pset(name)[0:n, c // 4, (c % 4) * P:(c % 4 + 1) * P], A[0][:, c * P:c * P + n], P)
                done(mm, name)
                for v in range(2):
                    done(project(f"gr{h}_{v}", FIRST_W["in", C_R + h * DV + v * P], Hh, Hl), f"gr{h}_{v}")
                att = lambda c: A[1][:, c % 2 * P:c % 2 * P + P]
                on = lambda c: A[1][:, 256 + c % 2 * DV:256 + (c % 2 + 1) * DV]
                St = lambda c: A[2][:, c % 2 * DV:(c % 2 + 1) * DV]
                QZ = A[2][:, 512:1024].rearrange("p (b t) -> p b t", b=NB)
                KEm = A[0][0:TS, 0:D].rearrange("p (b d) -> p b d", b=NB)
                Sb = lambda b: A[3][:, b % 2 * DV:(b % 2 + 1) * DV]

                def turn_o(c):
                    n = P if c < TT else TS
                    q = h * (TT + 1) + c
                    read(pe, f"go{h}_{c}")
                    if q:
                        pe.wait_ge(S("ymul"), q)
                    for v in range(2):
                        mm = turn(PM[:, 1, v * P:v * P + n],
                                  on(c)[0:n, v * P:(v + 1) * P], n)
                    mm.then_inc(S("ot"), 1)
                read(pe, f"gt{h}")
                read(pe, f"gvb{h}")
                for c in range(TT + 1):
                    n = P if c < TT else TS
                    name = f"go{h}_{c}"
                    q = h * (TT + 1) + c
                    free_set(pe, name)
                    cols = slice(c * P, c * P + n)
                    pe.matmul(pset(name)[0:n, 1, 0:n], KT[:, cols], QT[:, cols], start=True, stop=True)\
                        .then_inc(S("att"), 1)
                    if c < TT:
                        for i in range(2):
                            e = h * 24 + 2 * c + i
                            if i == 0 and e >= 2:
                                pe.wait_ge(S("s_upd"), e - 1)
                            pe.matmul(PM[:, 0, 0:256] if i == 0 else pset(name)[:, 2, 0:256],
                                      KEt[64 * i:64 * i + 64, c, :], V[64 * i:64 * i + 64, c, :],
                                      start=True, stop=True).then_inc(S("ds"), 1)
                        pe.wait_ge(S("att_m"), q + 1)
                        pe.matmul(pset(name)[:, 0, 0:DV], att(c), V[:, c, :], start=True, stop=False,
                                  skip_group_check=True)
                        for i in range(2):
                            e = h * 24 + 2 * c + i
                            if c == 0 and i == 0:
                                pe.wait_ge(S("s_zero"), h + 1)
                            else:
                                pe.wait_ge(S("s_upd"), e)
                            mm = pe.matmul(pset(name)[64 * i:64 * i + 64, 0, 0:DV],
                                           QT[:, c * P + 64 * i:c * P + 64 * i + 64], St(e),
                                           start=False, stop=True, skip_group_check=True)
                            if i == 0:
                                mm.then_inc(S("inter"), 1)
                    else:
                        pe.wait_ge(S("att_m"), q + 1)
                        pe.matmul(pset(name)[0:n, 0, 0:DV], att(c)[0:n, 0:n], V[0:n, c, :], start=True, stop=False,
                                  skip_group_check=True)
                        pe.wait_ge(S("kem"), h + 1)
                        for b in range(NB):
                            e = h * 24 + 16 + b
                            pe.wait_ge(S("s_upd"), e - 1)
                            pe.matmul(PM[:, 0, 0:256] if b % 2 == 0 else pset(name)[:, 2, 0:256], KEm[:, b, :], V[0:TS, c, :],
                                      start=True, stop=True).then_inc(S("ds"), 1)
                            pe.wait_ge(S(f"sb_in{b % 2}"), 16 * (h * 4 + b // 2 + 1))
                            mm = pe.matmul(pset(name)[0:n, 0, 0:DV], QZ[:, b, :], Sb(b), start=False,
                                           stop=(b == NB - 1), skip_group_check=True)
                            if b < NB - 1:
                                mm.then_inc(S("sb_int"), 1)
                    done(mm, name)
                    if c:
                        turn_o(c - 1)
                turn_o(TT)
            out_jobs(1, "gla_out")
            if stop < 3:
                return
            bT, cT = wk(0), wk(1)
            b_tok = wk(2).rearrange("p (c n) -> p c n", c=TT + 1)
            pe.wait_ge(S("dt_done"), 1)
            free_set(pe, "dtt")
            for s, src in enumerate((5, 6)):
                for c in range(TT + 1):
                    n = P if c < TT else TS
                    o = (s * (TT + 1) + c) * SH
                    mm = turn(pset("dtt")[0:n, 0, o:o + SH], wk(src)[0:SH, c * P:c * P + n], SH)
            done(mm, "dtt")

            def turn_channels(t):
                name = f"st{t}"
                pe.wait_ge(S("s_act"), t + 1)
                free_set(pe, name)
                src = wk(4) if t < DT else bT
                for c in range(TT + 1):
                    n = P if c < TT else TS
                    mm = turn(pset(name)[0:n, c // 4, (c % 4) * P:(c % 4 + 1) * P], src[:, c * P:c * P + n], P)
                done(mm, name)
            for t in range(CT):
                done(project(f"sx{t}", FIRST_W["in", C_XBC + t * P], Hh, Hl), f"sx{t}")
                if t < CT - 1:
                    turn_channels(t)
            free_set(pe, "qt")
            pe.wait_ge(S("sconv"), CT)
            for k in range(CT):
                mm = turn(pset("qt")[0:27, k // 4, (k % 4) * P:(k % 4 + 1) * P], CQ[:, k, :], P)
            done(mm, "qt")
            for z in range(4):
                wz = FIRST_W["in", C_Z + 2 * z * P]
                done(project_tokens(f"sza{z}", wz, range(0, 5)), f"sza{z}")
                done(project_tokens(f"szb{z}", wz, range(5, TT + 1)), f"szb{z}")

            def sums(c):
                n = P if c < TT else TS
                cols = slice(c * P, c * P + n)
                le, gt = (m_le, m_gt) if c < TT else (s_le, s_gt)
                da = DTK[0:n, 1, c, :]
                if c == 0:
                    pe.wait_ge(S("s_act"), CT)
                    read(pe, "dtt")
                    read(pe, f"st{CT - 2}")
                else:
                    pe.wait_ge(S("sc_exp"), c)
                    pe.wait_ge(S("cbm"), c)
                pe.matmul(PM[0:n, 0, 0:16], le[:], da, start=True, stop=True)
                pe.matmul(PM[0:n, 0, 16:32], gt[:], da, start=True, stop=True)
                if c < TT:
                    pe.matmul(PM[:, 0, 32:48], ones[:], da, start=True, stop=True)
                else:
                    pe.wait_ge(S("dab"), 1)
                    pe.matmul(PM[:, 0, 32:160], ones[0:n], DAB[0:n], start=True, stop=True)
                for g in range(2):
                    mm = pe.matmul(PM[0:n, g, 256:256 + n], bT[64 * g:64 * g + 64, cols], cT[64 * g:64 * g + 64, cols],
                                   start=True, stop=True)
                mm.then_inc(S("sums"), 1)

            def decays(q):
                n = P if q < 2 * TT else TS
                gt = m_gt if q < 2 * TT else s_gt
                name = f"ss{q}"
                pe.wait_ge(S("r"), q + 1)
                free_set(pe, name)
                m = 512 // n
                for i in range(8 // m):
                    mm = pe.matmul(pset(name)[0:n, i, :].rearrange("p (h i) -> p h i", i=n), gt[:],
                                   RM(q)[:, i * m:(i + 1) * m], start=True, stop=True)
                done(mm, name)

            def products(q):
                c, g = divmod(q, 2)
                n = P if c < TT else TS
                cols = slice(c * P, c * P + n)
                name = f"sy{q}"
                pe.wait_ge(S("m"), q + 1)
                pe.wait_ge(S("xdt"), q + 1)
                free_set(pe, name)
                ps = pset(name)
                if c < TT:
                    if q >= 2:
                        read(pe, f"sy{q - 2}")
                    else:
                        pe.wait_ge(S("h_zero"), 1)
                    pe.matmul(ps[0:n, 1, :], cT[64 * g:64 * g + 64, cols], H_ssd[64 * g:64 * g + 64],
                              start=True, stop=True)
                    pe.matmul(ps[64 * g:64 * g + 64, 2, :].rearrange("p (k w) -> p k w", k=4),
                              b_tok[0:n, c, 64 * g:64 * g + 64], XW(q), start=True, stop=True)
                for h in range(8):
                    mm = pe.matmul(ps[0:n, 0, h * HD:(h + 1) * HD], RM(q)[:, h], XDT(q)[:, h // 2, h % 2],
                                   start=True, stop=True)
                done(mm, name)

            def turn_y(q):
                n = P if q < 2 * TT else TS
                name = f"sn{q}"
                pe.wait_ge(S("y_norm"), q + 1)
                free_set(pe, name)
                for k in range(4):
                    mm = turn(pset(name)[:, 0, k * P:k * P + n], wk(4)[0:n, 512 + k * P:512 + (k + 1) * P], n)
                done(mm, name)
            sums(0)
            decays(0)
            for q in range(2 * TT):
                if q % 2 == 0:
                    sums(q // 2 + 1)
                products(q)
                if q + 1 < 2 * TT:
                    decays(q + 1)
                turn_y(q)
            read(pe, f"sy{2 * TT - 1}")
            free_set(pe, "po")
            for k in range(4):
                mm = turn(pset("po")[:, 0, k * P:(k + 1) * P], H_ssd[:, k * P:(k + 1) * P], P)
            done(mm, "po")
            pe.wait_ge(S("cz"), 1)
            pe.wait_ge(S("sc_exp"), TT + 1)
            pe.wait_ge(S("cbm"), TT + 1)
            pe.wait_ge(S("wx2"), 2)

            def turn_state(b):
                name = f"si{b}"
                pe.wait_ge(S(f"h_in{b % 2}"), 16 * 2 * (b // 2 + 1))
                free_set(pe, name)
                for k in range(4):
                    mm = turn(pset(name)[:, 0, k * P:(k + 1) * P], wk(0, P, b % 2 * 512 + k * P), P)
                done(mm, name)
            turn_state(0)
            for b in range(NB):
                name = f"ub{b}"
                pe.wait_ge(S("bm"), b + 1)
                free_set(pe, name)
                for g in range(2):
                    mm = pe.matmul(pset(name)[64 * g:64 * g + 64, 0, :], wk(5 + b % 2, P, D)[0:TS, 64 * g:64 * g + 64],
                                   wk(5)[0:TS, g * 512:(g + 1) * 512], start=True, stop=True)
                done(mm, name)
                if b + 1 < NB:
                    turn_state(b + 1)
                read(pe, f"si{b}")
                for g in range(2):
                    mm = pe.matmul(PM[0:TS, g, :], CZ[64 * g:64 * g + 64, b, :],
                                   wk(1, 512, b % 2 * 512)[64 * g:64 * g + 64], start=(b == 0), stop=(b == NB - 1))
                mm.then_inc(S("si_mm"), 1)
                name = f"uc{b}"
                read(pe, f"ub{b}")
                free_set(pe, name)
                for k in range(4):
                    mm = turn(pset(name)[:, 0, k * P:(k + 1) * P], wk(2, P, b % 2 * 512 + k * P), P)
                done(mm, name)
            q = 2 * TT
            decays(q)
            products(q)
            decays(q + 1)
            turn_y(q)
            products(q + 1)
            turn_y(q + 1)
            out_jobs(2, "ssd_out")
            if stop < 4:
                return
            for t in range(DT):
                name = f"mx{t}"
                project(name, FIRST_W["mix", t * P], Hh, Hl, by_tile="mi_lo" if t == 0 else None, last=False)
                pe.wait_ge(S(f"xt_in{t % 2}"), 32 * (t // 2 + 1))
                for c in range(TT + 1):
                    n = P if c < TT else TS
                    mm = pe.matmul(pset(name)[:, c // 3, c % 3 * P:c % 3 * P + n], XT[0:n, t % 2, c, :],
                                   ident[0:n, 0:n], start=False, stop=True, skip_group_check=True)
                done(mm, name)

            def sum_squares(i, name):
                free_set(pe, name)
                for k in range(DT):
                    pe.wait_ge(S("nrm_sq"), i * DT + k + 1)
                    for g, (t0, n) in enumerate(GROUPS):
                        mm = pe.matmul(pset(name)[:, g, 0:n], ones[:], wk(4 + k % 2)[:, t0:t0 + n],
                                       start=(k == 0), stop=(k == DT - 1))
                    if k < DT - 1:
                        mm.then_inc(S("nrm_mm"), 1)
                done(mm, name)
            sum_squares(0, "xn")
            for i in range(2):
                name = f"mt{i}"
                pe.wait_ge(S("mem_scaled"), 2)
                free_set(pe, name)
                for k in range(DT):
                    mm = turn(pset(name)[:, k // 4, k % 4 * P:(k % 4 + 1) * P], MV[:, i, k * P:(k + 1) * P], P)
                done(mm, name)
            pe.wait_ge(S("mem_lo"), 2)
            for i in range(4):
                done(project_tokens(f"mk{i}", FIRST_W["xk", 2 * i * P], range(2), MNh, MNl), f"mk{i}")
            for i in range(2):
                name = f"kt{i}"
                for j in range(4):
                    read(pe, f"mk{j}")
                free_set(pe, name)
                for k in range(DT):
                    mm = turn(pset(name)[:, k // 4, k % 4 * P:(k % 4 + 1) * P], KM[:, i, k * P:(k + 1) * P], P)
                done(mm, name)
            for i in range(4):
                done(project_tokens(f"mv{i}", FIRST_W["xv", 2 * i * P], range(2), MNh, MNl), f"mv{i}")
            pe.wait_ge(S("nrm_lo"), DT)
            for t in range(DT):
                done(project(f"xq{t}", FIRST_W["xq", t * P], Hh, Hl), f"xq{t}")

            def scores(c):
                name = f"xs{c}"
                free_set(pe, name)
                if c == 0:
                    read(pe, f"xq{DT - 2}")
                    read(pe, f"xq{DT - 1}")
                for h in range(XH):
                    for k in range(2):
                        mm = pe.matmul(pset(name)[:, h // 2, h % 2 * M:(h % 2 + 1) * M],
                                       Q[:, 2 * h + k, c * P:(c + 1) * P], KT_m[:, 2 * h + k, :],
                                       start=(k == 0), stop=(k == 1))
                done(mm, name)

            def turn_probs(c):
                n = P if c < TT else TS
                name = f"xp{c}"
                pe.wait_ge(S("x_p"), c + 1)
                free_set(pe, name)
                for k in range(DT):
                    mm = turn(pset(name)[:, k // 4, k % 4 * P:k % 4 * P + n], Pr(c)[0:n, k * P:(k + 1) * P], n)
                done(mm, name)

            def attend(c):
                name = f"xv{c}"
                read(pe, f"xp{c}")
                free_set(pe, name)
                for k in range(DT):
                    for m in range(2):
                        mm = pe.matmul(pset(name)[:, k // 4, k % 4 * P:(k % 4 + 1) * P], MV[:, m, k * P:(k + 1) * P],
                                       PrT(c)[:, k // 2 * 2 + m, :], start=(m == 0), stop=(m == 1))
                done(mm, name)
            scores(0)
            for c in range(TT):
                if c + 1 < TT:
                    scores(c + 1)
                turn_probs(c)
                attend(c)
            name = f"xs{TT}"
            free_set(pe, name)
            for s in range(4 * NB + 2):
                if s < 4 * NB:
                    b, h = divmod(s, 4)
                    if h == 0:
                        pe.wait_ge(S(f"kv_in{b % 2}"), 16 * (b // 2 + 1))
                    if s >= 2:
                        pe.wait_ge(S("kb_e"), s - 1)
                    for k in range(2):
                        for m in range(2):
                            mm = turn(PM[:, s % 2, (2 * k + m) * P:(2 * k + m + 1) * P],
                                      KVb[b % 2][:, m, (2 * h + k) * P:(2 * h + k + 1) * P], P)
                    mm.then_inc(S("kb_t"), 1)
                if s >= 2:
                    b, h = divmod(s - 2, 4)
                    pe.wait_ge(S("kb_e"), s - 1)
                    pe.wait_ge(S("qz"), b + 1)
                    for k in range(2):
                        mm = pe.matmul(pset(name)[0:TS, h // 2, h % 2 * M:(h % 2 + 1) * M],
                                       QZb[:, b % 2, 2 * h + k, 56 - LS * b:120 - LS * b], KTb[:, 2 * h + k, :],
                                       start=(b == 0 and k == 0 and h % 2 == 0), stop=(b == NB - 1 and k == 1),
                                       skip_group_check=True)
                    if s < 4 * NB + 1:
                        mm.then_inc(S("kb_s"), 1)
            done(mm, name)
            turn_probs(TT)
            name = f"xv{TT}"
            read(pe, f"xp{TT}")
            free_set(pe, name)
            for b in range(NB):
                pe.wait_ge(S(f"kv_in{b % 2}"), 16 * (4 + b // 2 + 1))
                for k in range(DT):
                    for m in range(2):
                        o = k % 4 * P + LS * b
                        mm = pe.matmul(pset(name)[:, k // 4, o:o + LS], KVb[b % 2][:, m, k * P:(k + 1) * P],
                                       PrT(TT)[:, k // 2 * 2 + m, LS * b:LS * b + LS], start=(m == 0), stop=(m == 1))
                if b < NB - 1:
                    mm.then_inc(S("vb"), 1)
            done(mm, name)
            read(pe, name)
            for t in range(DT):
                done(project(f"xo{t}", FIRST_W["xo", t * P], Hh, Hl), f"xo{t}")
            sum_squares(1, "fn")
            pe.wait_ge(S("nrm_lo"), 2 * DT)
            for c in range(FC + 1):
                if c < FC:
                    for i in range(2):
                        for kind in ("fg", "fu"):
                            name = f"{kind}{c}_{i}"
                            done(project(name, FIRST_W[kind, (2 * c + i) * P], Hh, Hl), name)
                if c:
                    e = c - 1
                    pe.wait_ge(S("f_lo"), 2 * c)
                    for t in range(DT):
                        name = f"fd{e}_{t}"
                        w = FIRST_W["fd", (e, t // 4)]
                        pe.wait_ge(w_split, w + 1)
                        free_set(pe, name)
                        for k in range(2):
                            for i, (L, R) in enumerate(((Wh, Fh), (Wh, Fl), (Wl, Fh))):
                                lhsT = L[:, w % 2].rearrange("p (k a) m -> p k (a m)", k=2)[:, k, t % 4 * P:(t % 4 + 1) * P]
                                for g, (t0, n) in enumerate(GROUPS):
                                    mm = pe.matmul(pset(name)[:, g, 0:n], lhsT, R[:, e % 2, k, t0:t0 + n],
                                                   start=(k == 0 and i == 0), stop=(k == 1 and i == 2))
                        done(mm, name)
            sum_squares(2, "yn")
            for c in range(TT + 1):
                n = P if c < TT else TS
                name = f"yt{c}"
                if c == 0:
                    pe.wait_ge(S("nrm_t"), 3 * DT)
                free_set(pe, name)
                for k in range(DT):
                    mm = turn(pset(name)[0:n, k // 4, k % 4 * P:(k % 4 + 1) * P], X[:, k, c * P:c * P + n], P)
                done(mm, name)

        @block.scalar
        def _(act):
            chain = [0]

            def link(ins):
                chain[0] += 1
                ins.then_inc(act_chain, 1)
                act.wait_ge(act_chain, chain[0])

            def sync_chain():
                act.wait_ge(act_chain, chain[0])

            def all_groups(name, dst, func, bias=0.0, scale=1.0):
                ready(act, name)
                for g, (t0, n) in enumerate(GROUPS):
                    ins = act.activation(dst[:, t0:t0 + n], pset(name)[:, g, 0:n], func, bias=bias, scale=scale)
                freed(ins, name)
                read(act, name)

            def store(dst, src):
                n_stores[0] += 1
                act.dma_start(dst, src).then_inc(stored, 16)

            def out_jobs(b):
                def put(t):
                    act.wait_ge(S(f"m_new{b}"), t + 1)
                    act.dma_start(merged[b, t], wk(4 + t % 2)[:, 0:T]).then_inc(S(f"m_put{t % 2}"), 16)
                for t in range(DT):
                    if b > 0:
                        if t >= 2:
                            act.wait_ge(S(f"m_new{b}"), t - 1)
                        else:
                            branch_done(act, b)
                        sum_stored(act, b - 1, t)
                        act.dma_start(wk(2 + t % 2)[:, 0:T], merged[b - 1, t]).then_inc(S(f"m_get{t % 2}"), 16)
                    if t >= 2:
                        read(act, f"ob{b}_{t - 2}")
                    else:
                        branch_done(act, b)
                    all_groups(f"og{b}_{t}", wk(t % 2), ACT.Tanh, scale=0.5)
                    if t:
                        put(t - 1)
                put(DT - 1)

            act.wait_ge(packs_zero, 2)
            for row, name, n in ((R_CW, "lru_conv_w", CW), (R_CB, "lru_conv_b", 1), (R_BA, "lru_ba", 1),
                                 (R_BX, "lru_bx", 1), (R_LAM, "lru_lambda", 1), (R_NMIX, "norm_mix", 1),
                                 (R_NX, "norm_xattn", 1), (R_NFFN, "norm_ffn", 1), (R_NMEM, "norm_mem", 1),
                                 (R_NSSD, "ssd_norm", 1)):
                src = I[name][0] if n > 1 else I[name]
                act.dma_start(wk(0)[row:row + n, 0:D], src).then_inc(packs, 16)
            act.dma_start(wk(0)[R_NFIN:R_NFIN + 1, 0:D], I["norm_final"].unsqueeze(0)).then_inc(packs, 16)
            act.dma_start(wk(0)[R_CONV:R_CONV + NB * HIST, 0:D],
                          I["state_lru_conv"][0].rearrange("b k f -> (b k) f")).then_inc(packs, 16)
            act.dma_start(wk(0)[R_H0:R_H0 + NB, 0:D], I["state_lru_h"][0]).then_inc(packs, 16)
            act.dma_start(wk(0)[R_GLA:R_GLA + 1, 0:GH * DK], I["gla_b_alpha"]).then_inc(packs, 16)
            act.dma_start(wk(0)[R_GLA:R_GLA + 1, GH * DK:GH * DK + DV], I["gla_norm"]).then_inc(packs, 16)
            pq = WK[:, WT:WT + SCC]
            act.dma_start(pq[Q_CONV:Q_CONV + NB * HIST],
                          I["state_ssd_conv"][0].rearrange("b k f -> (b k) f")).then_inc(packs, 16)
            act.dma_start(pq[Q_CW:Q_CW + CW], I["ssd_conv_w"][0]).then_inc(packs, 16)
            act.dma_start(pq[Q_CB:Q_CB + 1], I["ssd_conv_b"]).then_inc(packs, 16)
            for i, name in enumerate(("lru_wa", "lru_wx")):
                blocks = I[name][0].rearrange("(t two) i j -> two i t j", two=2)
                for h in range(2):
                    act.dma_start(YA[64 * h:64 * h + 64, DT:2 * DT, i * P + 64 * h:i * P + 64 * h + 64],
                                  blocks[h]).then_inc(S("wax"), 16)
            def load_x(c):
                n = P if c < TT else TS
                if c >= 2:
                    act.wait_ge(S("x_scaled"), c - 1)
                x = I["x_prompt"][0, c * P:c * P + n] if c < TT else I["x_sample"].rearrange("b l f -> (b l) f")
                act.dma_start(wk(3 + c % 2)[0:n, 0:D], x).then_inc(S(f"x_in{c % 2}"), 16)
            load_x(0)
            load_x(1)

            def split_x(c):
                n = P if c < TT else TS
                read(act, f"xt{c}")
                act.activation(Hh[:, :, c * P:c * P + n],
                               wk(7)[:, 0:DT * n].rearrange("p (k t) -> p k t", k=DT), ACT.Copy).then_inc(S("h_hi"), 1)
            for c in range(TT + 1):
                n = P if c < TT else TS
                act.wait_ge(S(f"x_in{c % 2}"), 16 * (c // 2 + 1))
                if c >= 2:
                    ready(act, f"xt{c - 2}")
                link(act.activation(wk(5 + c % 2)[0:n, 0:D], wk(3 + c % 2)[0:n, 0:D], ACT.Square,
                                    accum_out=ST[0:n, c:c + 1]))
                act.wait_ge(S("eps"), 1)
                act.activation(ST[0:n, c:c + 1], ST[0:n, c:c + 1], ACT.Sqrt, bias=EPSC[0:n],
                               scale=1.0 / D).then_inc(S("x_std"), 1)
                if c + 2 <= TT:
                    load_x(c + 2)
                if c:
                    split_x(c - 1)
            split_x(TT)
            if stop < 1:
                return
            read(act, "pk0")
            act.activation(LAM[:, 1], PV[:, :, R_LAM], ACT.Relu, scale=-1.0)
            link(act.activation(LAM[:, 0], PV[:, :, R_LAM], ACT.Abs))
            act.activation(LAM[:, 0], LAM[:, 0], ACT.Exp, scale=-1.0).then_inc(S("lam_exp"), 1)
            xin = WK[:, 0:HIST + LP + NB * (HIST + LS)]
            xin_p = xin[:, 0:HIST + LP]
            xin_s = xin[:, HIST + LP:].rearrange("p (b c) -> p b c", b=NB)
            for t in range(DT):
                name = f"lx{t}"
                ready(act, name)
                if t:
                    act.wait_ge(S("conv"), t)
                else:
                    act.wait_ge(S("h_lo"), TT + 1)
                for g, (t0, n) in enumerate(GROUPS):
                    np_ = min(n, LP - t0)
                    ins = act.activation(xin_p[:, HIST + t0:HIST + t0 + np_], pset(name)[:, g, 0:np_], ACT.Copy)
                ins = act.activation(xin_s[:, :, HIST:], pset(name)[:, 2, LP - 768:T - 768]
                                     .rearrange("p (b l) -> p b l", b=NB), ACT.Copy)
                freed(ins, name)
                if t:
                    act.wait_ge(S("y_lo"), t)
                all_groups(f"lg{t}", wk(5), ACT.Copy)
                act.activation(wk(6)[:, 0:T], wk(5)[:, 0:T], ACT.Square).then_inc(S("g_sq"), 1)
                if t == 0:
                    act.wait_ge(S("sc"), 1)
                all_groups(f"lr{t}", wk(2), ACT.Tanh, bias=SC[:, t, 1:2], scale=0.5)
                link(act.activation(wk(3)[:, 0:T], wk(2)[:, 0:T], ACT.Tanh, bias=SC[:, t, 0:1], scale=SC[:, t, 0:1]))
                act.activation(wk(2)[:, 0:T], wk(2)[:, 0:T], ACT.Exp, bias=NSC[:, t:t + 1],
                               scale=NSC[:, t:t + 1]).then_inc(S("a"), 1)
                all_groups(f"li{t}", wk(4), ACT.Tanh, bias=SC[:, t, 2:3], scale=0.5)
                act.wait_ge(S("g_inner"), t + 1)
                act.activation(wk(6)[:, 0:T], wk(6)[:, 0:T], ACT.Tanh, scale=GELU_C).then_inc(S("g_tanh"), 1)
                act.wait_ge(S("u_var"), t + 1)
                act.activation(wk(3)[:, 0:T], wk(3)[:, 0:T], ACT.Sqrt, scale=0.25).then_inc(S("u_mult"), 1)
                act.wait_ge(S("y"), t + 1)
                act.activation(Yh[:, t], wk(5)[:, 0:T], ACT.Copy).then_inc(S("y_hi"), 1)
            ready(act, "lt")
            branch_done(act, 0)
            freed(act.activation(wk(2)[0:36, 0:D], pset("lt")[0:36, 0:2].rearrange("p a c -> p (a c)"), ACT.Copy), "lt")
            read(act, "lt")
            store(O["p_lru_conv"][0, 0], wk(2)[0:3, 0:D])
            store(O["s_lru_conv"][0].rearrange("b k f -> (b k) f"), wk(2)[3:27, 0:D])
            store(O["p_lru_h"][0:1, 0, :], wk(2)[27:28, 0:D])
            store(O["s_lru_h"][0], wk(2)[28:36, 0:D])
            out_jobs(0)
            if stop < 2:
                return
            for t in range(DT - 2, DT):
                sum_stored(act, 0, t)
            act.wait_ge(S("m_new0"), DT)
            V = WK[:, 6 * WT:8 * WT].rearrange("p (c v) -> p c v", c=TT + 1)
            KEt = wk(1).rearrange("p (c d) -> p c d", c=TT + 1)
            RS = [wk(2)[:, 0:T], wk(5)[:, 0:T]]

            def load_alpha(h):
                if h >= 2:
                    ready(act, f"ga{h - 2}")
                act.dma_start(CB[0:16].rearrange("p k c -> p (k c)")[:, h % 2 * P:h % 2 * P + P],
                              I["gla_w_alpha"][0, :, h * P:(h + 1) * P]).then_inc(S(f"wal{h % 2}"), 16)
            load_alpha(0)
            load_alpha(1)
            ready(act, "low")
            for g, (t0, n) in enumerate(GROUPS):
                ins = act.activation(wk(0)[0:16, t0:t0 + n], pset("low")[0:16, g, 0:n], ACT.Copy)
            freed(ins, "low")
            ready(act, "dt")
            for g, (t0, n) in enumerate(GROUPS):
                ins = act.activation(wk(1)[0:16, t0:t0 + n], pset("dt")[0:16, g, 0:n], ACT.Copy)
            freed(ins, "dt")
            read(act, "dt")
            act.dma_start(dt_scr, wk(1)[0:16, 0:T]).then_inc(S("dt_put"), 16)
            act.wait_ge(S("dt_put"), 16)
            for h in range(GH):
                A = [YA[:, i] for i in (2 * h, 2 * h + 1, DT + 2 * h, DT + 2 * h + 1)]
                on = lambda c: A[1][:, 256 + c % 2 * DV:256 + (c % 2 + 1) * DV]
                St = lambda c: A[2][:, c % 2 * DV:(c % 2 + 1) * DV]
                Sb = lambda b: A[3][:, b % 2 * DV:(b % 2 + 1) * DV]
                So = lambda b: A[3][:, 512 + b % 2 * DV:512 + (b % 2 + 1) * DV]
                name = f"ga{h}"
                ready(act, name)
                act.wait_ge(S("nb"), 1)
                for g, (t0, n) in enumerate(GROUPS):
                    act.activation(A[0][:, t0:t0 + n], pset(name)[:, g, 0:n], ACT.Abs, bias=PV[:, h, R_GLA:R_GLA + 1])
                    ins = act.activation(A[1][:, t0:t0 + n], pset(name)[:, g, 0:n], ACT.Relu,
                                         bias=LAM[:, 3, h:h + 1], scale=-1.0)
                freed(ins, name)
                read(act, name)
                link(act.activation(A[0], A[0], ACT.Exp, scale=-1.0))
                act.activation(A[0], A[0], ACT.Ln, bias=1.0).then_inc(S("gl_ln"), 1)
                act.wait_ge(S("gl_cum"), h + 1)
                act.activation(A[2], A[1], ACT.Exp, scale=-1.0 / 16)
                act.activation(A[3], A[1], ACT.Exp, scale=1.0 / 16).then_inc(S("gl_exp"), 1)
                act.wait_ge(S("gl_d"), h + 1)
                act.activation(A[0], A[0], ACT.Exp, scale=-1.0 / 16).then_inc(S("gl_ed"), 1)
                read(act, f"gk{h}")
                for b in range(2):
                    act.dma_start(Sb(b), I["state_gla_S"][0, b, h]).then_inc(S(f"sb_in{b}"), 16)
                name = f"gva{h}"
                ready(act, name)
                act.activation(V[:, 0:4].rearrange("p (a c) v -> p a (c v)", a=2), pset(name)[:, 0:2, :], ACT.Copy)
                freed(act.activation(V[:, 4], pset(name)[:, 2, 0:DV], ACT.Copy), name)
                name = f"gvb{h}"
                ready(act, name)
                act.activation(V[:, 5:7].rearrange("p c v -> p (c v)"), pset(name)[:, 0, :], ACT.Copy)
                act.activation(V[:, 7], pset(name)[:, 1, 0:DV], ACT.Copy)
                freed(act.activation(V[0:TS, 8], pset(name)[0:TS, 1, DV:2 * DV], ACT.Copy), name)
                name = f"gt{h}"
                ready(act, name)
                act.activation(KEt[:, 0:8].rearrange("p (a c) d -> p a (c d)", a=2), pset(name)[:, 0:2, :], ACT.Copy)
                freed(act.activation(KEt[0:TS, 8], pset(name)[0:TS, 2, 0:P], ACT.Copy), name)
                if h:
                    act.wait_ge(S("gy_lo"), h)
                for v in range(2):
                    ready(act, f"gr{h}_{v}")
                    for g, (t0, n) in enumerate(GROUPS):
                        ins = act.activation(RS[v][:, t0:t0 + n], pset(f"gr{h}_{v}")[:, g, 0:n], ACT.Tanh, scale=0.5)
                    ins.then_inc(S("gr_th"), 1)
                if h + 2 < GH:
                    load_alpha(h + 2)
                for c in range(TT + 1):
                    n = P if c < TT else TS
                    q = h * (TT + 1) + c
                    name = f"go{h}_{c}"
                    if c == TT:
                        act.wait_ge(S("s_upd"), h * 24 + 16)
                        act.dma_start(O["p_gla_S"][0, 0, h], St(0)).then_inc(S("gs_put"), 16)
                        for b in range(NB):
                            act.wait_ge(S("s_upd"), h * 24 + 17 + b)
                            act.dma_start(O["s_gla_S"][0, b, h], So(b)).then_inc(S(f"sb_put{b % 2}"), 16)
                            if b + 2 < NB:
                                act.wait_ge(S("sb_int"), h * 7 + b + 1)
                                act.dma_start(Sb(b), I["state_gla_S"][0, b + 2, h]).then_inc(S(f"sb_in{b % 2}"), 16)
                    ready(act, name)
                    if q >= 2:
                        act.wait_ge(S("ot"), q - 1)
                    st = ST[0:n, 24 + q % 2:25 + q % 2]
                    link(act.activation(on(c)[0:n], pset(name)[0:n, 0, 0:DV], ACT.Square, accum_out=st))
                    act.activation(st, st, ACT.Sqrt, bias=EPSC[0:n], scale=1.0 / DV).then_inc(S("g_std"), 1)
                act.wait_ge(S("ymul"), (h + 1) * (TT + 1))
                act.wait_ge(S("gs_put"), 16 * (h + 1))
                for i in range(2):
                    act.wait_ge(S(f"sb_put{i}"), 16 * 4 * (h + 1))
                for v in range(2):
                    act.activation(Yh[:, 2 * h + v], RS[v], ACT.Copy).then_inc(S("gy_hi"), 1)
            out_jobs(1)
            if stop < 3:
                return
            for t in range(DT - 2, DT):
                sum_stored(act, 1, t)
            act.wait_ge(S("m_new1"), DT)
            act.dma_start(wk(6)[0:SH, 0:T], dt_scr).then_inc(S("dt_in"), 16)
            act.dma_start(ST[0:SH, 26:27], I["ssd_dt_bias"].rearrange("o h -> h o")).then_inc(S("dt_in"), 16)
            act.dma_start(ST[0:SH, 27:28], I["ssd_a_log"].rearrange("o h -> h o")).then_inc(S("dt_in"), 16)
            act.dma_start(DBC, I["ssd_d"].broadcast_to([P, SH])).then_inc(S("d_in"), 16)
            act.wait_ge(S("dt_in"), 48)
            act.activation(wk(1)[0:SH, 0:T], wk(6)[0:SH, 0:T], ACT.Relu, bias=ST[0:SH, 26:27])
            act.activation(ST[0:SH, 27:28], ST[0:SH, 27:28], ACT.Exp)
            link(act.activation(wk(0)[0:SH, 0:T], wk(6)[0:SH, 0:T], ACT.Abs, bias=ST[0:SH, 26:27]))
            act.activation(wk(0)[0:SH, 0:T], wk(0)[0:SH, 0:T], ACT.Exp, scale=-1.0).then_inc(S("dt_exp"), 1)
            xin = wk(3)
            xin_p = xin[:, 0:HIST + LP]
            xin_s = xin[:, HIST + LP:HIST + LP + NB * (HIST + LS)].rearrange("p (b c) -> p b c", b=NB)
            b_tok = wk(2).rearrange("p (c n) -> p c n", c=TT + 1)
            read(act, "dtt")
            for t in range(CT):
                name = f"sx{t}"
                ready(act, name)
                if t:
                    act.wait_ge(S("sconv"), t)
                for g, (t0, n) in enumerate(GROUPS):
                    np_ = min(n, LP - t0)
                    act.activation(xin_p[:, HIST + t0:HIST + t0 + np_], pset(name)[:, g, 0:np_], ACT.Copy)
                freed(act.activation(xin_s[:, :, HIST:], pset(name)[:, 2, LP - 768:T - 768]
                                     .rearrange("p (b l) -> p b l", b=NB), ACT.Copy), name)
                act.wait_ge(S("sconv"), t + 1)
                act.activation(wk(5)[:, 0:T], wk(4)[:, 0:T], ACT.Tanh, scale=0.5).then_inc(S("s_th"), 1)
                if t < CT - 1:
                    name = f"st{t}"
                    ready(act, name)
                    if t < DT:
                        if t:
                            act.wait_ge(S("x_put"), 32 * t)
                        dst, scale = wk(6).rearrange("p (c n) -> p c n", c=TT + 1), 0.5
                    else:
                        dst, scale = b_tok, 1.0
                    act.activation(dst[:, 0:8].rearrange("p (a c) n -> p a (c n)", a=2), pset(name)[:, 0:2, :],
                                   ACT.Copy, scale=scale)
                    freed(act.activation(dst[0:TS, 8], pset(name)[0:TS, 2, 0:P], ACT.Copy, scale=scale), name)
                    if t < DT:
                        read(act, name)
                        act.dma_start(x_scr[0:LP, t * P:(t + 1) * P].rearrange("(c p) n -> p c n", p=P),
                                      dst[:, 0:8]).then_inc(S("x_put"), 16)
                        act.dma_start(x_scr[LP:T, t * P:(t + 1) * P], dst[0:TS, 8]).then_inc(S("x_put"), 16)
            act.wait_ge(S("x_put"), 32 * DT)
            act.wait_ge(S("s_act"), CT)
            ready(act, "qt")
            tails = WK[0:27, 5 * WT:5 * WT + SCC]
            act.activation(tails[:, 0:D], pset("qt")[0:27, 0:2].rearrange("p a c -> p (a c)"), ACT.Copy)
            freed(act.activation(tails[:, D:SCC], pset("qt")[0:27, 2, 0:SCC - D], ACT.Copy), "qt")
            read(act, "qt")
            store(O["p_ssd_conv"][0, 0], tails[0:3])
            store(O["s_ssd_conv"][0].rearrange("b k f -> (b k) f"), tails[3:27])
            act.wait_ge(stored, 16 * n_stores[0])
            za = WK[:, 3 * WT:3 * WT + 5 * 256].rearrange("p (c n) -> p c n", n=256)
            zb = wk(5, D).rearrange("p (c n) -> p c n", n=256)
            for z in range(4):
                cols = slice(z * 256, (z + 1) * 256)
                name = f"sza{z}"
                ready(act, name)
                if z:
                    act.wait_ge(S("za_put"), 16 * z)
                act.activation(za[:, 0:4].rearrange("p (a c) n -> p a (c n)", a=2), pset(name)[:, 0:2, :], ACT.Tanh,
                               scale=0.5)
                act.activation(za[:, 4], pset(name)[:, 2, 0:256], ACT.Tanh, scale=0.5).then_inc(S("z_th"), 1)
                name = f"szb{z}"
                ready(act, name)
                if z:
                    act.wait_ge(S("zb_put"), 32 * z)
                act.activation(zb[:, 0:2].rearrange("p c n -> p (c n)"), pset(name)[:, 0, :], ACT.Tanh, scale=0.5)
                act.activation(zb[:, 2], pset(name)[:, 1, 0:256], ACT.Tanh, scale=0.5)
                act.activation(zb[0:TS, 3], pset(name)[0:TS, 1, 256:512], ACT.Tanh, scale=0.5).then_inc(S("z_th"), 1)
                read(act, f"sza{z}")
                act.dma_start(z_scr[0:5 * P, cols].rearrange("(c p) n -> p c n", p=P), za).then_inc(S("za_put"), 16)
                read(act, name)
                act.dma_start(z_scr[5 * P:8 * P, cols].rearrange("(c p) n -> p c n", p=P), zb[:, 0:3])\
                    .then_inc(S("zb_put"), 16)
                act.dma_start(z_scr[LP:T, cols], zb[0:TS, 3]).then_inc(S("zb_put"), 16)
            act.wait_ge(S("za_put"), 64)
            act.wait_ge(S("zb_put"), 128)

            def load_z(q):
                c, g = divmod(q, 2)
                n = P if c < TT else TS
                act.dma_start(wk(4)[0:n, 0:512], z_scr[c * P:c * P + n, g * 512:(g + 1) * 512]).then_inc(S("z_in"), 16)

            def load_xs(q):
                c, g = divmod(q, 2)
                n = P if c < TT else TS
                half = slice(g * 512, (g + 1) * 512)
                act.dma_start(wk(3)[0:n, half], x_scr[c * P:c * P + n, half]).then_inc(S(f"xs_in{g}"), 16)

            def state_in(b):
                src = I["state_ssd_h"][0, b].rearrange("(g k h) p n -> g (h p) k n", g=2, k=4)
                dst = wk(0, 512, b % 2 * 512).rearrange("p (k g n) -> p k g n", k=4, g=2)
                for g in range(2):
                    act.dma_start(dst[:, :, g], src[g]).then_inc(S(f"h_in{b % 2}"), 16)

            def state_out(dst, src, signal):
                d = dst.rearrange("(g k h) p n -> g (h p) k n", g=2, k=4)
                s = src.rearrange("p (k g n) -> p k g n", k=4, g=2)
                for g in range(2):
                    act.dma_start(d[g], s[:, :, g]).then_inc(signal, 16)

            def exp_sums(c):
                n = P if c < TT else TS
                m = 16 if c < TT else 128
                act.wait_ge(S("sums"), c + 1)
                act.activation(EC(c)[0:n], PM[0:n, 0, 0:32], ACT.Exp)
                act.activation(EL(c), PM[:, 0, 32:32 + m], ACT.Exp).then_inc(S("sc_exp"), 1)

            def exp_decays(q):
                n = P if q < 2 * TT else TS
                name = f"ss{q}"
                m = 512 // n
                ready(act, name)
                for i in range(8 // m):
                    ins = act.activation(RM(q)[:, i * m:(i + 1) * m],
                                         pset(name)[0:n, i, :].rearrange("p (h i) -> p h i", i=n), ACT.Exp)
                freed(ins, name)

            def square_y(q):
                n = P if q < 2 * TT else TS
                act.wait_ge(S("y_gated"), q + 1)
                st = ST[0:n, 28 + q % 2:29 + q % 2]
                link(act.activation(wk(4)[0:n, 0:512], wk(4)[0:n, 512:1024], ACT.Square, scale=0.5, accum_out=st))
                act.activation(st, st, ACT.Sqrt, bias=EPSC[0:n], scale=1.0 / 512).then_inc(S("y_std"), 1)
                if q + 1 < 2 * (TT + 1):
                    load_z(q + 1)

            def hi_y(q):
                c, g = divmod(q, 2)
                n = P if c < TT else TS
                read(act, f"sn{q}")
                act.activation(Yh[:, 4 * g:4 * g + 4, c * P:c * P + n],
                               YT[:, 0:4 * n].rearrange("p (k t) -> p k t", k=4), ACT.Copy).then_inc(S("sy_hi"), 1)
            load_z(0)
            load_xs(0)
            load_xs(1)
            exp_sums(0)
            exp_decays(0)
            for q in range(2 * TT):
                if q + 1 < 2 * TT:
                    exp_decays(q + 1)
                act.wait_ge(S("x_used"), q + 1)
                load_xs(q + 2)
                square_y(q)
                if q % 2 == 0:
                    exp_sums(q // 2 + 1)
                if q == 2 * TT - 1:
                    for b in range(2):
                        state_in(b)
                hi_y(q)
            ready(act, "po")
            freed(act.activation(wk(2, 512), pset("po")[:, 0, :], ACT.Copy), "po")
            read(act, "po")
            n_stores[0] += 2
            state_out(O["p_ssd_h"][0, 0], wk(2, 512), stored)
            SO = [wk(6, 512, 512), wk(4, 512, 512)]

            def copy_state(b):
                name = f"si{b}"
                ready(act, name)
                if b + 2 < NB:
                    state_in(b + 2)
                if b >= 2:
                    act.wait_ge(S("si_mm"), b - 1)
                    read(act, f"ub{b - 2}")
                freed(act.activation(wk(1, 512, b % 2 * 512), pset(name)[:, 0, :], ACT.Copy), name)
            act.wait_ge(stored, 16 * n_stores[0])
            act.wait_ge(S("cz"), 1)
            for b in range(NB + 1):
                if b < NB:
                    copy_state(b)
                if b:
                    name = f"uc{b - 1}"
                    ready(act, name)
                    if b >= 3:
                        act.wait_ge(S(f"h_put{(b - 1) % 2}"), 32 * ((b - 1) // 2))
                    freed(act.activation(SO[(b - 1) % 2], pset(name)[:, 0, :], ACT.Copy), name)
                    read(act, name)
                    state_out(O["s_ssd_h"][0, b - 1], SO[(b - 1) % 2], S(f"h_put{(b - 1) % 2}"))
            act.wait_ge(S("si_mm"), NB)
            act.activation(YI[0][0:TS], PM[0:TS, 0, :], ACT.Copy)
            act.activation(YI[1][0:TS], PM[0:TS, 1, :], ACT.Copy).then_inc(S("yi"), 1)
            q = 2 * TT
            exp_decays(q)
            exp_decays(q + 1)
            square_y(q)
            hi_y(q)
            square_y(q + 1)
            hi_y(q + 1)
            out_jobs(2)
            if stop < 4:
                return
            for t in range(DT - 2, DT):
                sum_stored(act, 2, t)
            act.wait_ge(S("m_new2"), DT)
            for i in range(2):
                act.dma_start(WK[:, 4 * i * WT:4 * (i + 1) * WT].rearrange("p (k w) -> p k w", k=4)[:, :, 0:T],
                              merged[2, 4 * i:4 * i + 4].rearrange("k p t -> p k t")).then_inc(S(f"mi_in{i}"), 16)

            def load_xt(t):
                cols = slice(t * P, (t + 1) * P)
                act.dma_start(XT[:, t % 2, 0:TT], I["x_prompt"][0, :, cols].rearrange("(c p) f -> p c f", p=P))\
                    .then_inc(S(f"xt_in{t % 2}"), 16)
                act.dma_start(XT[0:TS, t % 2, TT], I["x_sample"].rearrange("b l f -> (b l) f")[:, cols])\
                    .then_inc(S(f"xt_in{t % 2}"), 16)
            load_xt(0)
            load_xt(1)
            for k in range(DT):
                act.wait_ge(S(f"mi_in{k // 4}"), 16)
                act.activation(Hh[:, k], wk(k)[:, 0:T], ACT.Copy).then_inc(S("mi_hi"), 1)
            for t in range(DT):
                all_groups(f"mx{t}", X[:, t], ACT.Copy)
                if t + 2 < DT:
                    load_xt(t + 2)
            act.wait_ge(S("mi_lo"), DT)

            def norm(i, name, split):
                for k in range(DT):
                    if i == 1:
                        read(act, f"xo{k}")
                    if k >= 2:
                        act.wait_ge(S("nrm_mm"), i * (DT - 1) + k - 1)
                    act.activation(wk(4 + k % 2)[:, 0:T], X[:, k], ACT.Square).then_inc(S("nrm_sq"), 1)
                ready(act, name)
                for g, (t0, n) in enumerate(GROUPS):
                    ins = act.activation(wk(6)[:, t0:t0 + n], pset(name)[:, g, 0:n], ACT.Sqrt, bias=EPSC[:],
                                         scale=1.0 / D)
                freed(ins, name)
                if split:
                    for k in range(DT):
                        act.wait_ge(S("nrm_t"), i * DT + k + 1)
                        act.activation(Hh[:, k], wk(4 + k % 2)[:, 0:T], ACT.Copy).then_inc(S("nrm_hi"), 1)
            act.dma_start(MV, I["mem_prompt"][0].rearrange("(m p) f -> p m f", p=P)).then_inc(S("mem_in"), 16)
            norm(0, "xn", True)
            act.wait_ge(S("mem_in"), 16)
            for i in range(2):
                link(act.activation(wk(0)[:, 0:D], MV[:, i], ACT.Square, accum_out=ST[:, 30 + i:31 + i]))
            act.activation(ST[:, 30:32], ST[:, 30:32], ACT.Sqrt, bias=EPSC[:], scale=1.0 / D).then_inc(S("mem_std"), 1)
            for i in range(2):
                read(act, f"mt{i}")
                act.activation(MNh[:, :, i * P:(i + 1) * P], wk(7, D).rearrange("p (k m) -> p k m", k=DT), ACT.Copy)\
                    .then_inc(S("mem_hi"), 1)
            for i in range(4):
                name = f"mk{i}"
                ready(act, name)
                freed(act.activation(KM[:, :, i * 256:(i + 1) * 256],
                                     pset(name)[:, 0, :].rearrange("p (m f) -> p m f", m=2), ACT.Copy), name)
            for i in range(4):
                read(act, f"mk{i}")
            store(O["p_mem_k"][0, 0].rearrange("(m p) h d -> p m (h d)", p=P), KM[:])
            for i in range(2):
                name = f"kt{i}"
                ready(act, name)
                freed(act.activation(KT_m[:, :, i * P:(i + 1) * P],
                                     pset(name)[:, 0:2, :].rearrange("p a (k m) -> p (a k) m", k=4), ACT.Copy), name)
            for i in range(4):
                name = f"mv{i}"
                ready(act, name)
                freed(act.activation(MV[:, :, i * 256:(i + 1) * 256],
                                     pset(name)[:, 0, :].rearrange("p (m f) -> p m f", m=2), ACT.Copy), name)
            for i in range(4):
                read(act, f"mv{i}")
            store(O["p_mem_v"][0, 0].rearrange("(m p) h d -> p m (h d)", p=P), MV)
            act.wait_ge(stored, 16 * n_stores[0])
            for t in range(DT):
                all_groups(f"xq{t}", Q[:, t], ACT.Copy)

            def probs(c):
                n = P if c < TT else TS
                name = f"xs{c}"
                act.wait_ge(S("x_max"), c + 1)
                if 2 <= c < TT:
                    ready(act, f"xp{c - 2}")
                for h in range(XH):
                    ins = act.activation(Pr(c)[0:n, h * M:(h + 1) * M], pset(name)[0:n, h // 2, h % 2 * M:(h % 2 + 1) * M],
                                         ACT.Exp, bias=ST[0:n, 32 + 4 * (c % 2) + h:33 + 4 * (c % 2) + h],
                                         scale=XD ** -0.5,
                                         accum_out=ST[0:n, 40 + 4 * (c % 2) + h:41 + 4 * (c % 2) + h])
                freed(ins, name)

            def outputs(c):
                n = P if c < TT else TS
                name = f"xp{c}"
                ready(act, name)
                if 2 <= c < TT:
                    ready(act, f"xv{c - 2}")
                for a in range(2):
                    ins = act.activation(PrT(c)[:, 4 * a:4 * a + 4, 0:n],
                                         pset(name)[:, a, :].rearrange("p (k t) -> p k t", k=4)[:, :, 0:n], ACT.Copy)
                freed(ins, name)
                if c == TT:
                    for b in range(NB):
                        if b >= 2:
                            act.wait_ge(S("vb"), b - 1)
                            load_kv(b, "v")
                name = f"xv{c}"
                ready(act, name)
                for a in range(2):
                    ins = act.activation(Hh[:, 4 * a:4 * a + 4, c * P:c * P + n],
                                         pset(name)[:, a, :].rearrange("p (k t) -> p k t", k=4)[:, :, 0:n], ACT.Copy)
                ins.then_inc(S("xo_hi"), 1)

            def load_kv(b, which):
                act.dma_start(KVb[b % 2], I[f"cache_mem_{which}"][0, b].rearrange("(m p) h d -> p m (h d)", p=P))\
                    .then_inc(S(f"kv_in{b % 2}"), 16)
            probs(0)
            for c in range(TT):
                if c + 1 < TT:
                    probs(c + 1)
                outputs(c)
            load_kv(0, "k")
            load_kv(1, "k")
            for s in range(4 * NB):
                act.wait_ge(S("kb_t"), s + 1)
                if s >= 4:
                    act.wait_ge(S("kb_s"), s - 3)
                act.activation(KTb[:, s % 4 * 2:s % 4 * 2 + 2].rearrange("p k m -> p (k m)"), PM[:, s % 2, :], ACT.Copy)\
                    .then_inc(S("kb_e"), 1)
                if s % 4 == 3:
                    b = s // 4
                    load_kv(b % 2 if b + 2 >= NB else b + 2, "v" if b + 2 >= NB else "k")
            probs(TT)
            outputs(TT)
            norm(1, "fn", True)
            for c in range(FC):
                for i in range(2):
                    q = 2 * c + i
                    name = f"fg{c}_{i}"
                    ready(act, name)
                    if q >= 4:
                        act.wait_ge(S("f_lo"), q - 3)
                    for g, (t0, n) in enumerate(GROUPS):
                        ins = act.activation(wk(q % 4)[:, t0:t0 + n], pset(name)[:, g, 0:n], ACT.Tanh, scale=0.5)
                    ins.then_inc(S("f_th"), 1)
                    read(act, f"fu{c}_{i}")
                    if q >= 4:
                        ready(act, f"fd{c - 2}_{DT - 1}")
                    act.activation(Fh[:, c % 2, i], wk(q % 4)[:, 0:T], ACT.Copy).then_inc(S("f_hi"), 1)
            for i in range(2):
                read(act, f"fd{FC - 1}_{DT - 1 - i}")
            norm(2, "yn", False)
            for c in range(TT + 1):
                n = P if c < TT else TS
                name = f"yt{c}"
                ready(act, name)
                if c >= 2:
                    act.wait_ge(S(f"out{c % 2}"), 16 * (c // 2))
                freed(act.activation(wk(c % 2)[0:n, 0:D], pset(name)[0:n, 0:2].rearrange("p a c -> p (a c)"), ACT.Copy), name)
                read(act, name)
                y = O["y_prompt"][0, c * P:c * P + n] if c < TT else O["y_sample"].rearrange("b l f -> (b l) f")
                act.dma_start(y, wk(c % 2)[0:n, 0:D]).then_inc(S(f"out{c % 2}"), 16)
            act.wait_ge(S("out0"), 16 * 5)
            act.wait_ge(S("out1"), 16 * 4)
            act.wait_ge(stored, 16 * n_stores[0])

        @block.vector
        def _(dve):
            chain = [0]

            def link(ins):
                chain[0] += 1
                ins.then_inc(dve_chain, 1)
                dve.wait_ge(dve_chain, chain[0])

            def stt(out, in0, scalar, in1, op0, op1):
                return dve.scalar_tensor_tensor(out=out, in0=in0, scalar=scalar, in1=in1, op0=op0, op1=op1)

            MUL, ADD, SUB = ALU.mult, ALU.add, ALU.subtract

            def out_jobs(b):
                for t in range(DT):
                    th = wk(t % 2)
                    read(dve, f"og{b}_{t}")
                    ready(dve, f"ob{b}_{t}")
                    for g, (t0, n) in enumerate(GROUPS):
                        ins = stt(th[:, t0:t0 + n], th[:, t0:t0 + n], 1.0, pset(f"ob{b}_{t}")[:, g, 0:n], ADD, MUL)
                    freed(ins, f"ob{b}_{t}")
                    read(dve, f"ob{b}_{t}")
                    if t >= 2:
                        sum_stored(dve, b, t - 2)
                    if b == 0:
                        dve.tensor_scalar(wk(4 + t % 2)[:, 0:T], th[:, 0:T], 0.5, None, MUL).then_inc(S(f"m_new{b}"), 1)
                    else:
                        dve.wait_ge(S(f"m_get{t % 2}"), 16 * ((b - 1) * DT // 2 + t // 2 + 1))
                        stt(wk(4 + t % 2)[:, 0:T], th[:, 0:T], 0.5, wk(2 + t % 2)[:, 0:T], MUL, ADD)\
                            .then_inc(S(f"m_new{b}"), 1)

            def conv(xin_p, xin_s, dst, taps, bias, hist, tail):
                link(dve.tensor_copy(xin_s[:, :, 0:HIST], hist))
                for out, src in ((dst[:, 0:LP], lambda k: xin_p[:, k:k + LP]),
                                 (seqs(dst), lambda k: xin_s[:, :, k:k + LS])):
                    link(dve.tensor_scalar(out, src(0), taps[0], bias, MUL, ADD))
                    for k in range(1, CW):
                        link(stt(out, src(k), taps[k], out, MUL, ADD))
                link(dve.tensor_copy(tail[:, 0:HIST], xin_p[:, LP:LP + HIST]))
                return dve.tensor_copy(tail[:, HIST:HIST + NB * HIST].rearrange("p (b k) -> p b k", b=NB),
                                       xin_s[:, :, LS:LS + HIST])

            dve.memset(EPSC[:], EPS).then_inc(S("eps"), 1)
            dve.memset(wk(0)[0:NROW, 0:D], 0.0).then_inc(packs_zero, 1)
            dve.memset(YA[:, DT:2 * DT, 0:2 * P], 0.0).then_inc(packs_zero, 1)
            ready(dve, "pk0")
            freed(dve.tensor_copy(PV[:], pset("pk0")[:, 0, 0:DT * NROW].rearrange("p (k r) -> p k r", k=DT)), "pk0")
            ready(dve, "pk1")
            freed(dve.tensor_copy(PQ[:], pset("pk1")[:, 0, 0:CT * QROW].rearrange("p (k r) -> p k r", k=CT)), "pk1")
            read(dve, "pk0")
            read(dve, "pk1")
            def lo_x(c):
                n = P if c < TT else TS
                dve.wait_ge(S("h_hi"), c + 1)
                dve.tensor_tensor(Hl[:, :, c * P:c * P + n], wk(7)[:, 0:DT * n].rearrange("p (k t) -> p k t", k=DT),
                                  Hh[:, :, c * P:c * P + n].bitcast(F32), SUB).then_inc(S("h_lo"), 1)
            for c in range(TT + 1):
                n = P if c < TT else TS
                dve.wait_ge(S("x_std"), c + 1)
                link(dve.reciprocal(ST[0:n, c:c + 1], ST[0:n, c:c + 1]))
                dve.tensor_scalar(wk(5 + c % 2)[0:n, 0:D], wk(3 + c % 2)[0:n, 0:D], ST[0:n, c:c + 1], None, MUL)\
                    .then_inc(S("x_scaled"), 1)
                if c:
                    lo_x(c - 1)
                    dve.wait_ge(S("h_lo"), c)
                ready(dve, f"xt{c}")
                for i in range(2):
                    ins = dve.tensor_tensor(
                        wk(7)[:, i * 4 * n:(i + 1) * 4 * n].rearrange("p (k t) -> p k t", k=4),
                        pset(f"xt{c}")[:, i].rearrange("p (k t) -> p k t", k=4)[:, :, 0:n],
                        PV[:, 4 * i:4 * i + 4, R_NMIX:R_NMIX + 1].broadcast_to([P, 4, n]), MUL)
                    if i == 0:
                        link(ins)
                freed(ins, f"xt{c}")
                read(dve, f"xt{c}")
            lo_x(TT)
            if stop < 1:
                return

            def atanh_of(e, s, s2, p):
                link(dve.tensor_scalar(s, e, 2.0, None, ADD))
                link(dve.reciprocal(s, s))
                link(dve.tensor_tensor(s, s, e, MUL))
                link(dve.tensor_tensor(s2, s, s, MUL))
                link(dve.tensor_scalar(p, s2, 1.0 / 15, None, MUL))
                for m in (13, 11, 9, 7, 5, 3):
                    link(stt(p, p, 1.0 / m, s2, ADD, MUL))
                link(stt(s, p, 1.0, s, ADD, MUL))

            dve.wait_ge(S("lam_exp"), 1)
            atanh_of(LAM[:, 0], LAM[:, 2], LAM[:, 3], NSC[:])
            link(stt(NSC[:], LAM[:, 2], 2.0, LAM[:, 1], MUL, ADD))
            link(dve.tensor_scalar(SC[:, :, 0], NSC[:], 4.0, None, MUL))
            link(dve.tensor_scalar(NSC[:], NSC[:], -4.0, None, MUL))
            dve.tensor_scalar(SC[:, :, 1:3], PV[:, :, R_BA:R_BX + 1], 0.5, None, MUL).then_inc(S("sc"), 1)
            xin = WK[:, 0:HIST + LP + NB * (HIST + LS)]
            xin_p = xin[:, 0:HIST + LP]
            xin_s = xin[:, HIST + LP:].rearrange("p (b c) -> p b c", b=NB)
            link(dve.memset(xin_p[:, 0:HIST], 0.0))
            xc, A, TZ, TI, G, GP, U = (wk(i)[:, 0:T] for i in range(1, 8))
            for t in range(DT):
                read(dve, f"lx{t}")
                conv(xin_p, xin_s, xc, [PV[:, t, R_CW + k:R_CW + k + 1] for k in range(CW)],
                     PV[:, t, R_CB:R_CB + 1], PV[:, t, R_CONV:R_CONV + NB * HIST].rearrange("p (b k) -> p b k", b=NB),
                     CB[:, t]).then_inc(S("conv"), 1)
                dve.wait_ge(S("g_sq"), t + 1)
                link(dve.tensor_scalar(GP, GP, 0.044715, 1.0, MUL, ADD))
                dve.tensor_tensor(GP, GP, G, MUL).then_inc(S("g_inner"), 1)
                dve.wait_ge(S("a"), t + 1)
                link(dve.tensor_tensor(U, A, A, MUL))
                stt(TZ, U, 1.0, TZ, ADD, MUL).then_inc(S("u_var"), 1)
                read(dve, f"li{t}")
                link(stt(TI, TI, 1.0, xc, ADD, MUL))
                dve.wait_ge(S("u_mult"), t + 1)
                link(dve.tensor_tensor(TI, TI, TZ, MUL))
                h0 = PV[:, t, R_H0:R_H0 + NB]
                link(dve.tensor_tensor(LAM[:, 0], seqs(A)[:, :, 0], h0, MUL))
                link(dve.tensor_tensor(seqs(TI)[:, :, 0], seqs(TI)[:, :, 0], LAM[:, 0], ADD))
                link(dve.memset(seqs(A)[:, :, 0:1], 0.0))
                link(dve.tensor_tensor_scan(U, A, TI, 0.0, MUL, ADD))
                dve.tensor_copy(CB[:, t, 27:28], U[:, LP - 1:LP])
                dve.tensor_copy(CB[:, t, 28:36], seqs(U)[:, :, LS - 1]).then_inc(S("cb"), 1)
                dve.wait_ge(S("g_tanh"), t + 1)
                link(stt(GP, GP, 1.0, G, ADD, MUL))
                stt(G, GP, 0.5, U, MUL, MUL).then_inc(S("y"), 1)
                dve.wait_ge(S("y"), t + 1)
                dve.wait_ge(S("y_hi"), t + 1)
                ins = dve.tensor_tensor(Yl[:, t], G, Yh[:, t].bitcast(F32), SUB)
                ins.then_inc(S("y_lo"), 1)
            out_jobs(0)
            if stop < 2:
                return
            V = WK[:, 6 * WT:8 * WT].rearrange("p (c v) -> p c v", c=TT + 1)
            KEt = wk(1).rearrange("p (c d) -> p c d", c=TT + 1)
            QT, KT = wk(3)[:, 0:T], wk(4)[:, 0:T]
            RS = [wk(2)[:, 0:T], wk(5)[:, 0:T]]
            RS2 = WK[:, 2 * WT:8 * WT].rearrange("p (a w) -> p a w", a=2)
            dve.tensor_scalar(LAM[:, 3, 0:GH], PV[:, 0:GH, R_GLA], -1.0, None, MUL).then_inc(S("nb"), 1)

            def chunks(ap, size):
                return ap.rearrange("p (a c) -> p a c", c=size)
            for h in range(GH):
                A = [YA[:, i] for i in (2 * h, 2 * h + 1, DT + 2 * h, DT + 2 * h + 1)]
                att = lambda c: A[1][:, c % 2 * P:c % 2 * P + P]
                on = lambda c: A[1][:, 256 + c % 2 * DV:256 + (c % 2 + 1) * DV]
                St = lambda c: A[2][:, c % 2 * DV:(c % 2 + 1) * DV]
                QZ = A[2][:, 512:1024].rearrange("p (b t) -> p b t", b=NB)
                KEm = A[0][0:TS, 0:D].rearrange("p (b d) -> p b d", b=NB)
                Sb = lambda b: A[3][:, b % 2 * DV:(b % 2 + 1) * DV]
                So = lambda b: A[3][:, 512 + b % 2 * DV:512 + (b % 2 + 1) * DV]
                dve.wait_ge(S("gl_ln"), h + 1)
                link(dve.tensor_tensor(A[0], A[0], A[1], ADD))
                dve.tensor_tensor_scan(A[1], rmask, A[0], 0.0, MUL, ADD).then_inc(S("gl_cum"), 1)
                dve.wait_ge(S("gl_cum"), h + 1)
                for src, dst, size in ((A[1][:, 0:LP], A[0][:, 0:LP], GCH), (A[1][:, LP:T], A[0][:, LP:T], LS)):
                    s3 = chunks(src, size)
                    ins = dve.tensor_tensor(chunks(dst, size), s3[:, :, size - 1:size]
                                            .broadcast_to(list(s3.shape)), s3, SUB)
                ins.then_inc(S("gl_d"), 1)
                dve.wait_ge(S("gl_exp"), h + 1)
                dve.tensor_copy(ST[:, 0:16], chunks(A[2][:, 0:LP], GCH)[:, :, GCH - 1])
                link(dve.tensor_copy(ST[:, 16:24], seqs(A[2])[:, :, LS - 1]))
                ready(dve, f"gq{h}")
                for g, (t0, n) in enumerate(GROUPS):
                    ins = stt(QT[:, t0:t0 + n], pset(f"gq{h}")[:, g, 0:n], DK ** -0.5, A[2][:, t0:t0 + n], MUL, MUL)
                freed(ins, f"gq{h}")
                read(dve, f"gq{h}")
                ready(dve, f"gk{h}")
                for g, (t0, n) in enumerate(GROUPS):
                    link(dve.tensor_tensor(KT[:, t0:t0 + n], pset(f"gk{h}")[:, g, 0:n], A[3][:, t0:t0 + n], MUL))
                dve.wait_ge(S("gl_ed"), h + 1)
                for g, (t0, n) in enumerate(GROUPS):
                    ins = dve.tensor_tensor(A[0][:, t0:t0 + n], pset(f"gk{h}")[:, g, 0:n], A[0][:, t0:t0 + n], MUL)
                    if g < 2:
                        link(ins)
                freed(ins, f"gk{h}")
                read(dve, f"gk{h}")
                dve.memset(St(0), 0.0).then_inc(S("ke"), 1)
                dve.wait_ge(S("ke"), h + 1)
                dve.tensor_tensor(QZ, mid(QT[:, LP:T], NB), seqm[:], MUL).then_inc(S("s_zero"), 1)
                for v in range(2):
                    name = f"gr{h}_{v}"
                    dve.wait_ge(S("gr_th"), 2 * h + v + 1)
                    for g, (t0, n) in enumerate(GROUPS):
                        ins = stt(RS[v][:, t0:t0 + n], RS[v][:, t0:t0 + n], 1.0, pset(name)[:, g, 0:n], ADD, MUL)
                    freed(ins, name)
                    read(dve, name)
                    link(dve.tensor_scalar(RS[v], RS[v], PV[:, 4 + v, R_GLA:R_GLA + 1], 0.5, MUL, MUL))
                read(dve, f"gt{h}")
                dve.tensor_tensor(KEm, mid(KEt[0:TS, 8], NB), bc(seqcol[:], DK), MUL).then_inc(S("kem"), 1)

                def gate_o(c):
                    n = P if c < TT else TS
                    q = h * (TT + 1) + c
                    dve.wait_ge(S("ot"), q + 1)
                    r = RS2[:, :, c * P:c * P + n]
                    dve.tensor_tensor(r, PM[:, 1, 0:256].rearrange("p (v t) -> p v t", v=2)[:, :, 0:n],
                                      r, MUL).then_inc(S("ymul"), 1)

                def update(e, part, b=None):
                    i = e - 24 * h
                    dve.wait_ge(S("ds"), e + 1)
                    new, old = (St(e + 1), St(e)) if b is None else (So(b), Sb(b))
                    stt(new, old, ST[:, i:i + 1], part, MUL, ADD)\
                        .then_inc(S("s_upd"), 1)
                    dve.wait_ge(S("s_upd"), e + 1)
                for c in range(TT + 1):
                    n = P if c < TT else TS
                    q = h * (TT + 1) + c
                    name = f"go{h}_{c}"
                    dve.wait_ge(S("att"), q + 1)
                    mask = m_ch if c < TT else s_le
                    dve.tensor_tensor(att(c)[0:n, 0:n], pset(name)[0:n, 1, 0:n], mask[:], MUL).then_inc(S("att_m"), 1)
                    if c < TT:
                        if c:
                            ready(dve, f"go{h}_{c - 1}")
                        update(24 * h + 2 * c, PM[:, 0, 0:256])
                        dve.wait_ge(S("inter"), h * TT + c + 1)
                        update(24 * h + 2 * c + 1, pset(name)[:, 2, 0:256])
                    else:
                        for b in range(NB):
                            dve.wait_ge(S(f"sb_in{b % 2}"), 16 * (h * 4 + b // 2 + 1))
                            if h * NB + b >= 2:
                                dve.wait_ge(S(f"sb_put{b % 2}"), 16 * (h * 4 + b // 2))
                            update(24 * h + 16 + b, PM[:, 0, 0:256] if b % 2 == 0 else pset(name)[:, 2, 0:256], b)
                    dve.wait_ge(S("g_std"), q + 1)
                    st = ST[0:n, 24 + q % 2:25 + q % 2]
                    link(dve.reciprocal(st, st))
                    freed(dve.tensor_scalar(on(c)[0:n], pset(name)[0:n, 0, 0:DV], st, None, MUL), name)
                    if c:
                        gate_o(c - 1)
                gate_o(TT)
                for v in range(2):
                    dve.wait_ge(S("gy_hi"), 2 * h + v + 1)
                    ins = dve.tensor_tensor(Yl[:, 2 * h + v], RS[v], Yh[:, 2 * h + v].bitcast(F32), SUB)
                ins.then_inc(S("gy_lo"), 1)
                dve.wait_ge(S("gy_lo"), h + 1)
            out_jobs(1)
            if stop < 3:
                return
            dve.wait_ge(S("dt_exp"), 1)
            tl = [wk(i)[0:SH, 0:T] for i in range(7)]
            atanh_of(tl[0], tl[2], tl[3], tl[4])
            link(stt(tl[5], tl[2], 2.0, tl[1], MUL, ADD))
            dve.tensor_scalar(tl[6], tl[5], ST[0:SH, 27:28], -1.0, MUL, MUL).then_inc(S("dt_done"), 1)
            ready(dve, "dtt")
            turned = pset("dtt")[:, 0, 0:288].rearrange("p (s c h) -> p s c h", s=2, c=TT + 1)
            dve.wait_ge(S("d_in"), 16)
            dve.tensor_copy(DTK[:, :, 0:TT, :], turned[:, :, 0:TT, :])
            freed(dve.tensor_copy(DTK[0:TS, :, TT, :], turned[0:TS, :, TT, :]), "dtt")
            xin = wk(3)
            xin_p = xin[:, 0:HIST + LP]
            xin_s = xin[:, HIST + LP:HIST + LP + NB * (HIST + LS)].rearrange("p (b c) -> p b c", b=NB)
            b_tok = wk(2).rearrange("p (c n) -> p c n", c=TT + 1)
            dve.wait_ge(S("dt_done"), 1)
            link(dve.memset(xin_p[:, 0:HIST], 0.0))
            for t in range(CT):
                read(dve, f"sx{t}")
                if 1 <= t <= DT:
                    ready(dve, f"st{t - 1}")
                conv(xin_p, xin_s, wk(4)[:, 0:T], [PQ[:, t, Q_CW + k:Q_CW + k + 1] for k in range(CW)],
                     PQ[:, t, Q_CB:Q_CB + 1], PQ[:, t, Q_CONV:Q_CONV + NB * HIST].rearrange("p (b k) -> p b k", b=NB),
                     CQ[:, t]).then_inc(S("sconv"), 1)
                dve.wait_ge(S("s_th"), t + 1)
                dve.wait_ge(S("sconv"), t + 1)
                ins = stt(wk(4)[:, 0:T], wk(5)[:, 0:T], 1.0, wk(4)[:, 0:T], ADD, MUL)
                if t >= DT:
                    link(ins)
                    ins = dve.tensor_scalar(wk(t - DT)[:, 0:T], wk(4)[:, 0:T], 0.5, None, MUL)
                ins.then_inc(S("s_act"), 1)
            za = WK[:, 3 * WT:3 * WT + 5 * 256].rearrange("p (c n) -> p c n", n=256)
            zb = wk(5, D).rearrange("p (c n) -> p c n", n=256)

            def gate(zt, src):
                return stt(zt, zt, 1.0, src, ADD, MUL)
            for z in range(4):
                name = f"sza{z}"
                dve.wait_ge(S("z_th"), 2 * z + 1)
                gate(za[:, 0:4].rearrange("p (a c) n -> p a (c n)", a=2), pset(name)[:, 0:2, :])
                freed(gate(za[:, 4], pset(name)[:, 2, 0:256]), name)
                name = f"szb{z}"
                dve.wait_ge(S("z_th"), 2 * z + 2)
                gate(zb[:, 0:2].rearrange("p c n -> p (c n)"), pset(name)[:, 0, :])
                gate(zb[:, 2], pset(name)[:, 1, 0:256])
                freed(gate(zb[0:TS, 3], pset(name)[0:TS, 1, 256:512]), name)
            dve.memset(H_ssd, 0.0).then_inc(S("h_zero"), 1)
            dve.wait_ge(S("h_zero"), 1)

            def heads(ap):
                return ap.rearrange("p (h d) -> p h d", d=HD)

            def tile_sums(c):
                n = P if c < TT else TS
                le = m_le if c < TT else s_le
                dve.wait_ge(S("sc_exp"), c + 1)
                dve.tensor_tensor(WJ(c)[0:n], EC(c)[0:n, 16:32], DTK[0:n, 0, c, :], MUL).then_inc(S("wj"), 1)
                for g in range(2):
                    ins = dve.tensor_tensor(CBM[0:n, g * P:g * P + n], PM[0:n, g, 256:256 + n], le[:], MUL)
                ins.then_inc(S("cbm"), 1)

            def decay_steps(q):
                c, g = divmod(q, 2)
                n = P if c < TT else TS
                le = m_le if c < TT else s_le
                dve.tensor_tensor(RM(q), bc(DTK[0:n, 1, c, 8 * g:8 * g + 8], n), mid(le[:], 8), MUL)\
                    .then_inc(S("r"), 1)

            def matrices(q):
                c, g = divmod(q, 2)
                n = P if c < TT else TS
                dve.wait_ge(S("cbm"), c + 1)
                read(dve, f"ss{q}")
                dve.tensor_tensor(RM(q), RM(q), mid(CBM[0:n, g * P:g * P + n], 8), MUL).then_inc(S("m"), 1)

            def mark(ins):
                chain[0] += 1
                ins.then_inc(dve_chain, 1)
                return chain[0]

            def outputs(q):
                c, g = divmod(q, 2)
                n = P if c < TT else TS
                hs = slice(8 * g, 8 * g + 8)
                name = f"sy{q}"
                ready(dve, name)
                ps = pset(name)
                y = wk(4)[0:n, 512:1024]
                src = ps[0:n, 1, :] if c < TT else YI[g][0:n]
                y_state = mark(dve.tensor_tensor(heads(y), heads(src), bc(EC(c)[0:n, hs], HD), MUL))
                st = H_ssd[64 * g:64 * g + 64]
                if c < TT:
                    kept = mark(dve.tensor_tensor(heads(st), heads(st), bc(EL(c)[64 * g:64 * g + 64, hs], HD), MUL))
                dve.wait_ge(dve_chain, y_state)
                y_sum = mark(dve.tensor_tensor(y, y, ps[0:n, 0, :], ADD))
                if c < TT:
                    dve.wait_ge(dve_chain, kept)
                    freed(dve.tensor_tensor(st, st, ps[64 * g:64 * g + 64, 2, :], ADD), name)
                dve.wait_ge(S("xd"), q + 1)
                dve.wait_ge(dve_chain, y_sum)
                ins = dve.tensor_tensor(y, y, wk(3)[0:n, g * 512:(g + 1) * 512], ADD)
                if c < TT:
                    ins.then_inc(S("x_used"), 1)
                    dve.wait_ge(S("x_used"), q + 1)
                else:
                    freed(ins, name)
                    read(dve, name)
                dve.wait_ge(S("z_in"), 16 * (q + 1))
                dve.tensor_tensor(y, y, wk(4)[0:n, 0:512], MUL).then_inc(S("y_gated"), 1)

            def scale_y(q):
                n = P if q < 2 * TT else TS
                dve.wait_ge(S("y_std"), q + 1)
                y = wk(4)[0:n, 512:1024]
                sc = ST[0:n, 28 + q % 2:29 + q % 2]
                link(dve.reciprocal(sc, sc))
                dve.tensor_scalar(y, y, sc, 0.5, MUL, MUL).then_inc(S("y_norm"), 1)

            def split_y(q):
                c, g = divmod(q, 2)
                n = P if c < TT else TS
                name = f"sn{q}"
                ready(dve, name)
                if q:
                    dve.wait_ge(S("sy_lo"), q)
                yt = YT[:, 0:4 * n].rearrange("p (k t) -> p k t", k=4)
                freed(dve.tensor_tensor(yt, pset(name)[:, 0, :].rearrange("p (k t) -> p k t", k=4)[:, :, 0:n],
                                        PV[:, 4 * g:4 * g + 4, R_NSSD:R_NSSD + 1].broadcast_to([P, 4, n]), MUL),
                      name)
                dve.wait_ge(S("sy_hi"), q + 1)
                cols = slice(c * P, c * P + n)
                dve.tensor_tensor(Yl[:, 4 * g:4 * g + 4, cols], yt, Yh[:, 4 * g:4 * g + 4, cols].bitcast(F32),
                                  SUB).then_inc(S("sy_lo"), 1)
            for b in range(NB):
                ins = dve.tensor_scalar(DAB[0:TS, b * SH:(b + 1) * SH], DTK[0:TS, 1, TT, :], seqcol[:, b:b + 1],
                                        None, MUL)
            ins.then_inc(S("dab"), 1)
            decay_steps(0)
            tile_sums(0)
            decay_steps(1)
            matrices(0)
            for q in range(2 * TT):
                outputs(q)
                if q + 1 < 2 * TT:
                    matrices(q + 1)
                scale_y(q)
                if q % 2 == 0:
                    tile_sums(q // 2 + 1)
                if q + 2 < 2 * TT:
                    decay_steps(q + 2)
                split_y(q)
            dve.tensor_tensor(CZ, mid(wk(1)[:, LP:T], NB), seqm[:], MUL).then_inc(S("cz"), 1)
            decay_steps(2 * TT)
            for b in range(NB):
                if b >= 2:
                    ready(dve, f"ub{b - 2}")
                    ready(dve, f"uc{b - 2}")
                dve.tensor_scalar(wk(5 + b % 2, P, D)[0:TS], b_tok[0:TS, TT, :], seqcol[:, b:b + 1], None, MUL)\
                    .then_inc(S("bm"), 1)
                read(dve, f"si{b}")
                new = wk(2, 512, b % 2 * 512)
                for g in range(2):
                    r = slice(64 * g, 64 * g + 64)
                    kept = mark(dve.tensor_tensor(heads(new[r]), heads(wk(1, 512, b % 2 * 512)[r]),
                                                  bc(EL(TT)[r, b * SH + 8 * g:b * SH + 8 * g + 8], HD), MUL))
                dve.wait_ge(dve_chain, kept)
                ready(dve, f"ub{b}")
                freed(dve.tensor_tensor(new, new, pset(f"ub{b}")[:, 0, :], ADD), f"ub{b}")
            q = 2 * TT
            matrices(q)
            dve.wait_ge(S("si_mm"), NB)
            decay_steps(q + 1)
            for i in range(2):
                dve.wait_ge(S(f"h_put{i}"), 32 * 4)
            dve.wait_ge(S("yi"), 1)
            outputs(q)
            matrices(q + 1)
            scale_y(q)
            split_y(q)
            outputs(q + 1)
            scale_y(q + 1)
            split_y(q + 1)
            out_jobs(2)
            if stop < 4:
                return
            for k in range(DT):
                dve.wait_ge(S("mi_hi"), k + 1)
                dve.tensor_tensor(Hl[:, k], wk(k)[:, 0:T], Hh[:, k].bitcast(F32), SUB).then_inc(S("mi_lo"), 1)

            def norm(i, name, row, split):
                read(dve, name)
                link(dve.reciprocal(wk(6)[:, 0:T], wk(6)[:, 0:T]))
                for k in range(DT + 1):
                    if k < DT:
                        if split and k >= 2:
                            dve.wait_ge(S("nrm_lo"), i * DT + k - 1)
                        dst = wk(4 + k % 2)[:, 0:T] if split else X[:, k]
                        stt(dst, X[:, k], PV[:, k, row:row + 1], wk(6)[:, 0:T], MUL, MUL).then_inc(S("nrm_t"), 1)
                    if split and k:
                        dve.wait_ge(S("nrm_hi"), i * DT + k)
                        dve.tensor_tensor(Hl[:, k - 1], wk(4 + (k - 1) % 2)[:, 0:T], Hh[:, k - 1].bitcast(F32), SUB)\
                            .then_inc(S("nrm_lo"), 1)
            norm(0, "xn", R_NX, True)
            dve.wait_ge(S("mem_std"), 1)
            link(dve.reciprocal(ST[:, 30:32], ST[:, 30:32]))
            for i in range(2):
                dve.tensor_scalar(MV[:, i], MV[:, i], ST[:, 30 + i:31 + i], None, MUL).then_inc(S("mem_scaled"), 1)
            for i in range(2):
                name = f"mt{i}"
                ready(dve, name)
                if i:
                    dve.wait_ge(S("mem_lo"), i)
                for a in range(2):
                    ins = dve.tensor_tensor(wk(7, 512, a * 512).rearrange("p (k m) -> p k m", k=4),
                                            pset(name)[:, a, :].rearrange("p (k m) -> p k m", k=4),
                                            PV[:, 4 * a:4 * a + 4, R_NMEM:R_NMEM + 1].broadcast_to([P, 4, P]), MUL)
                    if a == 0:
                        link(ins)
                freed(ins, name)
                read(dve, name)
                dve.wait_ge(S("mem_hi"), i + 1)
                dve.tensor_tensor(MNl[:, :, i * P:(i + 1) * P], wk(7, D).rearrange("p (k m) -> p k m", k=DT),
                                  MNh[:, :, i * P:(i + 1) * P].bitcast(F32), SUB).then_inc(S("mem_lo"), 1)

            def maxima(c):
                n = P if c < TT else TS
                name = f"xs{c}"
                ready(dve, name)
                if c >= 2:
                    read(dve, f"xs{c - 2}")
                mx = ST[0:n, 32 + 4 * (c % 2):36 + 4 * (c % 2)]
                link(dve.tensor_reduce(mx, pset(name)[0:n, 0:2, :].rearrange("p a (h m) -> p (a h) m", h=2),
                                       AX_X, ALU.max))
                dve.tensor_scalar(mx, mx, -(XD ** -0.5), None, MUL).then_inc(S("x_max"), 1)

            def probs(c):
                n = P if c < TT else TS
                read(dve, f"xs{c}")
                sums = ST[0:n, 40 + 4 * (c % 2):44 + 4 * (c % 2)]
                link(dve.reciprocal(sums, sums))
                p = Pr(c)[0:n].rearrange("p (h m) -> p h m", h=XH)
                dve.tensor_tensor(p, p, bc(sums, M), MUL).then_inc(S("x_p"), 1)

            def outputs(c):
                n = P if c < TT else TS
                name = f"xv{c}"
                dve.wait_ge(S("xo_hi"), c + 1)
                for a in range(2):
                    cols = slice(c * P, c * P + n)
                    ins = dve.tensor_tensor(Hl[:, 4 * a:4 * a + 4, cols],
                                            pset(name)[:, a, :].rearrange("p (k t) -> p k t", k=4)[:, :, 0:n],
                                            Hh[:, 4 * a:4 * a + 4, cols].bitcast(F32), SUB)
                freed(ins, name)
            maxima(0)
            for c in range(TT):
                if c + 1 < TT:
                    maxima(c + 1)
                probs(c)
                outputs(c)
            link(dve.memset(WK[:, 6 * WT:6 * WT + 2 * DT * 120], 0.0))
            for b in range(NB):
                if b >= 2:
                    dve.wait_ge(S("kb_s"), 4 * (b - 1))
                dve.tensor_copy(QZb[:, b % 2, :, 56:56 + LS], Q[:, :, LP + LS * b:LP + LS * (b + 1)])\
                    .then_inc(S("qz"), 1)
            maxima(TT)
            probs(TT)
            outputs(TT)

            def add_to_x(name, t):
                ready(dve, name)
                for g, (t0, n) in enumerate(GROUPS):
                    ins = dve.tensor_tensor(X[:, t, t0:t0 + n], X[:, t, t0:t0 + n], pset(name)[:, g, 0:n], ADD)
                freed(ins, name)
            for t in range(DT):
                add_to_x(f"xo{t}", t)
            norm(1, "fn", R_NFFN, True)
            for c in range(FC + 1):
                for i in range(2 if c < FC else 0):
                    q = 2 * c + i
                    h = wk(q % 4)[:, 0:T]
                    dve.wait_ge(S("f_th"), q + 1)
                    name = f"fg{c}_{i}"
                    for g, (t0, n) in enumerate(GROUPS):
                        ins = stt(h[:, t0:t0 + n], h[:, t0:t0 + n], 1.0, pset(name)[:, g, 0:n], ADD, MUL)
                    freed(ins, name)
                    read(dve, name)
                    name = f"fu{c}_{i}"
                    ready(dve, name)
                    for g, (t0, n) in enumerate(GROUPS):
                        ins = stt(h[:, t0:t0 + n], h[:, t0:t0 + n], 0.5, pset(name)[:, g, 0:n], MUL, MUL)
                        if g < 2:
                            link(ins)
                    freed(ins, name)
                    read(dve, name)
                    dve.wait_ge(S("f_hi"), q + 1)
                    dve.tensor_tensor(Fl[:, c % 2, i], h, Fh[:, c % 2, i].bitcast(F32), SUB).then_inc(S("f_lo"), 1)
                if c:
                    for t in range(DT):
                        add_to_x(f"fd{c - 1}_{t}", t)
            norm(2, "yn", R_NFIN, False)


_OUTS = [("y_prompt", (1, LP, D)), ("y_sample", (NB, LS, D)), ("p_lru_h", (1, 1, D)), ("p_lru_conv", (1, 1, HIST, D)),
         ("p_gla_S", (1, 1, GH, DK, DV)), ("p_ssd_h", (1, 1, SH, HD, NS)), ("p_ssd_conv", (1, 1, HIST, SCC)),
         ("p_mem_k", (1, 1, M, XH, XD)), ("p_mem_v", (1, 1, M, XH, XD)), ("s_lru_h", (1, NB, D)),
         ("s_lru_conv", (1, NB, HIST, D)), ("s_gla_S", (1, NB, GH, DK, DV)), ("s_ssd_h", (1, NB, SH, HD, NS)),
         ("s_ssd_conv", (1, NB, HIST, SCC))]
_INS = ["x_prompt", "x_sample", "mem_prompt", "state_lru_h", "state_lru_conv", "state_gla_S", "state_ssd_h",
        "state_ssd_conv", "cache_mem_k", "cache_mem_v", "norm_mix", "w_in", "lru_conv_w", "lru_conv_b", "lru_wa",
        "lru_ba", "lru_wx", "lru_bx", "lru_lambda", "w_lru_out", "gla_w_alpha", "gla_b_alpha", "gla_norm",
        "w_gla_out", "ssd_conv_w", "ssd_conv_b", "ssd_dt_bias", "ssd_a_log", "ssd_d", "ssd_norm", "w_ssd_out",
        "w_mix_out", "norm_xattn", "norm_mem", "w_xq", "w_xk", "w_xv", "w_xo", "norm_ffn", "w_ffn_gate",
        "w_ffn_up", "w_ffn_down", "norm_final"]


def kernel(**inputs):
    import numpy as np
    import concourse.bacc as bacc
    from concourse.bass_utils import run_bass_kernel_spmd as run

    nc = bacc.Bacc("TRN2", target_bir_lowering=False, num_devices=1)
    arrays = {f"in_{name}": np.ascontiguousarray(inputs[name]) for name in _INS}
    ins = {name: nc.dram_tensor(f"in_{name}", arrays[f"in_{name}"].shape, F32, kind="ExternalInput").ap()
           for name in _INS}
    outs = {name: nc.dram_tensor(f"out_{name}", shape, F32, kind="ExternalOutput").ap() for name, shape in _OUTS}
    build(nc, ins, outs)
    r = run(nc, [arrays], core_ids=[0])
    return tuple(r.results[0][f"out_{name}"] for name, _ in _OUTS)
```

```python
from contextlib import ExitStack

import concourse.bass as bass
from concourse import mybir

F32 = mybir.dt.float32
F32R = mybir.dt.float32r
ALU = mybir.AluOpType
ACT = mybir.ActivationFunctionType
AX_X = mybir.AxisListType.X

P = 128
D = 1024
DT = D // P
LP = 1024
NB = 8
LS = 8
TS = NB * LS
T = LP + TS
TT = LP // P
GROUPS = [(0, 384), (384, 384), (768, 320)]
EPS = 1e-6
CW = 4
HIST = CW - 1
GH, DK, DV, GCH = 4, 128, 256, 64
SH, HD, NS = 16, 64, 64
SCC = D + 4 * NS
CT = SCC // P
M = 256
XH, XD = 4, 256
FF = 2816
FT = FF // P
FC = FT // 2
WT = 1152
SLOTS = 3
GELU_C = 0.7978845608028654

C_LX, C_LG, C_Q, C_K, C_V, C_R, C_LOW = 0, 1024, 2048, 2560, 3072, 4096, 5120
C_Z, C_XBC, C_DT, C_GATE = 5136, 6160, 7440, 7456

R_CONV, R_H0, R_CW, R_CB, R_BA, R_BX, R_LAM = 0, 24, 32, 36, 37, 38, 39
R_NMIX, R_NX, R_NFFN, R_NFIN, R_NMEM, R_NSSD, R_GLA, NROW = 40, 41, 42, 43, 44, 45, 46, 47
Q_CONV, Q_CW, Q_CB, QROW = 0, 24, 28, 29


def plan():
    w, jobs = [], ["pk0", "pk1"] + [f"xt{c}" for c in range(TT + 1)]

    def use(tiles, *names):
        jobs.extend(names)
        if len(tiles) == 2 and len(w) % SLOTS == SLOTS - 1:
            tiles = tiles[::-1]
        w.extend((*tile, names[-1]) for tile in tiles)

    def out_jobs(b, name):
        for t in range(DT):
            if b < 2 or t:
                use([("in", C_GATE + b * D + t * P)], f"og{b}_{t}")
            use([(name, t * P)], f"ob{b}_{t}")

    for t in range(DT):
        use([("in", C_LX + t * P)], f"lx{t}")
        use([("in", C_LG + t * P)], f"lg{t}")
        jobs.extend([f"lr{t}", f"li{t}"])
    use([("in", C_LOW)], "low")
    use([("in", C_DT)], "dt")
    jobs.append("lt")
    out_jobs(0, "lru_out")
    for h in range(GH):
        jobs.append(f"ga{h}")
        use([("in", C_Q + h * P)], f"gq{h}")
        use([("in", C_K + h * P)], f"gk{h}")
        for v in range(2):
            use([("in", C_R + h * DV + v * P)], f"gr{h}_{v}")
        use([("in", C_V + h * DV), ("in", C_V + h * DV + P)], f"gva{h}", f"gvb{h}")
        jobs.append(f"gt{h}")
        jobs.extend(f"go{h}_{c}" for c in range(TT + 1))
    out_jobs(1, "gla_out")
    jobs.append("dtt")
    for t in range(CT):
        use([("in", C_XBC + t * P)], f"sx{t}")
        if t:
            jobs.append(f"st{t - 1}")
    for t in range(DT):
        use([("in", C_Z + t * P)], f"sz{t}")
        jobs.append(f"zt{t - 1}" if t else "qt")
    jobs.append(f"zt{DT - 1}")
    jobs.extend(["ss0", "ss1"])
    for q in range(2 * TT):
        jobs.extend([f"sy{q}"] + ([f"ss{q + 2}"] if q + 2 < 2 * TT else []))
    jobs.extend(["po", "si0"])
    for b in range(NB):
        jobs.extend([f"ub{b}"] + ([f"si{b + 1}"] if b + 1 < NB else []) + [f"uc{b}"])
    q = 2 * TT
    jobs.extend([f"ss{q}", f"ss{q + 1}", f"sy{q}", f"sy{q + 1}"])
    use([("in", C_GATE + 2 * D)], "og2_0")
    out_jobs(2, "ssd_out")
    for t in range(DT):
        use([("mix", t * P)], f"mx{t}")
        if t in (4, 5):
            jobs.append(f"mt{t - 4}")
    for t in range(DT):
        use([("xk", t * P)], f"mk{t}")
        if t == 1:
            jobs.append("xn")
        if t == 6:
            jobs.append("kt0")
    for t in range(DT):
        use([("xv", t * P)], f"mv{t}")
        if t == 1:
            jobs.append("kt1")
        if t == 3:
            jobs.append("vt0")
    jobs.append("vt1")
    for t in range(DT):
        use([("xq", t * P)], f"xq{t}")
    jobs.append("xs0")
    for c in range(TT):
        jobs.extend([f"xp{c}"] + ([f"xs{c + 1}"] if c + 1 < TT else []) + [f"xv{c}"])
    jobs.extend([f"xs{TT}", f"xp{TT}", f"xv{TT}", "xw"])
    for t in range(DT):
        use([("xo", t * P)], f"xo{t}")
    jobs.append("fn")
    for c in range(FC + 1):
        for i in range(2 if c < FC else 0):
            use([("fg", (2 * c + i) * P)], f"fg{c}_{i}")
            use([("fu", (2 * c + i) * P)], f"fu{c}_{i}")
        for i in range(2 if c else 0):
            use([("fd", (c - 1, i))], *(f"fd{c - 1}_{t}" for t in range(4 * i, 4 * i + 4)))
    jobs.extend(f"yt{c}" for c in range(TT + 1))
    return w, jobs


WLIST, JOBS = plan()
JOB = {name: n for n, name in enumerate(JOBS)}
FIRST_W = {}
for _n, _tile in enumerate(WLIST):
    FIRST_W.setdefault(_tile[:2], _n)


def build(nc, ins, outs):
    I, O = ins, outs
    ctx = ExitStack()
    with ctx:
        def sb(name, shape, dt=F32):
            return ctx.enter_context(nc.sbuf_tensor(name, shape, dt))

        def sem(name):
            return ctx.enter_context(nc.semaphore(name))

        base = -(-nc.sbuf_base // 32) * 32
        arena = sb("arena", [P, (4 * DT * T) + SLOTS * DT * P + 8])

        def at(name, shape, dt, offset):
            return nc.alloc_sbuf_tensor_at(name, shape, dt, offset=base + offset)

        HALF = 4 * DT * T
        Hh = at("Hh", [P, DT, T], F32R, 0)
        Hl = at("Hl", [P, DT, T], F32R, HALF)
        Yh = at("Yh", [P, DT, T], F32R, 2 * HALF)
        Yl = at("Yl", [P, DT, T], F32R, 3 * HALF)
        YA = at("YA", [P, 2 * DT, T], F32, 2 * HALF)
        X = at("X", [P, DT, T], F32, 2 * HALF)
        XT = at("XT", [P, 2, TT + 1, P], F32, 3 * HALF + 24 * D)
        MNh = at("MNh", [P, DT, M], F32R, 3 * HALF)
        MNl = at("MNl", [P, DT, M], F32R, 3 * HALF + 4 * DT * M)
        KM = at("KM", [P, 2, D], F32, 3 * HALF + 8 * DT * M)
        Q = at("Q", [P, DT, T], F32, 3 * HALF)
        Fh = at("Fh", [P, 2, 2, T], F32R, 3 * HALF)
        Fl = at("Fl", [P, 2, 2, T], F32R, 3 * HALF + 16 * T)
        Wh = sb("Wh", [P, SLOTS, DT, P], F32R)
        Wr = at("Wr", [P, SLOTS, DT, P], F32, 4 * HALF)
        Wl = at("Wl", [P, SLOTS, DT, P], F32R, 4 * HALF)
        WK = sb("WK", [P, 8 * WT])
        ident = sb("ident", [P, P])
        ones = sb("ones", [P, P])
        m_le = sb("m_le", [P, P])
        m_gt = sb("m_gt", [P, P])
        m_ch = sb("m_ch", [P, P])
        s_le = sb("s_le", [TS, TS])
        s_gt = sb("s_gt", [TS, TS])
        seqcol = sb("seqcol", [TS, NB])
        seqm = sb("seqm", [P, NB, TS], mybir.dt.bfloat16)
        YT = sb("YT", [P, T // 2])
        rmask = YT[:].bitcast(mybir.dt.bfloat16)
        PV = sb("PV", [P, DT, NROW])
        PQ = sb("PQ", [P, CT, QROW])
        SC = sb("SC", [P, DT, 3])
        CB = sb("CB", [P, DT, 36])
        CQ = sb("CQ", [P, CT, 27])
        NSC = sb("NSC", [P, DT])
        LAM = sb("LAM", [P, 4, DT])
        EPSC = sb("EPSC", [P, 1])
        ST = sb("ST", [P, 48])

        def wk(i, n=WT, off=0):
            return WK[:, i * WT + off:i * WT + off + n]

        PS = ctx.enter_context(nc.psum_tensor("PS", [P, 2, 3, 512], F32))
        PM = ctx.enter_context(nc.psum_tensor("PM", [P, 2, 512], F32))

        DTK = wk(7, 288).rearrange("p (s c h) -> p s c h", s=2, c=TT + 1)
        H_ssd = wk(7, 512, 288)
        CBM = wk(7, 256, 800)
        DBC = wk(7, SH, 1056)
        DTB, ALOG = wk(7, SH, 1072), wk(7, SH, 1088)
        DAB = wk(6, 128, D)
        CZ = wk(6, 512).rearrange("p (b t) -> p b t", b=NB)
        YI = [wk(7, 512, 288), wk(0, 512)]
        Yhf = at("Yhf", [P, DT, T], F32, 2 * HALF)
        Ylf = at("Ylf", [P, DT, T], F32, 3 * HALF)

        def XS(c):
            return wk(2 + c % 3, D, P if c % 3 == 0 else 0)

        def MI(k):
            return wk((6, 7, 2)[k % 3] if k < DT - 2 else 4 + k % 2)[:, 0:T]

        def EC(c):
            return wk(4, 32, D + 48 * (c % 2))

        def WJ(c):
            return wk(4, 16, D + 48 * (c % 2) + 32)

        def EL(c):
            return wk(4, 16, D + 96 + 16 * (c % 2)) if c < TT else wk(3, 128, D)

        def YZ(q):
            return wk(4, 512, q % 2 * 512)[0:P if q < 2 * TT else TS]

        def RM(q):
            c, g = divmod(q, 2)
            n = P if c < TT else TS
            if g == 0:
                return Ylf[0:n, :, c * P:c * P + n]
            return wk(6)[0:n, 0:8 * n].rearrange("p (h i) -> p h i", h=8)

        def pairs(ap):
            return ap.rearrange("p (k a d) -> p k a d", k=4, a=2)

        def XDT(q):
            c, g = divmod(q, 2)
            if g == 0 and c < TT:
                return Yhf[:, 0:4, c * P:(c + 1) * P].rearrange("p k (a d) -> p k a d", a=2)
            if g == 0:
                return Yhf[0:TS, :, LP:T].rearrange("p (k a) d -> p k a d", a=2)
            return pairs(wk(5, 512)) if c < TT else pairs(wk(1, 512)[0:TS])

        def XW(q):
            c, g = divmod(q, 2)
            if g == 0:
                return Yhf[:, 4:8, c * P:(c + 1) * P]
            return wk(5, 512, 512).rearrange("p (k w) -> p k w", k=4)

        VF = wk(7, D).rearrange("p (k m) -> p k m", k=4)
        MV = WK[:, 2 * WT:2 * WT + 2 * D].rearrange("p (m f) -> p m f", m=2)
        KT_m = WK[:, 0:DT * M].rearrange("p (k m) -> p k m", k=DT)
        KVb = [WK[:, i * 2 * WT:i * 2 * WT + 2 * D].rearrange("p (m f) -> p m f", m=2) for i in range(2)]
        KTb = WK[:, 4 * WT:4 * WT + DT * M].rearrange("p (k m) -> p k m", k=DT)
        PZb = WK[:, 4 * WT:4 * WT + 2 * DT * 120].rearrange("p (a k t) -> p a k t", a=2, k=DT)
        QZb = WK[:, 6 * WT:6 * WT + 2 * DT * 120].rearrange("p (a k t) -> p a k t", a=2, k=DT)

        def Pr(c):
            return wk(4 + c % 2 if c < TT else 6, D)

        def PrT(c):
            return wk(6 + c % 2 if c < TT else 7, D).rearrange("p (k t) -> p k t", k=DT)

        merged = nc.dram_tensor("merged", (3, DT, P, T), F32, kind="Internal").ap()
        dt_scr = nc.dram_tensor("dt_scr", (SH, T), F32, kind="Internal").ap()
        x_scr = nc.dram_tensor("x_scr", ((TT + 1) * P, D), F32, kind="Internal").ap()
        z_scr = nc.dram_tensor("z_scr", ((TT + 1) * P, D), F32, kind="Internal").ap()

        ps_ready = [sem("ps_ready0"), sem("ps_ready1")]
        ps_free = [sem("ps_free0"), sem("ps_free1")]
        w_loaded = [sem(f"w_loaded{i}") for i in range(SLOTS)]
        w_split = sem("w_split")
        w_hi = sem("w_hi")
        masks = sem("masks")
        act_chain = sem("act_chain")
        dve_chain = sem("dve_chain")
        packs = sem("packs")
        packs_zero = sem("packs_zero")
        stored = sem("stored")
        pack_cols = sem("pack_cols")
        NMASK = 25
        NPACK = 18
        NW = len(WLIST)

        def ready(eng, name):
            n = JOB[name]
            eng.wait_ge(ps_ready[n % 2], n // 2 + 1)

        def read(eng, name):
            n = JOB[name]
            eng.wait_ge(ps_free[n % 2], n // 2 + 1)

        def free_set(eng, name):
            n = JOB[name]
            if n >= 2:
                eng.wait_ge(ps_free[n % 2], n // 2)

        def branch_done(eng, b):
            if b == 0:
                eng.wait_ge(S("y_lo"), DT)
            elif b == 1:
                eng.wait_ge(S("gy_lo"), GH)
            else:
                eng.wait_ge(S("sy_lo"), 2 * (TT + 1))

        def sum_stored(eng, b, t):
            eng.wait_ge(S(f"m_put{t % 2}"), 16 * (b * DT // 2 + t // 2 + 1))

        def gla_state_in(eng, h, b):
            eng.wait_ge(S(f"sb_in{b % 3}"), 16 * (h * (3, 3, 2)[b % 3] + b // 3 + 1))

        def pset(name):
            return PS[:, JOB[name] % 2]

        def done(ins, name):
            ins.then_inc(ps_ready[JOB[name] % 2], 1)

        def freed(ins, name):
            ins.then_inc(ps_free[JOB[name] % 2], 1)

        n_stores = [0]
        sems = {}

        def S(name):
            if name not in sems:
                sems[name] = sem(name)
            return sems[name]

        def seqs(ap):
            return ap[:, LP:T].rearrange("p (b l) -> p b l", b=NB)

        def bc(ap, n):
            return ap.unsqueeze(2).broadcast_to([ap.shape[0], ap.shape[1], n])

        def mid(ap, n):
            return ap.unsqueeze(1).broadcast_to([ap.shape[0], n, ap.shape[1]])

        block = ctx.enter_context(nc.Block())

        @block.sync
        def _(sp):
            src = {"in": "w_in", "lru_out": "w_lru_out", "gla_out": "w_gla_out", "ssd_out": "w_ssd_out",
                   "mix": "w_mix_out", "xk": "w_xk", "xv": "w_xv", "xq": "w_xq", "xo": "w_xo",
                   "fg": "w_ffn_gate", "fu": "w_ffn_up"}
            for n, (kind, col, _) in enumerate(WLIST):
                if n >= SLOTS:
                    ready(sp, WLIST[n - SLOTS][2])
                if kind == "fd":
                    c, half = col
                    tile = I["w_ffn_down"][0, 2 * c * P:(2 * c + 2) * P, half * 512:half * 512 + 512]
                    dst = Wr[:, n % SLOTS].rearrange("p (k a) m -> p k (a m)", k=2)
                    sp.dma_start(dst, tile.rearrange("(k p) m -> p k m", p=P)).then_inc(w_loaded[n % SLOTS], 16)
                else:
                    tile = I[src[kind]][0, :, col:col + P]
                    sp.dma_start(Wr[:, n % SLOTS], tile.rearrange("(k p) m -> p k m", p=P)).then_inc(w_loaded[n % SLOTS], 16)

        @block.gpsimd
        def _(pool):
            chain = [0]

            def link(ins):
                chain[0] += 1
                ins.then_inc(masks, 1)
                pool.wait_ge(masks, chain[0])

            def select(tile, compare, pattern, base, cm, fill=0.0):
                link(pool.affine_select(out=tile, in_=tile, pattern=pattern, compare_op=compare, fill=fill,
                                        base=base, channel_multiplier=cm))

            GE = ALU.is_ge
            link(pool.memset(ident[:], 0.0))
            select(ident[:], ALU.not_equal, [[-1, P]], 0, 1, 1.0)
            for tile in (ones, m_le, m_gt, m_ch, s_le, s_gt, seqcol, seqm):
                link(pool.memset(tile[:], 1.0))
            link(pool.memset(rmask, 1.0))
            select(m_le[:], GE, [[1, P]], 0, -1)
            select(m_gt[:], GE, [[-1, P]], -1, 1)
            select(m_ch[:], GE, [[1, P]], 0, -1)
            ch = m_ch[:].rearrange("p (a c) -> p a c", a=2)
            select(ch, GE, [[-GCH, 2], [0, GCH]], 0, 1)
            sl = s_le[:].rearrange("p (b c) -> p b c", b=NB)
            select(sl, GE, [[LS, NB], [1, LS]], 0, -1)
            select(sl, GE, [[-LS, NB], [0, LS]], 0, 1)
            sg = s_gt[:].rearrange("p (b c) -> p b c", b=NB)
            select(sg, GE, [[-LS, NB], [-1, LS]], -1, 1)
            select(sg, GE, [[LS, NB], [0, LS]], LS - 1, -1)
            select(seqcol[:], GE, [[-LS, NB]], 0, 1)
            select(seqcol[:], GE, [[LS, NB]], LS - 1, -1)
            select(seqm[:], GE, [[-LS, NB], [1, TS]], 0, 0)
            select(seqm[:], GE, [[LS, NB], [-1, TS]], LS - 1, 0)
            link(pool.memset(rmask[:, 0:LP].rearrange("p (a c) -> p a c", c=GCH)[:, :, 0:1], 0.0))
            link(pool.memset(seqs(rmask)[:, :, 0:1], 0.0))
            assert chain[0] == NMASK, chain[0]
            splits = [0]

            def split_to(end):
                for n in range(splits[0], min(end, NW)):
                    pool.wait_ge(w_loaded[n % SLOTS], 16 * (n // SLOTS + 1))
                    if WLIST[n][0] not in ("xk", "xv"):
                        pool.tensor_copy(Wh[:, n % SLOTS], Wr[:, n % SLOTS]).then_inc(w_hi, 1)
                    pool.wait_ge(w_hi, n + 1)
                    pool.tensor_tensor(Wl[:, n % SLOTS], Wr[:, n % SLOTS], Wh[:, n % SLOTS].bitcast(F32),
                                       ALU.subtract).then_inc(w_split, 1)
                splits[0] = max(splits[0], end)

            split_to(FIRST_W["in", C_Z + 7 * P] + 1 + SLOTS)

            def weight_x(q, part=None):
                c, g = divmod(q, 2)
                n = P if c < TT else TS
                dt = DTK[0:n, 0, c, :]
                x = pairs(wk(3)[0:n, g * 512:(g + 1) * 512])

                def per_head(ap):
                    ap = ap[0:n, 8 * g:8 * g + 8].rearrange("p (k a) -> p k a", a=2)
                    return ap.unsqueeze(3).broadcast_to([n, 4, 2, HD])
                if part != "skip":
                    pool.wait_ge(S(f"xs_in{g}"), 16 * (c + 1))
                    pool.wait_ge(S("wj"), c + 1)
                if part != "skip" and c < TT:
                    if q >= 2:
                        ready(pool, f"sy{q - 2}")
                    pool.tensor_tensor(XW(q).rearrange("p k (a d) -> p k a d", a=2), x, per_head(WJ(c)), ALU.mult)
                elif part != "skip":
                    dst = pairs(wk(5)[0:TS, g * 512:(g + 1) * 512])
                    pool.tensor_tensor(dst, x, per_head(WJ(c)), ALU.mult).then_inc(S("wx2"), 1)
                if part != "state":
                    pool.tensor_tensor(XDT(q), x, per_head(dt), ALU.mult).then_inc(S("xdt"), 1)
                    pool.wait_ge(S("xdt"), q + 1)
                    pool.tensor_tensor(x, x, per_head(DBC), ALU.mult).then_inc(S("xd"), 1)

            weight_x(0)
            weight_x(1)
            for q in range(2, 2 * TT):
                weight_x(q)
            q = 2 * TT
            ready(pool, f"sy{q - 1}")
            weight_x(q, "state")
            weight_x(q + 1, "state")
            pool.wait_ge(S("wx2"), 2)
            weight_x(q, "skip")
            pool.wait_ge(S("si_mm"), NB)
            read(pool, f"ub{NB - 1}")
            weight_x(q + 1, "skip")
            split_to(NW)

        @block.tensor
        def _(pe):
            def project(name, w, Rh, Rl, by_tile=None, last=True):
                pe.wait_ge(w_split, w + 1)
                free_set(pe, name)
                for k in range(DT):
                    if by_tile:
                        pe.wait_ge(S(by_tile[0]), by_tile[1] + k + 1)
                    for i, (L, R) in enumerate(((Wh, Rh), (Wh, Rl), (Wl, Rh))):
                        for g, (t0, n) in enumerate(GROUPS):
                            mm = pe.matmul(pset(name)[:, g, 0:n], L[:, w % SLOTS, k, :], R[:, k, t0:t0 + n],
                                           start=(k == 0 and i == 0), stop=(last and k == DT - 1 and i == 2),
                                           skip_group_check=not last)
                return mm

            def project_tokens(name, w, tiles, Ah=Hh, Al=Hl):
                pe.wait_ge(w_split, w + 2)
                free_set(pe, name)
                slots = slice(w % SLOTS, w % SLOTS + 2) if w % SLOTS < SLOTS - 1 else slice(0, SLOTS, SLOTS - 1)
                for j, c in enumerate(tiles):
                    n = P if c < TT else TS
                    for k in range(DT):
                        for i, (A, W) in enumerate(((Ah, Wh), (Al, Wh), (Ah, Wl))):
                            mm = pe.matmul(pset(name)[0:n, j // 2, (j % 2) * 256:(j % 2) * 256 + 256]
                                           .rearrange("p (a m) -> p a m", a=2),
                                           A[:, k, c * P:c * P + n], W[:, slots, k, :],
                                           start=(k == 0 and i == 0), stop=(k == DT - 1 and i == 2))
                return mm

            def turn(out, in_, n):
                return pe.transpose(out, in_, ident[0:n, 0:n])

            def fp32_all(name, lhsT, rhs):
                for g, (t0, n) in enumerate(GROUPS):
                    mm = pe.matmul(pset(name)[:, g, 0:n], lhsT, rhs[:, t0:t0 + n], start=True, stop=True)
                return mm

            def out_jobs(b, kind):
                for t in range(DT):
                    if b < 2 or t:
                        done(project(f"og{b}_{t}", FIRST_W["in", C_GATE + b * D + t * P], Hh, Hl), f"og{b}_{t}")
                    if t == 0:
                        branch_done(pe, b)
                    done(project(f"ob{b}_{t}", FIRST_W[kind, t * P], Yh, Yl), f"ob{b}_{t}")

            pe.wait_ge(masks, NMASK)
            pe.wait_ge(packs, 16 * NPACK)
            for k in range(DT):
                mm = turn(pset("pk0")[:, 0, k * NROW:(k + 1) * NROW], wk(0)[0:NROW, k * P:(k + 1) * P], NROW)
            done(mm, "pk0")
            for k in range(CT):
                mm = turn(pset("pk1")[:, 0, k * QROW:(k + 1) * QROW], WK[0:QROW, WT + k * P:WT + (k + 1) * P], QROW)
            done(mm, "pk1")
            for c in range(TT + 1):
                n = P if c < TT else TS
                pe.wait_ge(S("x_scaled"), c + 1)
                free_set(pe, f"xt{c}")
                for k in range(DT):
                    mm = turn(pset(f"xt{c}")[:, k // 4, (k % 4) * P:(k % 4) * P + n],
                              wk(5 + c % 2)[0:n, k * P:(k + 1) * P], n)
                done(mm, f"xt{c}")
            pe.wait_ge(w_split, 2)
            free_set(pe, "lx0")
            free_set(pe, "lg0")
            for g, (t0, n) in enumerate(GROUPS):
                pe.wait_ge(S("h_lo"), min(3 * g + 3, TT + 1))
                for w, name in enumerate(("lx0", "lg0")):
                    for k in range(DT):
                        for i, (L, R) in enumerate(((Wh, Hh), (Wh, Hl), (Wl, Hh))):
                            mm = pe.matmul(pset(name)[:, g, 0:n], L[:, w, k, :], R[:, k, t0:t0 + n],
                                           start=(k == 0 and i == 0), stop=(k == DT - 1 and i == 2))
                    if g == len(GROUPS) - 1:
                        done(mm, name)
            for t in range(DT):
                if t:
                    done(project(f"lx{t}", FIRST_W["in", C_LX + t * P], Hh, Hl), f"lx{t}")
                    done(project(f"lg{t}", FIRST_W["in", C_LG + t * P], Hh, Hl), f"lg{t}")
                if t == 0:
                    pe.wait_ge(S("wax"), 64)
                pe.wait_ge(S("conv"), t + 1)
                for name, off in ((f"lr{t}", 0), (f"li{t}", P)):
                    free_set(pe, name)
                    done(fp32_all(name, YA[:, DT + t, off:off + P], wk(1)), name)
            done(project("low", FIRST_W["in", C_LOW], Hh, Hl), "low")
            done(project("dt", FIRST_W["in", C_DT], Hh, Hl), "dt")
            pe.wait_ge(S("cb"), DT)
            free_set(pe, "lt")
            for k in range(DT):
                mm = turn(pset("lt")[0:36, k // 4, (k % 4) * P:(k % 4 + 1) * P], CB[:, k, :], P)
            done(mm, "lt")
            out_jobs(0, "lru_out")
            V = WK[:, 6 * WT:8 * WT].rearrange("p (c v) -> p c v", c=TT + 1)
            KEt = wk(1).rearrange("p (c d) -> p c d", c=TT + 1)
            QT, KT = wk(0)[:, 0:T], wk(4)[:, 0:T]

            def log_gates(h):
                name = f"ga{h}"
                read(pe, "low")
                pe.wait_ge(S(f"wal{h % 2}"), 16 * (h // 2 + 1))
                free_set(pe, name)
                done(fp32_all(name, CB[0:16].rearrange("p k c -> p (k c)")[:, h % 2 * P:h % 2 * P + P],
                              wk(3)[0:16]), name)
            log_gates(0)
            for h in range(GH):
                A = [YA[:, i] for i in (2 * h, 2 * h + 1, DT + 2 * h, DT + 2 * h + 1)]
                done(project(f"gq{h}", FIRST_W["in", C_Q + h * P], Hh, Hl), f"gq{h}")
                done(project(f"gk{h}", FIRST_W["in", C_K + h * P], Hh, Hl), f"gk{h}")
                for v in range(2):
                    done(project(f"gr{h}_{v}", FIRST_W["in", C_R + h * DV + v * P], Hh, Hl), f"gr{h}_{v}")
                wv = min(FIRST_W["in", C_V + h * DV], FIRST_W["in", C_V + h * DV + P])
                done(project_tokens(f"gva{h}", wv, range(0, 5)), f"gva{h}")
                done(project_tokens(f"gvb{h}", wv, range(5, TT + 1)), f"gvb{h}")
                name = f"gt{h}"
                pe.wait_ge(S("ke"), h + 1)
                free_set(pe, name)
                for c in range(TT + 1):
                    n = P if c < TT else TS
                    mm = turn(pset(name)[0:n, c // 4, (c % 4) * P:(c % 4 + 1) * P], A[0][:, c * P:c * P + n], P)
                done(mm, name)
                att = lambda c: A[1][:, c % 2 * P:c % 2 * P + P]
                on = lambda c: A[1][:, 256 + c % 2 * DV:256 + (c % 2 + 1) * DV]
                St = lambda c: A[2][:, c % 2 * DV:(c % 2 + 1) * DV]
                QZ = A[2][:, 512:1024].rearrange("p (b t) -> p b t", b=NB)
                KEm = A[0][0:TS, 0:D].rearrange("p (b d) -> p b d", b=NB)
                Sb = lambda b: A[3][:, b % 3 * DV:(b % 3 + 1) * DV] if b % 3 < 2 else A[1][:, 768:1024]

                def turn_o(c):
                    n = P if c < TT else TS
                    q = h * (TT + 1) + c
                    read(pe, f"go{h}_{c}")
                    if q:
                        pe.wait_ge(S("ymul"), q)
                    for v in range(2):
                        mm = turn(PM[:, 1, v * P:v * P + n],
                                  on(c)[0:n, v * P:(v + 1) * P], n)
                    mm.then_inc(S("ot"), 1)
                read(pe, f"gt{h}")
                read(pe, f"gvb{h}")
                for c in range(TT + 1):
                    n = P if c < TT else TS
                    name = f"go{h}_{c}"
                    q = h * (TT + 1) + c
                    free_set(pe, name)
                    cols = slice(c * P, c * P + n)
                    pe.matmul(pset(name)[0:n, 1, 0:n], KT[:, cols], QT[:, cols], start=True, stop=True)\
                        .then_inc(S("att"), 1)
                    if c < TT:
                        for i in range(2):
                            e = h * 24 + 2 * c + i
                            if i == 0 and e >= 2:
                                pe.wait_ge(S("s_upd"), e - 1)
                            pe.matmul(PM[:, 0, 0:256] if i == 0 else pset(name)[:, 2, 0:256],
                                      KEt[64 * i:64 * i + 64, c, :], V[64 * i:64 * i + 64, c, :],
                                      start=True, stop=True).then_inc(S("ds"), 1)
                        pe.wait_ge(S("att_m"), q + 1)
                        pe.matmul(pset(name)[:, 0, 0:DV], att(c), V[:, c, :], start=True, stop=False,
                                  skip_group_check=True)
                        for i in range(2):
                            e = h * 24 + 2 * c + i
                            if c == 0 and i == 0:
                                pe.wait_ge(S("s_zero"), h + 1)
                            else:
                                pe.wait_ge(S("s_upd"), e)
                            mm = pe.matmul(pset(name)[64 * i:64 * i + 64, 0, 0:DV],
                                           QT[:, c * P + 64 * i:c * P + 64 * i + 64], St(e),
                                           start=False, stop=True, skip_group_check=True)
                            if i == 0:
                                mm.then_inc(S("inter"), 1)
                    else:
                        pe.wait_ge(S("att_m"), q + 1)
                        pe.matmul(pset(name)[0:n, 0, 0:DV], att(c)[0:n, 0:n], V[0:n, c, :], start=True, stop=False,
                                  skip_group_check=True)
                        pe.wait_ge(S("kem"), h + 1)
                        for b in range(NB):
                            e = h * 24 + 16 + b
                            pe.wait_ge(S("s_upd"), e - 1)
                            pe.matmul(PM[:, 0, 0:256] if b % 2 == 0 else pset(name)[:, 2, 0:256], KEm[:, b, :], V[0:TS, c, :],
                                      start=True, stop=True).then_inc(S("ds"), 1)
                            gla_state_in(pe, h, b)
                            mm = pe.matmul(pset(name)[0:n, 0, 0:DV], QZ[:, b, :], Sb(b), start=False,
                                           stop=(b == NB - 1), skip_group_check=True)
                            if b < NB - 1:
                                mm.then_inc(S("sb_int"), 1)
                    done(mm, name)
                    if c:
                        turn_o(c - 1)
                if h + 1 < GH:
                    log_gates(h + 1)
                turn_o(TT)
            out_jobs(1, "gla_out")
            bT, cT = wk(0), wk(1)
            b_tok = wk(2).rearrange("p (c n) -> p c n", c=TT + 1)
            pe.wait_ge(S("dt_in"), 64)
            free_set(pe, "dtt")
            for c in range(TT + 1):
                n = P if c < TT else TS
                mm = turn(pset("dtt")[0:n, 0, c * SH:(c + 1) * SH], wk(6)[0:SH, c * P:c * P + n], SH)
            done(mm, "dtt")

            def turn_tile(name, src):
                free_set(pe, name)
                for c in range(TT + 1):
                    n = P if c < TT else TS
                    mm = turn(pset(name)[0:n, c // 4, (c % 4) * P:(c % 4 + 1) * P], src[:, c * P:c * P + n], P)
                done(mm, name)
            for t in range(CT):
                done(project(f"sx{t}", FIRST_W["in", C_XBC + t * P], Hh, Hl), f"sx{t}")
                if t:
                    pe.wait_ge(S("s_act"), t)
                    turn_tile(f"st{t - 1}", wk(4) if t - 1 < DT else bT)
            for t in range(DT + 1):
                if t < DT:
                    done(project(f"sz{t}", FIRST_W["in", C_Z + t * P], Hh, Hl), f"sz{t}")
                if t:
                    read(pe, f"sz{t - 1}")
                    turn_tile(f"zt{t - 1}", wk(3 + (t - 1) % 2))
                else:
                    free_set(pe, "qt")
                    pe.wait_ge(S("sconv"), CT)
                    for k in range(CT):
                        mm = turn(pset("qt")[0:27, k // 4, (k % 4) * P:(k % 4 + 1) * P], CQ[:, k, :], P)
                    done(mm, "qt")

            def sums(c):
                n = P if c < TT else TS
                cols = slice(c * P, c * P + n)
                le, gt = (m_le, m_gt) if c < TT else (s_le, s_gt)
                da = DTK[0:n, 1, c, :]
                if c == 0:
                    pe.wait_ge(S("s_act"), CT)
                    pe.wait_ge(S("dt_done"), 1)
                    read(pe, f"st{CT - 2}")
                else:
                    pe.wait_ge(S("sc_exp"), c)
                    pe.wait_ge(S("cbm"), c)

                def c_dot_b(g):
                    return pe.matmul(PM[0:n, 0, 160 + g * P:160 + g * P + n], bT[64 * g:64 * g + 64, cols],
                                     cT[64 * g:64 * g + 64, cols], start=True, stop=True)
                c_dot_b(0)
                pe.matmul(PM[0:n, 0, 0:16], le[:], da, start=True, stop=True)
                pe.matmul(PM[0:n, 0, 16:32], gt[:], da, start=True, stop=True)
                if c < TT:
                    pe.matmul(PM[:, 0, 32:48], ones[:], da, start=True, stop=True).then_inc(S("cb0"), 1)
                else:
                    pe.wait_ge(S("dab"), 1)
                    pe.matmul(PM[:, 0, 32:160], ones[0:n], DAB[0:n], start=True, stop=True)\
                        .then_inc(S("cb0"), 1)
                pe.wait_ge(S("cb0"), c + 1)
                c_dot_b(1).then_inc(S("sums"), 1)

            def decays(q):
                n = P if q < 2 * TT else TS
                gt = m_gt if q < 2 * TT else s_gt
                name = f"ss{q}"
                pe.wait_ge(S("r"), q + 1)
                free_set(pe, name)
                m = 512 // n
                for i in range(8 // m):
                    mm = pe.matmul(pset(name)[0:n, i, :].rearrange("p (h i) -> p h i", i=n), gt[:],
                                   RM(q)[:, i * m:(i + 1) * m], start=True, stop=True)
                done(mm, name)

            def products(q):
                c, g = divmod(q, 2)
                n = P if c < TT else TS
                cols = slice(c * P, c * P + n)
                name = f"sy{q}"
                pe.wait_ge(S("m"), q + 1)
                pe.wait_ge(S("xdt"), q + 1)
                free_set(pe, name)
                ps = pset(name)
                if c < TT:
                    if q >= 2:
                        read(pe, f"sy{q - 2}")
                    else:
                        pe.wait_ge(S("h_zero"), 1)
                    pe.matmul(ps[0:n, 1, :], cT[64 * g:64 * g + 64, cols], H_ssd[64 * g:64 * g + 64],
                              start=True, stop=True)
                    pe.matmul(ps[64 * g:64 * g + 64, 2, :].rearrange("p (k w) -> p k w", k=4),
                              b_tok[0:n, c, 64 * g:64 * g + 64], XW(q), start=True, stop=True)
                for h in range(8):
                    mm = pe.matmul(ps[0:n, 0, h * HD:(h + 1) * HD], RM(q)[:, h], XDT(q)[:, h // 2, h % 2],
                                   start=True, stop=True)
                done(mm, name)

            def turn_y(q):
                n = P if q < 2 * TT else TS
                pe.wait_ge(S("y_norm"), q + 1)
                if q:
                    pe.wait_ge(S("sy_lo"), q)
                for k in range(4):
                    mm = turn(PM[:, 1, k * P:k * P + n], YZ(q)[:, k * P:(k + 1) * P], n)
                mm.then_inc(S("y_turned"), 1)
            sums(0)
            decays(0)
            decays(1)
            for q in range(2 * TT):
                if q % 2 == 0:
                    sums(q // 2 + 1)
                products(q)
                if q:
                    turn_y(q - 1)
                if q + 2 < 2 * TT:
                    decays(q + 2)
            turn_y(2 * TT - 1)
            read(pe, f"sy{2 * TT - 1}")
            free_set(pe, "po")
            for k in range(4):
                mm = turn(pset("po")[:, 0, k * P:(k + 1) * P], H_ssd[:, k * P:(k + 1) * P], P)
            done(mm, "po")
            pe.wait_ge(S("cz"), 1)
            pe.wait_ge(S("sc_exp"), TT + 1)
            pe.wait_ge(S("cbm"), TT + 1)
            pe.wait_ge(S("sy_lo"), 2 * TT)
            pe.wait_ge(S("wx2"), 2)

            def turn_state(b):
                name = f"si{b}"
                pe.wait_ge(S(f"h_in{b % 2}"), 16 * 2 * (b // 2 + 1))
                free_set(pe, name)
                for k in range(4):
                    mm = turn(pset(name)[:, 0, k * P:(k + 1) * P], wk(0, P, b % 2 * 512 + k * P), P)
                done(mm, name)
            turn_state(0)
            for b in range(NB):
                name = f"ub{b}"
                pe.wait_ge(S("bm"), b + 1)
                free_set(pe, name)
                for g in range(2):
                    mm = pe.matmul(pset(name)[64 * g:64 * g + 64, 0, :], wk(5 + b % 2, P, D)[0:TS, 64 * g:64 * g + 64],
                                   wk(5)[0:TS, g * 512:(g + 1) * 512], start=True, stop=True)
                done(mm, name)
                if b + 1 < NB:
                    turn_state(b + 1)
                read(pe, f"si{b}")
                for g in range(2):
                    mm = pe.matmul(PM[0:TS, g, :], CZ[64 * g:64 * g + 64, b, :],
                                   wk(1, 512, b % 2 * 512)[64 * g:64 * g + 64], start=(b == 0), stop=(b == NB - 1))
                mm.then_inc(S("si_mm"), 1)
                name = f"uc{b}"
                read(pe, f"ub{b}")
                free_set(pe, name)
                for k in range(4):
                    mm = turn(pset(name)[:, 0, k * P:(k + 1) * P], wk(2, P, b % 2 * 512 + k * P), P)
                done(mm, name)
            q = 2 * TT
            pe.wait_ge(S("yi"), 1)
            decays(q)
            decays(q + 1)
            products(q)
            products(q + 1)
            done(project("og2_0", FIRST_W["in", C_GATE + 2 * D], Hh, Hl), "og2_0")
            turn_y(q)
            turn_y(q + 1)
            out_jobs(2, "ssd_out")
            def sum_squares(i, k):
                pe.wait_ge(S("nrm_sq"), i * DT + k + 1)
                for c in range(TT + 1):
                    n = P if c < TT else TS
                    mm = pe.matmul(PM[0:n, 0, c:c + 1], wk(4 + k % 2)[:, c * P:c * P + n], ones[:, 0:1],
                                   start=(k == 0 and c == 0), stop=(k == DT - 1), skip_group_check=True)
                mm.then_inc(S("nrm_mm"), 1)

            def spread(i, name):
                pe.wait_ge(S("nrm_rs"), i + 1)
                free_set(pe, name)
                for c in range(TT + 1):
                    n = P if c < TT else TS
                    mm = pe.matmul(pset(name)[:, c // 3, c % 3 * P:c % 3 * P + n],
                                   ST[0:n, c:c + 1].broadcast_to([n, P]), ident[0:n, 0:n], start=True, stop=True)
                done(mm, name)

            def turn_memory(i):
                name = f"mt{i}"
                pe.wait_ge(S("mem_scaled"), 2)
                free_set(pe, name)
                for k in range(DT):
                    mm = turn(pset(name)[:, k // 4, k % 4 * P:(k % 4 + 1) * P], MV[:, i, k * P:(k + 1) * P], P)
                done(mm, name)

            def project_memory(name, w):
                pe.wait_ge(w_split, w + 1)
                free_set(pe, name)
                for k in range(DT):
                    for i, (L, R) in enumerate(((Wh, MNh), (Wh, MNl), (Wl, MNh))):
                        mm = pe.matmul(pset(name)[:, 0, 0:M], L[:, w % SLOTS, k, :], R[:, k, :],
                                       start=(k == 0 and i == 0), stop=(k == DT - 1 and i == 2))
                done(mm, name)

            def turn_kv(name, src, last):
                read(pe, last)
                free_set(pe, name)
                for m in range(2):
                    for t in range(4):
                        mm = turn(pset(name)[:, m, t * P:(t + 1) * P], src[:, t, m * P:(m + 1) * P], P)
                done(mm, name)
            for t in range(DT):
                name = f"mx{t}"
                project(name, FIRST_W["mix", t * P], Hh, Hl, by_tile=("mi_lo", 0) if t == 0 else None, last=False)
                pe.wait_ge(S(f"xt_in{t % 2}"), 32 * (t // 2 + 1))
                for c in range(TT + 1):
                    n = P if c < TT else TS
                    mm = pe.matmul(pset(name)[:, c // 3, c % 3 * P:c % 3 * P + n], XT[0:n, t % 2, c, :],
                                   ident[0:n, 0:n], start=False, stop=True, skip_group_check=True)
                done(mm, name)
                if t in (4, 5):
                    turn_memory(t - 4)
                if t:
                    sum_squares(0, t - 1)
            pe.wait_ge(S("mem_lo"), 2)
            for t in range(DT):
                project_memory(f"mk{t}", FIRST_W["xk", t * P])
                if t == 0:
                    sum_squares(0, DT - 1)
                if t == 1:
                    spread(0, "xn")
                if t == 6:
                    turn_kv("kt0", KT_m[:, 0:4], "mk3")
            for t in range(DT):
                if t == 4:
                    read(pe, "vt0")
                project_memory(f"mv{t}", FIRST_W["xv", t * P])
                if t == 1:
                    turn_kv("kt1", KT_m[:, 4:8], f"mk{DT - 1}")
                if t == 3:
                    turn_kv("vt0", VF, "mv3")
            turn_kv("vt1", VF, f"mv{DT - 1}")
            for t in range(DT):
                done(project(f"xq{t}", FIRST_W["xq", t * P], Hh, Hl, by_tile=("nrm_lo", 0) if t == 0 else None), f"xq{t}")

            def scores(c):
                name = f"xs{c}"
                free_set(pe, name)
                if c == 0:
                    read(pe, f"xq{DT - 2}")
                    read(pe, f"xq{DT - 1}")
                for h in range(XH):
                    for k in range(2):
                        mm = pe.matmul(pset(name)[:, h // 2, h % 2 * M:(h % 2 + 1) * M],
                                       Q[:, 2 * h + k, c * P:(c + 1) * P], KT_m[:, 2 * h + k, :],
                                       start=(k == 0), stop=(k == 1))
                done(mm, name)

            def turn_probs(c):
                n = P if c < TT else TS
                name = f"xp{c}"
                pe.wait_ge(S("x_p"), c + 1)
                free_set(pe, name)
                for k in range(DT):
                    mm = turn(pset(name)[:, k // 4, k % 4 * P:k % 4 * P + n], Pr(c)[0:n, k * P:(k + 1) * P], n)
                done(mm, name)

            def attend(c):
                name = f"xv{c}"
                read(pe, f"xp{c}")
                free_set(pe, name)
                for k in range(DT):
                    for m in range(2):
                        mm = pe.matmul(pset(name)[:, k // 4, k % 4 * P:(k % 4 + 1) * P], MV[:, m, k * P:(k + 1) * P],
                                       PrT(c)[:, k // 2 * 2 + m, :], start=(m == 0), stop=(m == 1))
                done(mm, name)
            scores(0)
            for c in range(TT):
                turn_probs(c)
                if c + 1 < TT:
                    scores(c + 1)
                attend(c)
            name = f"xs{TT}"
            free_set(pe, name)
            for s in range(4 * NB + 2):
                if s < 4 * NB:
                    b, h = divmod(s, 4)
                    if h == 0:
                        pe.wait_ge(S(f"kv_in{b % 2}"), 16 * (b // 2 + 1))
                    if s >= 2:
                        pe.wait_ge(S("kb_e"), s - 1)
                    for k in range(2):
                        for m in range(2):
                            mm = turn(PM[:, s % 2, (2 * k + m) * P:(2 * k + m + 1) * P],
                                      KVb[b % 2][:, m, (2 * h + k) * P:(2 * h + k + 1) * P], P)
                    mm.then_inc(S("kb_t"), 1)
                if s >= 2:
                    b, h = divmod(s - 2, 4)
                    pe.wait_ge(S("kb_e"), s - 1)
                    pe.wait_ge(S("qz"), b + 1)
                    for k in range(2):
                        mm = pe.matmul(pset(name)[0:TS, h // 2, h % 2 * M:(h % 2 + 1) * M],
                                       QZb[:, b % 2, 2 * h + k, 56 - LS * b:120 - LS * b], KTb[:, 2 * h + k, :],
                                       start=(b == 0 and k == 0 and h % 2 == 0), stop=(b == NB - 1 and k == 1),
                                       skip_group_check=True)
                    if s < 4 * NB + 1:
                        mm.then_inc(S("kb_s"), 1)
            done(mm, name)
            turn_probs(TT)
            name = f"xv{TT}"
            read(pe, f"xp{TT}")
            free_set(pe, name)
            for b in range(NB):
                pe.wait_ge(S(f"kv_in{b % 2}"), 16 * (4 + b // 2 + 1))
                pe.wait_ge(S("pz"), b + 1)
                for h in range(XH):
                    for m in range(2):
                        mm = pe.matmul(pset(name)[0:TS, h // 2, h % 2 * XD:(h % 2 + 1) * XD],
                                       PZb[:, b % 2, 2 * h + m, 56 - LS * b:120 - LS * b],
                                       KVb[b % 2][:, m, h * XD:(h + 1) * XD],
                                       start=(b == 0 and m == 0 and h % 2 == 0), stop=(b == NB - 1 and m == 1),
                                       skip_group_check=True)
                if b < NB - 1:
                    mm.then_inc(S("vb"), 1)
            done(mm, name)
            read(pe, name)
            free_set(pe, "xw")
            for k in range(DT):
                mm = turn(pset("xw")[:, k // 4, k % 4 * P:k % 4 * P + TS], wk(6)[0:TS, k * P:(k + 1) * P], TS)
            done(mm, "xw")
            read(pe, "xw")
            for t in range(DT):
                done(project(f"xo{t}", FIRST_W["xo", t * P], Hh, Hl), f"xo{t}")
                if t:
                    sum_squares(1, t - 1)
            sum_squares(1, DT - 1)
            spread(1, "fn")
            for c in range(FC + 1):
                if c < FC:
                    for i in range(2):
                        for kind in ("fg", "fu"):
                            name = f"{kind}{c}_{i}"
                            first = c == 0 and i == 0 and kind == "fg"
                            done(project(name, FIRST_W[kind, (2 * c + i) * P], Hh, Hl,
                                         by_tile=("nrm_lo", DT) if first else None), name)
                if c:
                    e = c - 1
                    pe.wait_ge(S("f_lo"), 2 * c)
                    for t in range(DT):
                        name = f"fd{e}_{t}"
                        w = FIRST_W["fd", (e, t // 4)]
                        pe.wait_ge(w_split, w + 1)
                        free_set(pe, name)
                        for k in range(2):
                            for i, (L, R) in enumerate(((Wh, Fh), (Wh, Fl), (Wl, Fh))):
                                lhsT = L[:, w % SLOTS].rearrange("p (k a) m -> p k (a m)", k=2)[:, k, t % 4 * P:(t % 4 + 1) * P]
                                for g, (t0, n) in enumerate(GROUPS):
                                    mm = pe.matmul(pset(name)[:, g, 0:n], lhsT, R[:, e % 2, k, t0:t0 + n],
                                                   start=(k == 0 and i == 0), stop=(k == 1 and i == 2))
                        done(mm, name)
                        if c == FC and t:
                            sum_squares(2, t - 1)
            sum_squares(2, DT - 1)
            for c in range(TT + 1):
                n = P if c < TT else TS
                name = f"yt{c}"
                if c == 0:
                    pe.wait_ge(S("gained"), DT)
                free_set(pe, name)
                for k in range(DT):
                    mm = turn(pset(name)[0:n, k // 4, k % 4 * P:(k % 4 + 1) * P], X[:, k, c * P:c * P + n], P)
                done(mm, name)

        @block.scalar
        def _(act):
            chain = [0]

            def link(ins):
                chain[0] += 1
                ins.then_inc(act_chain, 1)
                act.wait_ge(act_chain, chain[0])

            def sync_chain():
                act.wait_ge(act_chain, chain[0])

            def all_groups(name, dst, func, bias=0.0, scale=1.0):
                ready(act, name)
                for g, (t0, n) in enumerate(GROUPS):
                    ins = act.activation(dst[:, t0:t0 + n], pset(name)[:, g, 0:n], func, bias=bias, scale=scale)
                freed(ins, name)
                read(act, name)

            def store(dst, src):
                n_stores[0] += 1
                act.dma_start(dst, src).then_inc(stored, 16)

            def out_jobs(b):
                def put(t):
                    act.wait_ge(S(f"m_new{b}"), t + 1)
                    act.dma_start(merged[b, t], wk(4 + t % 2)[:, 0:T]).then_inc(S(f"m_put{t % 2}"), 16)
                for t in range(DT):
                    if b > 0:
                        if t >= 2:
                            act.wait_ge(S(f"m_new{b}"), t - 1)
                        else:
                            branch_done(act, b)
                        sum_stored(act, b - 1, t)
                        act.dma_start(wk(2 + t % 2)[:, 0:T], merged[b - 1, t]).then_inc(S(f"m_get{t % 2}"), 16)
                    if t >= 2:
                        read(act, f"ob{b}_{t - 2}")
                    else:
                        branch_done(act, b)
                    all_groups(f"og{b}_{t}", wk(t % 2), ACT.Tanh, scale=0.5)
                    if t and (b < 2 or t <= DT - 2):
                        put(t - 1)
                if b < 2:
                    put(DT - 1)
                    return
                def get(k):
                    sum_stored(act, 2, k)
                    act.dma_start(MI(k), merged[2, k]).then_inc(S(f"mi_in{k % 3}"), 16)
                for k in range(3):
                    if k == 2:
                        act.wait_ge(S("m_new2"), DT - 1)
                    get(k)
                for k in range(DT):
                    if k < DT - 2:
                        act.wait_ge(S(f"mi_in{k % 3}"), 16 * (k // 3 + 1))
                    else:
                        act.wait_ge(S("m_new2"), k + 1)
                    act.activation(Hh[:, k], MI(k), ACT.Copy).then_inc(S("mi_hi"), 1)
                    if k + 3 < DT - 2:
                        act.wait_ge(S("mi_lo"), k + 1)
                        get(k + 3)

            act.wait_ge(packs_zero, 2)
            for row, name, n in ((R_CW, "lru_conv_w", CW), (R_CB, "lru_conv_b", 1), (R_BA, "lru_ba", 1),
                                 (R_BX, "lru_bx", 1), (R_LAM, "lru_lambda", 1), (R_NMIX, "norm_mix", 1),
                                 (R_NX, "norm_xattn", 1), (R_NFFN, "norm_ffn", 1), (R_NMEM, "norm_mem", 1),
                                 (R_NSSD, "ssd_norm", 1)):
                src = I[name][0] if n > 1 else I[name]
                act.dma_start(wk(0)[row:row + n, 0:D], src).then_inc(packs, 16)
            act.dma_start(wk(0)[R_NFIN:R_NFIN + 1, 0:D], I["norm_final"].unsqueeze(0)).then_inc(packs, 16)
            act.dma_start(wk(0)[R_CONV:R_CONV + NB * HIST, 0:D],
                          I["state_lru_conv"][0].rearrange("b k f -> (b k) f")).then_inc(packs, 16)
            act.dma_start(wk(0)[R_H0:R_H0 + NB, 0:D], I["state_lru_h"][0]).then_inc(packs, 16)
            act.dma_start(wk(0)[R_GLA:R_GLA + 1, 0:GH * DK], I["gla_b_alpha"]).then_inc(packs, 16)
            act.dma_start(wk(0)[R_GLA:R_GLA + 1, GH * DK:GH * DK + DV], I["gla_norm"]).then_inc(packs, 16)
            pq = WK[:, WT:WT + SCC]
            act.dma_start(pq[Q_CONV:Q_CONV + NB * HIST],
                          I["state_ssd_conv"][0].rearrange("b k f -> (b k) f")).then_inc(packs, 16)
            act.dma_start(pq[Q_CW:Q_CW + CW], I["ssd_conv_w"][0]).then_inc(packs, 16)
            act.dma_start(pq[Q_CB:Q_CB + 1], I["ssd_conv_b"]).then_inc(packs, 16)
            for i, name in enumerate(("lru_wa", "lru_wx")):
                blocks = I[name][0].rearrange("(t two) i j -> two i t j", two=2)
                for h in range(2):
                    act.dma_start(YA[64 * h:64 * h + 64, DT:2 * DT, i * P + 64 * h:i * P + 64 * h + 64],
                                  blocks[h]).then_inc(S("wax"), 16)
            def load_x(c):
                n = P if c < TT else TS
                if c >= 3:
                    act.wait_ge(S("x_scaled"), c - 2)
                x = I["x_prompt"][0, c * P:c * P + n] if c < TT else I["x_sample"].rearrange("b l f -> (b l) f")
                act.dma_start(XS(c)[0:n], x).then_inc(S(f"x_in{c % 3}"), 16)
            for c in range(3):
                load_x(c)

            def split_x(c):
                n = P if c < TT else TS
                read(act, f"xt{c}")
                act.activation(Hh[:, :, c * P:c * P + n],
                               wk(7)[:, 0:DT * n].rearrange("p (k t) -> p k t", k=DT), ACT.Copy).then_inc(S("h_hi"), 1)

            def roots_x(c):
                n = P if c < TT else TS
                act.wait_ge(S(f"x_in{c % 3}"), 16 * (c // 3 + 1))
                if c >= 2:
                    ready(act, f"xt{c - 2}")
                link(act.activation(wk(5 + c % 2)[0:n, 0:D], XS(c)[0:n], ACT.Square,
                                    accum_out=ST[0:n, c:c + 1]))
                if c == 0:
                    act.wait_ge(S("eps"), 1)
                act.activation(ST[0:n, c:c + 1], ST[0:n, c:c + 1], ACT.Sqrt, bias=EPSC[0:n],
                               scale=1.0 / D).then_inc(S("x_std"), 1)
            roots_x(0)
            roots_x(1)
            for c in range(TT + 1):
                if c + 3 <= TT:
                    load_x(c + 3)
                if c + 2 <= TT:
                    roots_x(c + 2)
                split_x(c)
            read(act, "pk0")
            act.activation(LAM[:, 1], PV[:, :, R_LAM], ACT.Relu, scale=-1.0)
            link(act.activation(LAM[:, 0], PV[:, :, R_LAM], ACT.Abs))
            act.activation(LAM[:, 0], LAM[:, 0], ACT.Exp, scale=-1.0).then_inc(S("lam_exp"), 1)
            xin = WK[:, 0:HIST + LP + NB * (HIST + LS)]
            xin_p = xin[:, 0:HIST + LP]
            xin_s = xin[:, HIST + LP:].rearrange("p (b c) -> p b c", b=NB)
            for t in range(DT):
                name = f"lx{t}"
                ready(act, name)
                if t:
                    act.wait_ge(S("conv"), t)
                else:
                    act.wait_ge(S("h_lo"), TT + 1)
                for g, (t0, n) in enumerate(GROUPS):
                    np_ = min(n, LP - t0)
                    ins = act.activation(xin_p[:, HIST + t0:HIST + t0 + np_], pset(name)[:, g, 0:np_], ACT.Copy)
                ins = act.activation(xin_s[:, :, HIST:], pset(name)[:, 2, LP - 768:T - 768]
                                     .rearrange("p (b l) -> p b l", b=NB), ACT.Copy)
                freed(ins, name)
                if t:
                    act.wait_ge(S("y_lo"), t)
                all_groups(f"lg{t}", wk(5), ACT.Copy)
                act.activation(wk(6)[:, 0:T], wk(5)[:, 0:T], ACT.Square).then_inc(S("g_sq"), 1)
                if t == 0:
                    act.wait_ge(S("sc"), 1)
                all_groups(f"lr{t}", wk(2), ACT.Tanh, bias=SC[:, t, 1:2], scale=0.5)
                link(act.activation(wk(3)[:, 0:T], wk(2)[:, 0:T], ACT.Tanh, bias=SC[:, t, 0:1], scale=SC[:, t, 0:1]))
                act.activation(wk(2)[:, 0:T], wk(2)[:, 0:T], ACT.Exp, bias=NSC[:, t:t + 1],
                               scale=NSC[:, t:t + 1]).then_inc(S("a"), 1)
                all_groups(f"li{t}", wk(4), ACT.Tanh, bias=SC[:, t, 2:3], scale=0.5)
                act.wait_ge(S("g_inner"), t + 1)
                act.activation(wk(6)[:, 0:T], wk(6)[:, 0:T], ACT.Tanh, scale=GELU_C).then_inc(S("g_tanh"), 1)
                act.wait_ge(S("u_var"), t + 1)
                act.activation(wk(3)[:, 0:T], wk(3)[:, 0:T], ACT.Sqrt, scale=0.25).then_inc(S("u_mult"), 1)
                act.wait_ge(S("y"), t + 1)
                act.activation(Yh[:, t], wk(5)[:, 0:T], ACT.Copy).then_inc(S("y_hi"), 1)
            branch_done(act, 0)
            ready(act, "low")
            for g, (t0, n) in enumerate(GROUPS):
                ins = act.activation(wk(3)[0:16, t0:t0 + n], pset("low")[0:16, g, 0:n], ACT.Copy)
            freed(ins, "low")
            ready(act, "dt")
            for g, (t0, n) in enumerate(GROUPS):
                ins = act.activation(wk(7)[0:16, t0:t0 + n], pset("dt")[0:16, g, 0:n], ACT.Copy)
            freed(ins, "dt")
            read(act, "dt")
            act.dma_start(dt_scr, wk(7)[0:16, 0:T]).then_inc(S("dt_put"), 16)
            ready(act, "lt")
            freed(act.activation(wk(2)[0:36, 0:D], pset("lt")[0:36, 0:2].rearrange("p a c -> p (a c)"), ACT.Copy), "lt")
            read(act, "lt")
            store(O["p_lru_conv"][0, 0], wk(2)[0:3, 0:D])
            store(O["s_lru_conv"][0].rearrange("b k f -> (b k) f"), wk(2)[3:27, 0:D])
            store(O["p_lru_h"][0:1, 0, :], wk(2)[27:28, 0:D])
            store(O["s_lru_h"][0], wk(2)[28:36, 0:D])

            def load_alpha(h):
                if h >= 2:
                    ready(act, f"ga{h - 2}")
                act.dma_start(CB[0:16].rearrange("p k c -> p (k c)")[:, h % 2 * P:h % 2 * P + P],
                              I["gla_w_alpha"][0, :, h * P:(h + 1) * P]).then_inc(S(f"wal{h % 2}"), 16)
            load_alpha(0)
            load_alpha(1)
            out_jobs(0)
            for t in range(DT - 2, DT):
                sum_stored(act, 0, t)
            act.wait_ge(S("m_new0"), DT)
            V = WK[:, 6 * WT:8 * WT].rearrange("p (c v) -> p c v", c=TT + 1)
            KEt = wk(1).rearrange("p (c d) -> p c d", c=TT + 1)
            RS = [wk(2)[:, 0:T], wk(5)[:, 0:T]]

            act.wait_ge(S("dt_put"), 16)
            for h in range(GH):
                A = [YA[:, i] for i in (2 * h, 2 * h + 1, DT + 2 * h, DT + 2 * h + 1)]
                on = lambda c: A[1][:, 256 + c % 2 * DV:256 + (c % 2 + 1) * DV]
                St = lambda c: A[2][:, c % 2 * DV:(c % 2 + 1) * DV]
                Sb = lambda b: A[3][:, b % 3 * DV:(b % 3 + 1) * DV] if b % 3 < 2 else A[1][:, 768:1024]
                So = lambda b: A[3][:, 512 + b % 2 * DV:512 + (b % 2 + 1) * DV]
                name = f"ga{h}"
                ready(act, name)
                act.wait_ge(S("nb"), 1)
                for g, (t0, n) in enumerate(GROUPS):
                    act.activation(A[0][:, t0:t0 + n], pset(name)[:, g, 0:n], ACT.Abs, bias=PV[:, h, R_GLA:R_GLA + 1])
                    ins = act.activation(A[1][:, t0:t0 + n], pset(name)[:, g, 0:n], ACT.Relu,
                                         bias=LAM[:, 3, h:h + 1], scale=-1.0)
                freed(ins, name)
                read(act, name)
                link(act.activation(A[0], A[0], ACT.Exp, scale=-1.0))
                act.activation(A[0], A[0], ACT.Ln, bias=1.0).then_inc(S("gl_ln"), 1)
                act.wait_ge(S("gl_cum"), h + 1)
                act.activation(A[2], A[1], ACT.Exp, scale=-1.0 / 16)
                act.activation(A[3], A[1], ACT.Exp, scale=1.0 / 16).then_inc(S("gl_exp"), 1)
                act.wait_ge(S("gl_d"), h + 1)
                act.activation(A[0], A[0], ACT.Exp, scale=-1.0 / 16).then_inc(S("gl_ed"), 1)
                if h:
                    act.wait_ge(S("gy_lo"), h)
                for v in range(2):
                    ready(act, f"gr{h}_{v}")
                    for g, (t0, n) in enumerate(GROUPS):
                        ins = act.activation(RS[v][:, t0:t0 + n], pset(f"gr{h}_{v}")[:, g, 0:n], ACT.Tanh, scale=0.5)
                    ins.then_inc(S("gr_th"), 1)
                read(act, f"gk{h}")
                for b in range(3):
                    act.dma_start(Sb(b), I["state_gla_S"][0, b, h]).then_inc(S(f"sb_in{b}"), 16)
                name = f"gva{h}"
                ready(act, name)
                act.activation(V[:, 0:4].rearrange("p (a c) v -> p a (c v)", a=2), pset(name)[:, 0:2, :], ACT.Copy)
                freed(act.activation(V[:, 4], pset(name)[:, 2, 0:DV], ACT.Copy), name)
                name = f"gvb{h}"
                ready(act, name)
                act.activation(V[:, 5:7].rearrange("p c v -> p (c v)"), pset(name)[:, 0, :], ACT.Copy)
                act.activation(V[:, 7], pset(name)[:, 1, 0:DV], ACT.Copy)
                freed(act.activation(V[0:TS, 8], pset(name)[0:TS, 1, DV:2 * DV], ACT.Copy), name)
                name = f"gt{h}"
                ready(act, name)
                act.activation(KEt[:, 0:8].rearrange("p (a c) d -> p a (c d)", a=2), pset(name)[:, 0:2, :], ACT.Copy)
                freed(act.activation(KEt[0:TS, 8], pset(name)[0:TS, 2, 0:P], ACT.Copy), name)
                if h + 2 < GH:
                    load_alpha(h + 2)
                for c in range(TT + 1):
                    n = P if c < TT else TS
                    q = h * (TT + 1) + c
                    name = f"go{h}_{c}"
                    if c == TT:
                        act.wait_ge(S("s_upd"), h * 24 + 16)
                        act.dma_start(O["p_gla_S"][0, 0, h], St(0)).then_inc(S("gs_put"), 16)
                        for b in range(NB):
                            act.wait_ge(S("s_upd"), h * 24 + 17 + b)
                            act.dma_start(O["s_gla_S"][0, b, h], So(b)).then_inc(S(f"sb_put{b % 2}"), 16)
                            if b + 3 < NB:
                                act.wait_ge(S("sb_int"), h * 7 + b + 1)
                                act.dma_start(Sb(b), I["state_gla_S"][0, b + 3, h]).then_inc(S(f"sb_in{b % 3}"), 16)
                    ready(act, name)
                    if q >= 2:
                        act.wait_ge(S("ot"), q - 1)
                    st = ST[0:n, 24 + q % 2:25 + q % 2]
                    link(act.activation(on(c)[0:n], pset(name)[0:n, 0, 0:DV], ACT.Square, accum_out=st))
                    act.activation(st, st, ACT.Sqrt, bias=EPSC[0:n], scale=1.0 / DV).then_inc(S("g_std"), 1)
                act.wait_ge(S("ymul"), (h + 1) * (TT + 1))
                act.wait_ge(S("gs_put"), 16 * (h + 1))
                for i in range(2):
                    act.wait_ge(S(f"sb_put{i}"), 16 * 4 * (h + 1))
                for v in range(2):
                    act.activation(Yh[:, 2 * h + v], RS[v], ACT.Copy).then_inc(S("gy_hi"), 1)
            branch_done(act, 1)
            act.dma_start(wk(6)[0:SH, 0:T], dt_scr).then_inc(S("dt_in"), 16)
            act.dma_start(DTB, I["ssd_dt_bias"].broadcast_to([P, SH])).then_inc(S("dt_in"), 16)
            act.dma_start(ALOG, I["ssd_a_log"].broadcast_to([P, SH])).then_inc(S("dt_in"), 16)
            act.dma_start(DBC, I["ssd_d"].broadcast_to([P, SH])).then_inc(S("dt_in"), 16)
            out_jobs(1)
            DT0, DT1 = wk(7, 144, 288), wk(7, 144, 432)
            act.wait_ge(S("dt_raw"), 1)
            act.activation(DT1, DTK[:, 0].rearrange("p c h -> p (c h)"), ACT.Relu)
            act.activation(ALOG, ALOG, ACT.Exp)
            link(act.activation(DT0, DTK[:, 0].rearrange("p c h -> p (c h)"), ACT.Abs))
            act.activation(DT0, DT0, ACT.Exp, scale=-1.0).then_inc(S("dt_exp"), 1)
            for t in range(DT - 2, DT):
                sum_stored(act, 1, t)
            act.wait_ge(S("m_new1"), DT)
            xin = wk(3)
            xin_p = xin[:, 0:HIST + LP]
            xin_s = xin[:, HIST + LP:HIST + LP + NB * (HIST + LS)].rearrange("p (b c) -> p b c", b=NB)
            b_tok = wk(2).rearrange("p (c n) -> p c n", c=TT + 1)
            read(act, "dtt")

            def copy_turned(name, dst, scale=1.0):
                ready(act, name)
                act.activation(dst[:, 0:8].rearrange("p (a c) n -> p a (c n)", a=2), pset(name)[:, 0:2, :],
                               ACT.Copy, scale=scale)
                freed(act.activation(dst[0:TS, 8], pset(name)[0:TS, 2, 0:P], ACT.Copy, scale=scale), name)

            def put_turned(name, dst, scratch, t, signal):
                read(act, name)
                act.dma_start(scratch[0:LP, t * P:(t + 1) * P].rearrange("(c p) n -> p c n", p=P),
                              dst[:, 0:8]).then_inc(S(signal), 16)
                act.dma_start(scratch[LP:T, t * P:(t + 1) * P], dst[0:TS, 8]).then_inc(S(signal), 16)

            def put_x(t):
                if t < DT:
                    dst = wk(6).rearrange("p (c n) -> p c n", c=TT + 1)
                    if t:
                        act.wait_ge(S("x_put"), 32 * t)
                    copy_turned(f"st{t}", dst, 0.5)
                    put_turned(f"st{t}", dst, x_scr, t, "x_put")
                else:
                    copy_turned(f"st{t}", b_tok)
            for t in range(CT):
                name = f"sx{t}"
                ready(act, name)
                if t:
                    act.wait_ge(S("sconv"), t)
                for g, (t0, n) in enumerate(GROUPS):
                    np_ = min(n, LP - t0)
                    act.activation(xin_p[:, HIST + t0:HIST + t0 + np_], pset(name)[:, g, 0:np_], ACT.Copy)
                freed(act.activation(xin_s[:, :, HIST:], pset(name)[:, 2, LP - 768:T - 768]
                                     .rearrange("p (b l) -> p b l", b=NB), ACT.Copy), name)
                if t:
                    put_x(t - 1)
                act.wait_ge(S("sconv"), t + 1)
                act.activation(wk(5)[:, 0:T], wk(4)[:, 0:T], ACT.Tanh, scale=0.5).then_inc(S("s_th"), 1)
            def put_z(t):
                dst = wk(5 + t % 2).rearrange("p (c n) -> p c n", c=TT + 1)
                if t >= 2:
                    act.wait_ge(S(f"z_put{t % 2}"), 32 * (t // 2))
                copy_turned(f"zt{t}", dst)
                put_turned(f"zt{t}", dst, z_scr, t, f"z_put{t % 2}")
            act.wait_ge(S("s_act"), CT)
            act.wait_ge(S("x_put"), 32 * DT)
            for t in range(DT):
                name = f"sz{t}"
                ready(act, name)
                if t >= 2:
                    ready(act, f"zt{t - 2}")
                for g, (t0, n) in enumerate(GROUPS):
                    ins = act.activation(wk(3 + t % 2)[:, t0:t0 + n], pset(name)[:, g, 0:n], ACT.Tanh, scale=0.5)
                ins.then_inc(S("z_th"), 1)
                if t:
                    put_z(t - 1)
                    continue
                ready(act, "qt")
                tails = [wk(7, 768, 288)[0:27], YT[0:27, 0:512]]
                act.activation(tails[0][:, 0:512], pset("qt")[0:27, 0, :], ACT.Copy)
                act.activation(tails[0][:, 512:768], pset("qt")[0:27, 1, 0:256], ACT.Copy)
                act.activation(tails[1][:, 0:256], pset("qt")[0:27, 1, 256:512], ACT.Copy)
                freed(act.activation(tails[1][:, 256:512], pset("qt")[0:27, 2, 0:256], ACT.Copy), "qt")
                read(act, "qt")
                for tail, cols in zip(tails, (slice(0, 768), slice(768, SCC))):
                    store(O["p_ssd_conv"][0, 0, :, cols], tail[0:3])
                    store(O["s_ssd_conv"][0].rearrange("b k f -> (b k) f")[:, cols], tail[3:27])
            put_z(DT - 1)
            for i in range(2):
                act.wait_ge(S(f"z_put{i}"), 32 * 4)
            act.wait_ge(stored, 16 * n_stores[0])

            def load_z(q):
                c, g = divmod(q, 2)
                n = P if c < TT else TS
                if q >= 2:
                    act.wait_ge(S("y_turned"), q - 1)
                act.dma_start(YZ(q), z_scr[c * P:c * P + n, g * 512:(g + 1) * 512]).then_inc(S(f"z_in{q % 2}"), 16)

            def load_xs(q):
                c, g = divmod(q, 2)
                n = P if c < TT else TS
                half = slice(g * 512, (g + 1) * 512)
                act.dma_start(wk(3)[0:n, half], x_scr[c * P:c * P + n, half]).then_inc(S(f"xs_in{g}"), 16)

            def state_in(b):
                src = I["state_ssd_h"][0, b].rearrange("(g k h) p n -> g (h p) k n", g=2, k=4)
                dst = wk(0, 512, b % 2 * 512).rearrange("p (k g n) -> p k g n", k=4, g=2)
                for g in range(2):
                    act.dma_start(dst[:, :, g], src[g]).then_inc(S(f"h_in{b % 2}"), 16)

            def state_out(dst, src, signal):
                d = dst.rearrange("(g k h) p n -> g (h p) k n", g=2, k=4)
                s = src.rearrange("p (k g n) -> p k g n", k=4, g=2)
                for g in range(2):
                    act.dma_start(d[g], s[:, :, g]).then_inc(signal, 16)

            def exp_sums(c):
                n = P if c < TT else TS
                m = 16 if c < TT else 128
                act.wait_ge(S("sums"), c + 1)
                act.activation(EC(c)[0:n], PM[0:n, 0, 0:32], ACT.Exp)
                act.activation(EL(c), PM[:, 0, 32:32 + m], ACT.Exp).then_inc(S("sc_exp"), 1)

            def exp_decays(q):
                n = P if q < 2 * TT else TS
                name = f"ss{q}"
                m = 512 // n
                ready(act, name)
                for i in range(8 // m):
                    ins = act.activation(RM(q)[:, i * m:(i + 1) * m],
                                         pset(name)[0:n, i, :].rearrange("p (h i) -> p h i", i=n), ACT.Exp)
                freed(ins, name)

            def roots_y(q):
                n = P if q < 2 * TT else TS
                act.wait_ge(S("y_gated"), q + 1)
                st = ST[0:n, 28 + q % 2:29 + q % 2]
                link(act.activation(YT[0:n, 0:512], YZ(q), ACT.Square, scale=0.5, accum_out=st))
                act.activation(st, st, ACT.Sqrt, bias=EPSC[0:n], scale=1.0 / 512).then_inc(S("y_std"), 1)

            def hi_y(q):
                c, g = divmod(q, 2)
                n = P if c < TT else TS
                act.wait_ge(S("y_turned"), q + 1)
                for k in range(4):
                    ins = act.activation(Yh[:, 4 * g + k, c * P:c * P + n], PM[:, 1, k * P:k * P + n], ACT.Copy,
                                         scale=PV[:, 4 * g + k, R_NSSD:R_NSSD + 1])
                ins.then_inc(S("sy_hi"), 1)
            load_z(0)
            load_z(1)
            load_xs(0)
            load_xs(1)
            exp_sums(0)
            exp_decays(0)
            exp_decays(1)
            for q in range(2 * TT):
                if q % 2 == 0:
                    exp_sums(q // 2 + 1)
                if q:
                    hi_y(q - 1)
                    load_z(q + 1)
                if q + 2 < 2 * TT:
                    exp_decays(q + 2)
                act.wait_ge(S("x_used"), q + 1)
                load_xs(q + 2)
                roots_y(q)
            for b in range(2):
                state_in(b)
            hi_y(2 * TT - 1)
            ready(act, "po")
            freed(act.activation(wk(2, 512), pset("po")[:, 0, :], ACT.Copy), "po")
            read(act, "po")
            n_stores[0] += 2
            state_out(O["p_ssd_h"][0, 0], wk(2, 512), stored)
            SO = [wk(6, 512, 512), wk(4, 512, 512)]

            def copy_state(b):
                name = f"si{b}"
                ready(act, name)
                if b + 2 < NB:
                    state_in(b + 2)
                if b >= 2:
                    act.wait_ge(S("si_mm"), b - 1)
                    read(act, f"ub{b - 2}")
                freed(act.activation(wk(1, 512, b % 2 * 512), pset(name)[:, 0, :], ACT.Copy), name)
            act.wait_ge(stored, 16 * n_stores[0])
            act.wait_ge(S("cz"), 1)
            for b in range(NB + 1):
                if b < NB:
                    copy_state(b)
                if b:
                    name = f"uc{b - 1}"
                    ready(act, name)
                    if b >= 3:
                        act.wait_ge(S(f"h_put{(b - 1) % 2}"), 32 * ((b - 1) // 2))
                    freed(act.activation(SO[(b - 1) % 2], pset(name)[:, 0, :], ACT.Copy), name)
                    read(act, name)
                    state_out(O["s_ssd_h"][0, b - 1], SO[(b - 1) % 2], S(f"h_put{(b - 1) % 2}"))
            act.wait_ge(S("si_mm"), NB)
            act.activation(YI[0][0:TS], PM[0:TS, 0, :], ACT.Copy)
            act.activation(YI[1][0:TS], PM[0:TS, 1, :], ACT.Copy).then_inc(S("yi"), 1)
            q = 2 * TT
            exp_decays(q)
            exp_decays(q + 1)
            for i in range(2):
                act.wait_ge(S(f"h_put{i}"), 32 * 4)
            load_z(q + 1)
            roots_y(q)
            roots_y(q + 1)
            hi_y(q)
            hi_y(q + 1)
            out_jobs(2)
            def load_xt(t):
                cols = slice(t * P, (t + 1) * P)
                act.dma_start(XT[:, t % 2, 0:TT], I["x_prompt"][0, :, cols].rearrange("(c p) f -> p c f", p=P))\
                    .then_inc(S(f"xt_in{t % 2}"), 16)
                act.dma_start(XT[0:TS, t % 2, TT], I["x_sample"].rearrange("b l f -> (b l) f")[:, cols])\
                    .then_inc(S(f"xt_in{t % 2}"), 16)
            load_xt(0)
            load_xt(1)
            act.wait_ge(S("mi_lo"), DT)
            act.dma_start(MV, I["mem_prompt"][0].rearrange("(m p) f -> p m f", p=P)).then_inc(S("mem_in"), 16)

            def square(i, k):
                if k >= 2:
                    act.wait_ge(S("nrm_mm"), i * DT + k - 1)
                act.activation(wk(4 + k % 2)[:, 0:T], X[:, k], ACT.Square).then_inc(S("nrm_sq"), 1)

            def roots(i):
                act.wait_ge(S("nrm_mm"), (i + 1) * DT)
                act.activation(ST[:, 0:TT], PM[:, 0, 0:TT], ACT.Sqrt, bias=EPSC[:], scale=1.0 / D)
                act.activation(ST[0:TS, TT:TT + 1], PM[0:TS, 0, TT:TT + 1], ACT.Sqrt, bias=EPSC[0:TS], scale=1.0 / D)\
                    .then_inc(S("nrm_std"), 1)

            def copy_spread(name):
                ready(act, name)
                for g, (t0, n) in enumerate(GROUPS):
                    ins = act.activation(wk(6)[:, t0:t0 + n], pset(name)[:, g, 0:n], ACT.Copy)
                freed(ins, name)

            def mem_hi(i):
                read(act, f"mt{i}")
                act.activation(MNh[:, :, i * P:(i + 1) * P], wk(7, D).rearrange("p (k m) -> p k m", k=DT), ACT.Copy)\
                    .then_inc(S("mem_hi"), 1)
            for t in range(DT):
                all_groups(f"mx{t}", X[:, t], ACT.Copy)
                if t + 2 < DT:
                    load_xt(t + 2)
                square(0, t)
                if t == 1:
                    act.wait_ge(S("mem_in"), 16)
                    for i in range(2):
                        link(act.activation(wk(i)[:, 0:D], MV[:, i], ACT.Square, accum_out=ST[:, 30 + i:31 + i]))
                    act.activation(ST[:, 30:32], ST[:, 30:32], ACT.Sqrt, bias=EPSC[:], scale=1.0 / D)\
                        .then_inc(S("mem_std"), 1)
                if t in (5, 6):
                    mem_hi(t - 5)
            def hi_weights(n):
                act.wait_ge(w_loaded[n % SLOTS], 16 * (n // SLOTS + 1))
                act.wait_ge(w_hi, n)
                act.activation(Wh[:, n % SLOTS], Wr[:, n % SLOTS], ACT.Copy).then_inc(w_hi, 1)

            def copy_turned_kv(name, dst):
                ready(act, name)
                freed(act.activation(dst, pset(name)[:, 0:2, :], ACT.Copy), name)
            w0 = FIRST_W["xk", 0]
            for t in range(SLOTS):
                hi_weights(w0 + t)
            for t in range(2 * DT):
                name = f"mk{t}" if t < DT else f"mv{t - DT}"
                dst = KT_m[:, t] if t < DT else VF[:, t % 4]
                ready(act, name)
                if t == DT + 4:
                    ready(act, "vt0")
                freed(act.activation(dst, pset(name)[:, 0, 0:M], ACT.Copy), name)
                if t + SLOTS < 2 * DT:
                    hi_weights(w0 + t + SLOTS)
                if t == 0:
                    roots(0)
                if t == 1:
                    copy_spread("xn")
                if t == 6:
                    copy_turned_kv("kt0", KM[:, :, 0:512])
                if t == DT + 1:
                    copy_turned_kv("kt1", KM[:, :, 512:D])
                    read(act, "kt0")
                    read(act, "kt1")
                    store(O["p_mem_k"][0, 0].rearrange("(m p) h d -> p m (h d)", p=P), KM[:])
                if t == DT + 3:
                    copy_turned_kv("vt0", MV[:, :, 0:512])
            copy_turned_kv("vt1", MV[:, :, 512:D])
            read(act, "vt0")
            read(act, "vt1")
            store(O["p_mem_v"][0, 0].rearrange("(m p) h d -> p m (h d)", p=P), MV)
            act.wait_ge(stored, 16 * n_stores[0])
            for t in range(DT):
                all_groups(f"xq{t}", Q[:, t], ACT.Copy)

            def probs(c):
                n = P if c < TT else TS
                name = f"xs{c}"
                act.wait_ge(S("x_max"), c + 1)
                if 2 <= c < TT:
                    ready(act, f"xp{c - 2}")
                for h in range(XH):
                    ins = act.activation(Pr(c)[0:n, h * M:(h + 1) * M], pset(name)[0:n, h // 2, h % 2 * M:(h % 2 + 1) * M],
                                         ACT.Exp, bias=ST[0:n, 32 + 4 * (c % 2) + h:33 + 4 * (c % 2) + h],
                                         scale=XD ** -0.5,
                                         accum_out=ST[0:n, 40 + 4 * (c % 2) + h:41 + 4 * (c % 2) + h])
                freed(ins, name)

            def turned_probs(c):
                n = P if c < TT else TS
                name = f"xp{c}"
                ready(act, name)
                if 2 <= c < TT:
                    ready(act, f"xv{c - 2}")
                for a in range(2):
                    ins = act.activation(PrT(c)[:, 4 * a:4 * a + 4, 0:n],
                                         pset(name)[:, a, :].rearrange("p (k t) -> p k t", k=4)[:, :, 0:n], ACT.Copy)
                freed(ins, name)

            def outputs(c):
                n = P if c < TT else TS
                name = f"xv{c}" if c < TT else "xw"
                ready(act, name)
                for a in range(2):
                    ins = act.activation(Hh[:, 4 * a:4 * a + 4, c * P:c * P + n],
                                         pset(name)[:, a, :].rearrange("p (k t) -> p k t", k=4)[:, :, 0:n], ACT.Copy)
                ins.then_inc(S("xo_hi"), 1)

            def load_kv(b, which):
                act.dma_start(KVb[b % 2], I[f"cache_mem_{which}"][0, b].rearrange("(m p) h d -> p m (h d)", p=P))\
                    .then_inc(S(f"kv_in{b % 2}"), 16)
            probs(0)
            for c in range(TT):
                turned_probs(c)
                if c + 1 < TT:
                    probs(c + 1)
                outputs(c)
            load_kv(0, "k")
            load_kv(1, "k")
            for s in range(4 * NB):
                act.wait_ge(S("kb_t"), s + 1)
                if s >= 4:
                    act.wait_ge(S("kb_s"), s - 3)
                act.activation(KTb[:, s % 4 * 2:s % 4 * 2 + 2].rearrange("p k m -> p (k m)"), PM[:, s % 2, :], ACT.Copy)\
                    .then_inc(S("kb_e"), 1)
                if s % 4 == 3:
                    b = s // 4
                    load_kv(b % 2 if b + 2 >= NB else b + 2, "v" if b + 2 >= NB else "k")
            probs(TT)
            turned_probs(TT)
            for b in range(2, NB):
                act.wait_ge(S("vb"), b - 1)
                load_kv(b, "v")
            name = f"xv{TT}"
            ready(act, name)
            freed(act.activation(wk(6)[0:TS, 0:D], pset(name)[0:TS, 0:2, :].rearrange("p a c -> p (a c)"), ACT.Copy), name)
            outputs(TT)
            for t in range(DT):
                read(act, f"xo{t}")
                square(1, t)
            roots(1)
            copy_spread("fn")
            for k in range(DT):
                act.wait_ge(S("nrm_t"), k + 1)
                act.activation(Hh[:, k], wk(4 + k % 2)[:, 0:T], ACT.Copy).then_inc(S("nrm_hi"), 1)
            for c in range(FC):
                for i in range(2):
                    q = 2 * c + i
                    name = f"fg{c}_{i}"
                    ready(act, name)
                    if q >= 4:
                        act.wait_ge(S("f_lo"), q - 3)
                    for g, (t0, n) in enumerate(GROUPS):
                        ins = act.activation(wk(q % 4)[:, t0:t0 + n], pset(name)[:, g, 0:n], ACT.Tanh, scale=0.5)
                    ins.then_inc(S("f_th"), 1)
                    read(act, f"fu{c}_{i}")
                    if q >= 4:
                        ready(act, f"fd{c - 2}_{DT - 1}")
                    act.activation(Fh[:, c % 2, i], wk(q % 4)[:, 0:T], ACT.Copy).then_inc(S("f_hi"), 1)
            for t in range(DT):
                read(act, f"fd{FC - 1}_{t}")
                square(2, t)
            roots(2)
            act.wait_ge(S("nrm_rs"), 3)
            for c in range(TT + 1):
                n = P if c < TT else TS
                name = f"yt{c}"
                ready(act, name)
                if c >= 2:
                    act.wait_ge(S(f"out{c % 2}"), 16 * (c // 2))
                freed(act.activation(wk(c % 2)[0:n, 0:D], pset(name)[0:n, 0:2].rearrange("p a c -> p (a c)"), ACT.Copy,
                                     scale=ST[0:n, c:c + 1]), name)
                read(act, name)
                y = O["y_prompt"][0, c * P:c * P + n] if c < TT else O["y_sample"].rearrange("b l f -> (b l) f")
                act.dma_start(y, wk(c % 2)[0:n, 0:D]).then_inc(S(f"out{c % 2}"), 16)
            act.wait_ge(S("out0"), 16 * 5)
            act.wait_ge(S("out1"), 16 * 4)
            act.wait_ge(stored, 16 * n_stores[0])

        @block.vector
        def _(dve):
            chain = [0]

            def link(ins):
                chain[0] += 1
                ins.then_inc(dve_chain, 1)
                dve.wait_ge(dve_chain, chain[0])

            def stt(out, in0, scalar, in1, op0, op1):
                return dve.scalar_tensor_tensor(out=out, in0=in0, scalar=scalar, in1=in1, op0=op0, op1=op1)

            MUL, ADD, SUB = ALU.mult, ALU.add, ALU.subtract

            def lo_sum(k):
                dve.wait_ge(S("mi_hi"), k + 1)
                dve.tensor_tensor(Hl[:, k], MI(k), Hh[:, k].bitcast(F32), SUB).then_inc(S("mi_lo"), 1)

            def out_jobs(b):
                for t in range(DT):
                    if b == 2 and t == DT - 1:
                        for k in range(DT - 2):
                            lo_sum(k)
                    th = wk(t % 2)
                    read(dve, f"og{b}_{t}")
                    ready(dve, f"ob{b}_{t}")
                    for g, (t0, n) in enumerate(GROUPS):
                        ins = stt(th[:, t0:t0 + n], th[:, t0:t0 + n], 1.0, pset(f"ob{b}_{t}")[:, g, 0:n], ADD, MUL)
                    freed(ins, f"ob{b}_{t}")
                    read(dve, f"ob{b}_{t}")
                    if t >= 2:
                        sum_stored(dve, b, t - 2)
                    if b == 0:
                        dve.tensor_scalar(wk(4 + t % 2)[:, 0:T], th[:, 0:T], 0.5, None, MUL).then_inc(S(f"m_new{b}"), 1)
                    else:
                        dve.wait_ge(S(f"m_get{t % 2}"), 16 * ((b - 1) * DT // 2 + t // 2 + 1))
                        stt(wk(4 + t % 2)[:, 0:T], th[:, 0:T], 0.5, wk(2 + t % 2)[:, 0:T], MUL, ADD)\
                            .then_inc(S(f"m_new{b}"), 1)

            def conv(xin_p, xin_s, dst, taps, bias, hist, tail):
                link(dve.tensor_copy(xin_s[:, :, 0:HIST], hist))
                for out, src in ((dst[:, 0:LP], lambda k: xin_p[:, k:k + LP]),
                                 (seqs(dst), lambda k: xin_s[:, :, k:k + LS])):
                    link(dve.tensor_scalar(out, src(0), taps[0], bias, MUL, ADD))
                    for k in range(1, CW):
                        link(stt(out, src(k), taps[k], out, MUL, ADD))
                link(dve.tensor_copy(tail[:, 0:HIST], xin_p[:, LP:LP + HIST]))
                return dve.tensor_copy(tail[:, HIST:HIST + NB * HIST].rearrange("p (b k) -> p b k", b=NB),
                                       xin_s[:, :, LS:LS + HIST])

            dve.memset(EPSC[:], EPS).then_inc(S("eps"), 1)
            dve.memset(wk(0)[0:NROW, 0:D], 0.0).then_inc(packs_zero, 1)
            dve.memset(YA[:, DT:2 * DT, 0:2 * P], 0.0).then_inc(packs_zero, 1)
            ready(dve, "pk0")
            freed(dve.tensor_copy(PV[:], pset("pk0")[:, 0, 0:DT * NROW].rearrange("p (k r) -> p k r", k=DT)), "pk0")
            ready(dve, "pk1")
            freed(dve.tensor_copy(PQ[:], pset("pk1")[:, 0, 0:CT * QROW].rearrange("p (k r) -> p k r", k=CT)), "pk1")
            read(dve, "pk0")
            read(dve, "pk1")
            def lo_x(c):
                n = P if c < TT else TS
                dve.wait_ge(S("h_hi"), c + 1)
                dve.tensor_tensor(Hl[:, :, c * P:c * P + n], wk(7)[:, 0:DT * n].rearrange("p (k t) -> p k t", k=DT),
                                  Hh[:, :, c * P:c * P + n].bitcast(F32), SUB).then_inc(S("h_lo"), 1)
            def scale_x(c):
                n = P if c < TT else TS
                dve.wait_ge(S("x_std"), c + 1)
                link(dve.reciprocal(ST[0:n, c:c + 1], ST[0:n, c:c + 1]))
                dve.tensor_scalar(wk(5 + c % 2)[0:n, 0:D], XS(c)[0:n], ST[0:n, c:c + 1], None, MUL)\
                    .then_inc(S("x_scaled"), 1)
            scale_x(0)
            for c in range(TT + 1):
                n = P if c < TT else TS
                if c + 1 <= TT:
                    scale_x(c + 1)
                if c:
                    lo_x(c - 1)
                    dve.wait_ge(S("h_lo"), c)
                ready(dve, f"xt{c}")
                for i in range(2):
                    ins = dve.tensor_tensor(
                        wk(7)[:, i * 4 * n:(i + 1) * 4 * n].rearrange("p (k t) -> p k t", k=4),
                        pset(f"xt{c}")[:, i].rearrange("p (k t) -> p k t", k=4)[:, :, 0:n],
                        PV[:, 4 * i:4 * i + 4, R_NMIX:R_NMIX + 1].broadcast_to([P, 4, n]), MUL)
                    if i == 0:
                        link(ins)
                freed(ins, f"xt{c}")
                read(dve, f"xt{c}")
            lo_x(TT)

            def atanh_of(e, s, s2, p):
                link(dve.tensor_scalar(s, e, 2.0, None, ADD))
                link(dve.reciprocal(s, s))
                link(dve.tensor_tensor(s, s, e, MUL))
                link(dve.tensor_tensor(s2, s, s, MUL))
                link(dve.tensor_scalar(p, s2, 1.0 / 15, None, MUL))
                for m in (13, 11, 9, 7, 5, 3):
                    link(stt(p, p, 1.0 / m, s2, ADD, MUL))
                link(stt(s, p, 1.0, s, ADD, MUL))

            dve.wait_ge(S("lam_exp"), 1)
            atanh_of(LAM[:, 0], LAM[:, 2], LAM[:, 3], NSC[:])
            link(stt(NSC[:], LAM[:, 2], 2.0, LAM[:, 1], MUL, ADD))
            link(dve.tensor_scalar(SC[:, :, 0], NSC[:], 4.0, None, MUL))
            link(dve.tensor_scalar(NSC[:], NSC[:], -4.0, None, MUL))
            dve.tensor_scalar(SC[:, :, 1:3], PV[:, :, R_BA:R_BX + 1], 0.5, None, MUL).then_inc(S("sc"), 1)
            xin = WK[:, 0:HIST + LP + NB * (HIST + LS)]
            xin_p = xin[:, 0:HIST + LP]
            xin_s = xin[:, HIST + LP:].rearrange("p (b c) -> p b c", b=NB)
            link(dve.memset(xin_p[:, 0:HIST], 0.0))
            xc, A, TZ, TI, G, GP, U = (wk(i)[:, 0:T] for i in range(1, 8))
            for t in range(DT):
                read(dve, f"lx{t}")
                conv(xin_p, xin_s, xc, [PV[:, t, R_CW + k:R_CW + k + 1] for k in range(CW)],
                     PV[:, t, R_CB:R_CB + 1], PV[:, t, R_CONV:R_CONV + NB * HIST].rearrange("p (b k) -> p b k", b=NB),
                     CB[:, t]).then_inc(S("conv"), 1)
                dve.wait_ge(S("g_sq"), t + 1)
                link(dve.tensor_scalar(GP, GP, 0.044715, 1.0, MUL, ADD))
                dve.tensor_tensor(GP, GP, G, MUL).then_inc(S("g_inner"), 1)
                dve.wait_ge(S("a"), t + 1)
                link(dve.tensor_tensor(U, A, A, MUL))
                stt(TZ, U, 1.0, TZ, ADD, MUL).then_inc(S("u_var"), 1)
                read(dve, f"li{t}")
                link(stt(TI, TI, 1.0, xc, ADD, MUL))
                dve.wait_ge(S("u_mult"), t + 1)
                link(dve.tensor_tensor(TI, TI, TZ, MUL))
                h0 = PV[:, t, R_H0:R_H0 + NB]
                link(dve.tensor_tensor(LAM[:, 0], seqs(A)[:, :, 0], h0, MUL))
                link(dve.tensor_tensor(seqs(TI)[:, :, 0], seqs(TI)[:, :, 0], LAM[:, 0], ADD))
                link(dve.memset(seqs(A)[:, :, 0:1], 0.0))
                link(dve.tensor_tensor_scan(U, A, TI, 0.0, MUL, ADD))
                dve.tensor_copy(CB[:, t, 27:28], U[:, LP - 1:LP])
                dve.tensor_copy(CB[:, t, 28:36], seqs(U)[:, :, LS - 1]).then_inc(S("cb"), 1)
                dve.wait_ge(S("g_tanh"), t + 1)
                link(stt(GP, GP, 1.0, G, ADD, MUL))
                stt(G, GP, 0.5, U, MUL, MUL).then_inc(S("y"), 1)
                dve.wait_ge(S("y"), t + 1)
                dve.wait_ge(S("y_hi"), t + 1)
                ins = dve.tensor_tensor(Yl[:, t], G, Yh[:, t].bitcast(F32), SUB)
                ins.then_inc(S("y_lo"), 1)
            out_jobs(0)
            V = WK[:, 6 * WT:8 * WT].rearrange("p (c v) -> p c v", c=TT + 1)
            KEt = wk(1).rearrange("p (c d) -> p c d", c=TT + 1)
            QT, KT = wk(0)[:, 0:T], wk(4)[:, 0:T]
            RS = [wk(2)[:, 0:T], wk(5)[:, 0:T]]
            RS2 = WK[:, 2 * WT:8 * WT].rearrange("p (a w) -> p a w", a=2)
            dve.tensor_scalar(LAM[:, 3, 0:GH], PV[:, 0:GH, R_GLA], -1.0, None, MUL).then_inc(S("nb"), 1)

            def chunks(ap, size):
                return ap.rearrange("p (a c) -> p a c", c=size)
            for h in range(GH):
                A = [YA[:, i] for i in (2 * h, 2 * h + 1, DT + 2 * h, DT + 2 * h + 1)]
                att = lambda c: A[1][:, c % 2 * P:c % 2 * P + P]
                on = lambda c: A[1][:, 256 + c % 2 * DV:256 + (c % 2 + 1) * DV]
                St = lambda c: A[2][:, c % 2 * DV:(c % 2 + 1) * DV]
                QZ = A[2][:, 512:1024].rearrange("p (b t) -> p b t", b=NB)
                KEm = A[0][0:TS, 0:D].rearrange("p (b d) -> p b d", b=NB)
                Sb = lambda b: A[3][:, b % 3 * DV:(b % 3 + 1) * DV] if b % 3 < 2 else A[1][:, 768:1024]
                So = lambda b: A[3][:, 512 + b % 2 * DV:512 + (b % 2 + 1) * DV]
                dve.wait_ge(S("gl_ln"), h + 1)
                link(dve.tensor_tensor(A[0], A[0], A[1], ADD))
                dve.tensor_tensor_scan(A[1], rmask, A[0], 0.0, MUL, ADD).then_inc(S("gl_cum"), 1)
                dve.wait_ge(S("gl_cum"), h + 1)
                for src, dst, size in ((A[1][:, 0:LP], A[0][:, 0:LP], GCH), (A[1][:, LP:T], A[0][:, LP:T], LS)):
                    s3 = chunks(src, size)
                    ins = dve.tensor_tensor(chunks(dst, size), s3[:, :, size - 1:size]
                                            .broadcast_to(list(s3.shape)), s3, SUB)
                ins.then_inc(S("gl_d"), 1)
                dve.wait_ge(S("gl_exp"), h + 1)
                dve.tensor_copy(ST[:, 0:16], chunks(A[2][:, 0:LP], GCH)[:, :, GCH - 1])
                link(dve.tensor_copy(ST[:, 16:24], seqs(A[2])[:, :, LS - 1]))
                ready(dve, f"gq{h}")
                for g, (t0, n) in enumerate(GROUPS):
                    ins = stt(QT[:, t0:t0 + n], pset(f"gq{h}")[:, g, 0:n], DK ** -0.5, A[2][:, t0:t0 + n], MUL, MUL)
                freed(ins, f"gq{h}")
                read(dve, f"gq{h}")
                ready(dve, f"gk{h}")
                for g, (t0, n) in enumerate(GROUPS):
                    link(dve.tensor_tensor(KT[:, t0:t0 + n], pset(f"gk{h}")[:, g, 0:n], A[3][:, t0:t0 + n], MUL))
                dve.wait_ge(S("gl_ed"), h + 1)
                for g, (t0, n) in enumerate(GROUPS):
                    ins = dve.tensor_tensor(A[0][:, t0:t0 + n], pset(f"gk{h}")[:, g, 0:n], A[0][:, t0:t0 + n], MUL)
                    if g < 2:
                        link(ins)
                freed(ins, f"gk{h}")
                read(dve, f"gk{h}")
                dve.memset(St(0), 0.0).then_inc(S("ke"), 1)
                dve.wait_ge(S("ke"), h + 1)
                dve.tensor_tensor(QZ, mid(QT[:, LP:T], NB), seqm[:], MUL).then_inc(S("s_zero"), 1)
                for v in range(2):
                    name = f"gr{h}_{v}"
                    dve.wait_ge(S("gr_th"), 2 * h + v + 1)
                    for g, (t0, n) in enumerate(GROUPS):
                        ins = stt(RS[v][:, t0:t0 + n], RS[v][:, t0:t0 + n], 1.0, pset(name)[:, g, 0:n], ADD, MUL)
                    freed(ins, name)
                    read(dve, name)
                    link(dve.tensor_scalar(RS[v], RS[v], PV[:, 4 + v, R_GLA:R_GLA + 1], 0.5, MUL, MUL))
                read(dve, f"gt{h}")
                dve.tensor_tensor(KEm, mid(KEt[0:TS, 8], NB), bc(seqcol[:], DK), MUL).then_inc(S("kem"), 1)

                def gate_o(c):
                    n = P if c < TT else TS
                    q = h * (TT + 1) + c
                    dve.wait_ge(S("ot"), q + 1)
                    r = RS2[:, :, c * P:c * P + n]
                    dve.tensor_tensor(r, PM[:, 1, 0:256].rearrange("p (v t) -> p v t", v=2)[:, :, 0:n],
                                      r, MUL).then_inc(S("ymul"), 1)

                def update(e, part, b=None):
                    i = e - 24 * h
                    dve.wait_ge(S("ds"), e + 1)
                    new, old = (St(e + 1), St(e)) if b is None else (So(b), Sb(b))
                    stt(new, old, ST[:, i:i + 1], part, MUL, ADD)\
                        .then_inc(S("s_upd"), 1)
                    dve.wait_ge(S("s_upd"), e + 1)
                for c in range(TT + 1):
                    n = P if c < TT else TS
                    q = h * (TT + 1) + c
                    name = f"go{h}_{c}"
                    dve.wait_ge(S("att"), q + 1)
                    mask = m_ch if c < TT else s_le
                    dve.tensor_tensor(att(c)[0:n, 0:n], pset(name)[0:n, 1, 0:n], mask[:], MUL).then_inc(S("att_m"), 1)
                    if c < TT:
                        if c:
                            ready(dve, f"go{h}_{c - 1}")
                        update(24 * h + 2 * c, PM[:, 0, 0:256])
                        dve.wait_ge(S("inter"), h * TT + c + 1)
                        update(24 * h + 2 * c + 1, pset(name)[:, 2, 0:256])
                    else:
                        for b in range(NB):
                            gla_state_in(dve, h, b)
                            if h * NB + b >= 2:
                                dve.wait_ge(S(f"sb_put{b % 2}"), 16 * (h * 4 + b // 2))
                            update(24 * h + 16 + b, PM[:, 0, 0:256] if b % 2 == 0 else pset(name)[:, 2, 0:256], b)
                    dve.wait_ge(S("g_std"), q + 1)
                    st = ST[0:n, 24 + q % 2:25 + q % 2]
                    link(dve.reciprocal(st, st))
                    freed(dve.tensor_scalar(on(c)[0:n], pset(name)[0:n, 0, 0:DV], st, None, MUL), name)
                    if c:
                        gate_o(c - 1)
                gate_o(TT)
                for v in range(2):
                    dve.wait_ge(S("gy_hi"), 2 * h + v + 1)
                    ins = dve.tensor_tensor(Yl[:, 2 * h + v], RS[v], Yh[:, 2 * h + v].bitcast(F32), SUB)
                ins.then_inc(S("gy_lo"), 1)
                dve.wait_ge(S("gy_lo"), h + 1)
            out_jobs(1)
            link(dve.memset(DTK, 0.0))
            dve.wait_ge(S("dt_in"), 64)
            ready(dve, "dtt")
            turned = pset("dtt")[:, 0, 0:144].rearrange("p (c h) -> p c h", c=TT + 1)
            dve.tensor_tensor(DTK[:, 0, 0:TT, :], turned[:, 0:TT, :], mid(DTB, TT), ADD)
            freed(dve.tensor_tensor(DTK[0:TS, 0, TT, :], turned[0:TS, TT, :], DTB[0:TS], ADD), "dtt")
            read(dve, "dtt")
            dve.memset(DTK[:, 1], 0.0).then_inc(S("dt_raw"), 1)
            dve.wait_ge(S("dt_raw"), 1)
            dve.wait_ge(S("dt_exp"), 1)
            tl = [wk(7, 144, 288 + 144 * i) for i in range(5)]
            atanh_of(tl[0], tl[2], tl[3], tl[4])
            dt = DTK[:, 0].rearrange("p c h -> p (c h)")
            link(stt(dt, tl[2], 2.0, tl[1], MUL, ADD))
            link(dve.tensor_scalar(tl[2], dt, -1.0, None, MUL))
            dve.tensor_tensor(DTK[:, 1], tl[2].rearrange("p (c h) -> p c h", c=TT + 1), mid(ALOG, TT + 1), MUL)\
                .then_inc(S("dt_done"), 1)
            dve.wait_ge(S("dt_done"), 1)
            xin = wk(3)
            xin_p = xin[:, 0:HIST + LP]
            xin_s = xin[:, HIST + LP:HIST + LP + NB * (HIST + LS)].rearrange("p (b c) -> p b c", b=NB)
            b_tok = wk(2).rearrange("p (c n) -> p c n", c=TT + 1)
            b_tok = wk(2).rearrange("p (c n) -> p c n", c=TT + 1)
            link(dve.memset(xin_p[:, 0:HIST], 0.0))
            for t in range(CT):
                read(dve, f"sx{t}")
                if 1 <= t <= DT:
                    ready(dve, f"st{t - 1}")
                conv(xin_p, xin_s, wk(4)[:, 0:T], [PQ[:, t, Q_CW + k:Q_CW + k + 1] for k in range(CW)],
                     PQ[:, t, Q_CB:Q_CB + 1], PQ[:, t, Q_CONV:Q_CONV + NB * HIST].rearrange("p (b k) -> p b k", b=NB),
                     CQ[:, t]).then_inc(S("sconv"), 1)
                dve.wait_ge(S("s_th"), t + 1)
                dve.wait_ge(S("sconv"), t + 1)
                ins = stt(wk(4)[:, 0:T], wk(5)[:, 0:T], 1.0, wk(4)[:, 0:T], ADD, MUL)
                if t >= DT:
                    link(ins)
                    ins = dve.tensor_scalar(wk(t - DT)[:, 0:T], wk(4)[:, 0:T], 0.5, None, MUL)
                ins.then_inc(S("s_act"), 1)
            for t in range(DT):
                name = f"sz{t}"
                dve.wait_ge(S("z_th"), t + 1)
                zt = wk(3 + t % 2)
                for g, (t0, n) in enumerate(GROUPS):
                    ins = stt(zt[:, t0:t0 + n], zt[:, t0:t0 + n], 1.0, pset(name)[:, g, 0:n], ADD, MUL)
                freed(ins, name)
            dve.wait_ge(S("z_in0"), 16)
            dve.memset(H_ssd, 0.0).then_inc(S("h_zero"), 1)
            dve.wait_ge(S("h_zero"), 1)

            def heads(ap):
                return ap.rearrange("p (h d) -> p h d", d=HD)

            def tile_sums(c):
                n = P if c < TT else TS
                le = m_le if c < TT else s_le
                dve.wait_ge(S("sc_exp"), c + 1)
                dve.tensor_tensor(WJ(c)[0:n], EC(c)[0:n, 16:32], DTK[0:n, 0, c, :], MUL).then_inc(S("wj"), 1)
                for g in range(2):
                    ins = dve.tensor_tensor(CBM[0:n, g * P:g * P + n], PM[0:n, 0, 160 + g * P:160 + g * P + n], le[:], MUL)
                ins.then_inc(S("cbm"), 1)

            def decay_steps(q):
                c, g = divmod(q, 2)
                n = P if c < TT else TS
                le = m_le if c < TT else s_le
                dve.tensor_tensor(RM(q), bc(DTK[0:n, 1, c, 8 * g:8 * g + 8], n), mid(le[:], 8), MUL)\
                    .then_inc(S("r"), 1)

            def matrices(q):
                c, g = divmod(q, 2)
                n = P if c < TT else TS
                dve.wait_ge(S("cbm"), c + 1)
                read(dve, f"ss{q}")
                dve.tensor_tensor(RM(q), RM(q), mid(CBM[0:n, g * P:g * P + n], 8), MUL).then_inc(S("m"), 1)

            def mark(ins):
                chain[0] += 1
                ins.then_inc(dve_chain, 1)
                return chain[0]

            def outputs(q):
                c, g = divmod(q, 2)
                n = P if c < TT else TS
                hs = slice(8 * g, 8 * g + 8)
                name = f"sy{q}"
                ready(dve, name)
                ps = pset(name)
                y = YT[0:n, 0:512]
                src = ps[0:n, 1, :] if c < TT else YI[g][0:n]
                y_state = mark(dve.tensor_tensor(heads(y), heads(src), bc(EC(c)[0:n, hs], HD), MUL))
                st = H_ssd[64 * g:64 * g + 64]
                if c < TT:
                    kept = mark(dve.tensor_tensor(heads(st), heads(st), bc(EL(c)[64 * g:64 * g + 64, hs], HD), MUL))
                dve.wait_ge(dve_chain, y_state)
                y_sum = mark(dve.tensor_tensor(y, y, ps[0:n, 0, :], ADD))
                if c < TT:
                    dve.wait_ge(dve_chain, kept)
                    freed(dve.tensor_tensor(st, st, ps[64 * g:64 * g + 64, 2, :], ADD), name)
                dve.wait_ge(S("xd"), q + 1)
                dve.wait_ge(dve_chain, y_sum)
                ins = dve.tensor_tensor(y, y, wk(3)[0:n, g * 512:(g + 1) * 512], ADD)
                if c < TT:
                    ins.then_inc(S("x_used"), 1)
                    dve.wait_ge(S("x_used"), q + 1)
                else:
                    freed(ins, name)
                    read(dve, name)
                dve.wait_ge(S(f"z_in{q % 2}"), 16 * (q // 2 + 1))
                dve.tensor_tensor(YZ(q), y, YZ(q), MUL).then_inc(S("y_gated"), 1)

            def scale_y(q):
                n = P if q < 2 * TT else TS
                dve.wait_ge(S("y_std"), q + 1)
                sc = ST[0:n, 28 + q % 2:29 + q % 2]
                link(dve.reciprocal(sc, sc))
                dve.tensor_scalar(YZ(q), YZ(q), sc, 0.5, MUL, MUL).then_inc(S("y_norm"), 1)

            def split_y(q):
                c, g = divmod(q, 2)
                n = P if c < TT else TS
                dve.wait_ge(S("sy_hi"), q + 1)
                cols = slice(c * P, c * P + n)
                for k in range(4 * g, 4 * g + 4):
                    ins = stt(Yl[:, k, cols], PM[:, 1, k % 4 * P:k % 4 * P + n], PV[:, k, R_NSSD:R_NSSD + 1],
                              Yh[:, k, cols].bitcast(F32), MUL, SUB)
                ins.then_inc(S("sy_lo"), 1)
            for b in range(NB):
                ins = dve.tensor_scalar(DAB[0:TS, b * SH:(b + 1) * SH], DTK[0:TS, 1, TT, :], seqcol[:, b:b + 1],
                                        None, MUL)
            ins.then_inc(S("dab"), 1)
            decay_steps(0)
            tile_sums(0)
            decay_steps(1)
            matrices(0)
            matrices(1)
            for q in range(2 * TT):
                ready(dve, f"sy{q}")
                if q + 2 < 2 * TT:
                    decay_steps(q + 2)
                if q:
                    dve.wait_ge(S("y_std"), q)
                outputs(q)
                if q % 2 == 0:
                    tile_sums(q // 2 + 1)
                if q + 2 < 2 * TT:
                    matrices(q + 2)
                if q:
                    split_y(q - 1)
                scale_y(q)
            split_y(2 * TT - 1)
            dve.tensor_tensor(CZ, mid(wk(1)[:, LP:T], NB), seqm[:], MUL).then_inc(S("cz"), 1)
            decay_steps(2 * TT)
            for b in range(NB):
                if b >= 2:
                    ready(dve, f"ub{b - 2}")
                    ready(dve, f"uc{b - 2}")
                dve.tensor_scalar(wk(5 + b % 2, P, D)[0:TS], b_tok[0:TS, TT, :], seqcol[:, b:b + 1], None, MUL)\
                    .then_inc(S("bm"), 1)
                read(dve, f"si{b}")
                new = wk(2, 512, b % 2 * 512)
                for g in range(2):
                    r = slice(64 * g, 64 * g + 64)
                    kept = mark(dve.tensor_tensor(heads(new[r]), heads(wk(1, 512, b % 2 * 512)[r]),
                                                  bc(EL(TT)[r, b * SH + 8 * g:b * SH + 8 * g + 8], HD), MUL))
                dve.wait_ge(dve_chain, kept)
                ready(dve, f"ub{b}")
                freed(dve.tensor_tensor(new, new, pset(f"ub{b}")[:, 0, :], ADD), f"ub{b}")
            q = 2 * TT
            matrices(q)
            dve.wait_ge(S("si_mm"), NB)
            decay_steps(q + 1)
            matrices(q + 1)
            dve.wait_ge(S("yi"), 1)
            outputs(q)
            scale_y(q)
            outputs(q + 1)
            scale_y(q + 1)
            split_y(q)
            split_y(q + 1)
            out_jobs(2)
            for k in range(DT - 2, DT):
                lo_sum(k)

            def inverses(i):
                dve.wait_ge(S("nrm_std"), i + 1)
                dve.reciprocal(ST[:, 0:TT], ST[:, 0:TT])
                dve.reciprocal(ST[0:TS, TT:TT + 1], ST[0:TS, TT:TT + 1]).then_inc(S("nrm_rs"), 1)
            dve.wait_ge(S("mem_std"), 1)
            link(dve.reciprocal(ST[:, 30:32], ST[:, 30:32]))
            for i in range(2):
                dve.tensor_scalar(MV[:, i], MV[:, i], ST[:, 30 + i:31 + i], None, MUL).then_inc(S("mem_scaled"), 1)
            for i in range(2):
                name = f"mt{i}"
                ready(dve, name)
                if i:
                    dve.wait_ge(S("mem_lo"), i)
                for a in range(2):
                    ins = dve.tensor_tensor(wk(7, 512, a * 512).rearrange("p (k m) -> p k m", k=4),
                                            pset(name)[:, a, :].rearrange("p (k m) -> p k m", k=4),
                                            PV[:, 4 * a:4 * a + 4, R_NMEM:R_NMEM + 1].broadcast_to([P, 4, P]), MUL)
                    if a == 0:
                        link(ins)
                freed(ins, name)
                read(dve, name)
                dve.wait_ge(S("mem_hi"), i + 1)
                dve.tensor_tensor(MNl[:, :, i * P:(i + 1) * P], wk(7, D).rearrange("p (k m) -> p k m", k=DT),
                                  MNh[:, :, i * P:(i + 1) * P].bitcast(F32), SUB).then_inc(S("mem_lo"), 1)
            inverses(0)
            read(dve, "xn")
            for k in range(DT):
                if k >= 2:
                    dve.wait_ge(S("nrm_lo"), k - 1)
                dst = wk(4 + k % 2)[:, 0:T]
                link(stt(dst, X[:, k], PV[:, k, R_NX:R_NX + 1], wk(6)[:, 0:T], MUL, MUL))
                link(dve.tensor_copy(Hh[:, k], dst))
                dve.tensor_tensor(Hl[:, k], dst, Hh[:, k].bitcast(F32), SUB).then_inc(S("nrm_lo"), 1)

            def maxima(c):
                n = P if c < TT else TS
                name = f"xs{c}"
                ready(dve, name)
                if c >= 2:
                    read(dve, f"xs{c - 2}")
                mx = ST[0:n, 32 + 4 * (c % 2):36 + 4 * (c % 2)]
                link(dve.tensor_reduce(mx, pset(name)[0:n, 0:2, :].rearrange("p a (h m) -> p (a h) m", h=2),
                                       AX_X, ALU.max))
                dve.tensor_scalar(mx, mx, -(XD ** -0.5), None, MUL).then_inc(S("x_max"), 1)

            def probs(c):
                n = P if c < TT else TS
                read(dve, f"xs{c}")
                sums = ST[0:n, 40 + 4 * (c % 2):44 + 4 * (c % 2)]
                link(dve.reciprocal(sums, sums))
                p = Pr(c)[0:n].rearrange("p (h m) -> p h m", h=XH)
                dve.tensor_tensor(p, p, bc(sums, M), MUL).then_inc(S("x_p"), 1)

            def outputs(c):
                n = P if c < TT else TS
                name = f"xv{c}" if c < TT else "xw"
                dve.wait_ge(S("xo_hi"), c + 1)
                for a in range(2):
                    cols = slice(c * P, c * P + n)
                    ins = dve.tensor_tensor(Hl[:, 4 * a:4 * a + 4, cols],
                                            pset(name)[:, a, :].rearrange("p (k t) -> p k t", k=4)[:, :, 0:n],
                                            Hh[:, 4 * a:4 * a + 4, cols].bitcast(F32), SUB)
                freed(ins, name)
            maxima(0)
            probs(0)
            for c in range(TT):
                if c + 1 < TT:
                    maxima(c + 1)
                    probs(c + 1)
                outputs(c)
            link(dve.memset(WK[:, 6 * WT:6 * WT + 2 * DT * 120], 0.0))
            for b in range(NB):
                if b >= 2:
                    dve.wait_ge(S("kb_s"), 4 * (b - 1))
                dve.tensor_copy(QZb[:, b % 2, :, 56:56 + LS], Q[:, :, LP + LS * b:LP + LS * (b + 1)])\
                    .then_inc(S("qz"), 1)
            maxima(TT)
            probs(TT)
            link(dve.memset(PZb.rearrange("p a k t -> p (a k t)"), 0.0))
            read(dve, f"xp{TT}")
            for b in range(NB):
                if b >= 2:
                    dve.wait_ge(S("vb"), b - 1)
                dve.tensor_copy(PZb[:, b % 2, :, 56:56 + LS], PrT(TT)[:, :, LS * b:LS * (b + 1)]).then_inc(S("pz"), 1)
            outputs(TT)

            def add_to_x(name, t):
                ready(dve, name)
                for g, (t0, n) in enumerate(GROUPS):
                    ins = dve.tensor_tensor(X[:, t, t0:t0 + n], X[:, t, t0:t0 + n], pset(name)[:, g, 0:n], ADD)
                freed(ins, name)
            for t in range(DT):
                add_to_x(f"xo{t}", t)
            inverses(1)
            read(dve, "fn")
            for k in range(DT + 1):
                if k < DT:
                    if k >= 2:
                        dve.wait_ge(S("nrm_lo"), DT + k - 1)
                    stt(wk(4 + k % 2)[:, 0:T], X[:, k], PV[:, k, R_NFFN:R_NFFN + 1], wk(6)[:, 0:T], MUL, MUL)\
                        .then_inc(S("nrm_t"), 1)
                if k:
                    dve.wait_ge(S("nrm_hi"), k)
                    dve.tensor_tensor(Hl[:, k - 1], wk(4 + (k - 1) % 2)[:, 0:T], Hh[:, k - 1].bitcast(F32), SUB)\
                        .then_inc(S("nrm_lo"), 1)
            def gain(t):
                dve.wait_ge(S("nrm_sq"), 2 * DT + t + 1)
                dve.tensor_scalar(X[:, t], X[:, t], PV[:, t, R_NFIN:R_NFIN + 1], None, MUL).then_inc(S("gained"), 1)
            for c in range(FC + 1):
                for i in range(2 if c < FC else 0):
                    q = 2 * c + i
                    h = wk(q % 4)[:, 0:T]
                    dve.wait_ge(S("f_th"), q + 1)
                    name = f"fg{c}_{i}"
                    for g, (t0, n) in enumerate(GROUPS):
                        ins = stt(h[:, t0:t0 + n], h[:, t0:t0 + n], 1.0, pset(name)[:, g, 0:n], ADD, MUL)
                    freed(ins, name)
                    read(dve, name)
                    name = f"fu{c}_{i}"
                    ready(dve, name)
                    for g, (t0, n) in enumerate(GROUPS):
                        ins = stt(h[:, t0:t0 + n], h[:, t0:t0 + n], 0.5, pset(name)[:, g, 0:n], MUL, MUL)
                        if g < 2:
                            link(ins)
                    freed(ins, name)
                    read(dve, name)
                    dve.wait_ge(S("f_hi"), q + 1)
                    dve.tensor_tensor(Fl[:, c % 2, i], h, Fh[:, c % 2, i].bitcast(F32), SUB).then_inc(S("f_lo"), 1)
                if c:
                    for t in range(DT):
                        add_to_x(f"fd{c - 1}_{t}", t)
                        if c == FC and t:
                            gain(t - 1)
            gain(DT - 1)
            inverses(2)


_OUTS = [("y_prompt", (1, LP, D)), ("y_sample", (NB, LS, D)), ("p_lru_h", (1, 1, D)), ("p_lru_conv", (1, 1, HIST, D)),
         ("p_gla_S", (1, 1, GH, DK, DV)), ("p_ssd_h", (1, 1, SH, HD, NS)), ("p_ssd_conv", (1, 1, HIST, SCC)),
         ("p_mem_k", (1, 1, M, XH, XD)), ("p_mem_v", (1, 1, M, XH, XD)), ("s_lru_h", (1, NB, D)),
         ("s_lru_conv", (1, NB, HIST, D)), ("s_gla_S", (1, NB, GH, DK, DV)), ("s_ssd_h", (1, NB, SH, HD, NS)),
         ("s_ssd_conv", (1, NB, HIST, SCC))]
_INS = ["x_prompt", "x_sample", "mem_prompt", "state_lru_h", "state_lru_conv", "state_gla_S", "state_ssd_h",
        "state_ssd_conv", "cache_mem_k", "cache_mem_v", "norm_mix", "w_in", "lru_conv_w", "lru_conv_b", "lru_wa",
        "lru_ba", "lru_wx", "lru_bx", "lru_lambda", "w_lru_out", "gla_w_alpha", "gla_b_alpha", "gla_norm",
        "w_gla_out", "ssd_conv_w", "ssd_conv_b", "ssd_dt_bias", "ssd_a_log", "ssd_d", "ssd_norm", "w_ssd_out",
        "w_mix_out", "norm_xattn", "norm_mem", "w_xq", "w_xk", "w_xv", "w_xo", "norm_ffn", "w_ffn_gate",
        "w_ffn_up", "w_ffn_down", "norm_final"]


def kernel(**inputs):
    import numpy as np
    import concourse.bacc as bacc
    from concourse.bass_utils import run_bass_kernel_spmd as run

    nc = bacc.Bacc("TRN2", target_bir_lowering=False, num_devices=1)
    arrays = {f"in_{name}": np.ascontiguousarray(inputs[name]) for name in _INS}
    ins = {name: nc.dram_tensor(f"in_{name}", arrays[f"in_{name}"].shape, F32, kind="ExternalInput").ap()
           for name in _INS}
    outs = {name: nc.dram_tensor(f"out_{name}", shape, F32, kind="ExternalOutput").ap() for name, shape in _OUTS}
    build(nc, ins, outs)
    r = run(nc, [arrays], core_ids=[0])
    return tuple(r.results[0][f"out_{name}"] for name, _ in _OUTS)
```
